# Optimizing a Trainium2 kernel written in Bass

```python
import math
import jax, jax.numpy as jnp
from jax import lax
import numpy as np

D_MODEL = 1024
BATCH = 1
SEQ = 256
DEPTH = 2

GRID_W = 64
CTX_LEN = 256
HEAD_DIM = 64
ROPE_THETA = 10000.0
Q_BLOCK = 128

MLA_HEADS = 8
MLA_Q_RANK = 256
MLA_KV_RANK = 128
MLA_NOPE = 64
MLA_ROPE = 32
MLA_V = 64
SWA_HEADS = 8
SWA_KV_HEADS = 2
SWA_GROUP = SWA_HEADS // SWA_KV_HEADS
WINDOW = 128
DIFF_HEADS = D_MODEL // (2 * HEAD_DIM)
D_FF = 2816

ALPHA = (2 * DEPTH) ** 0.25
BETA = (8 * DEPTH) ** -0.25
LN_EPS = 1e-5
RMS_EPS = 1e-6
NEG_INF = -1e30
N_EVEN = (DEPTH + 1) // 2
N_ODD = DEPTH // 2

EVEN_Q_SIZES = (MLA_Q_RANK, SWA_HEADS * HEAD_DIM)
EVEN_KV_SIZES = (MLA_KV_RANK, MLA_ROPE, SWA_KV_HEADS * HEAD_DIM, SWA_KV_HEADS * HEAD_DIM)
EVEN_Q_COLS = sum(EVEN_Q_SIZES)
EVEN_IN = EVEN_Q_COLS + sum(EVEN_KV_SIZES)
EVEN_OUT = MLA_HEADS * MLA_V + SWA_HEADS * HEAD_DIM
DIFF_QK_COLS = DIFF_HEADS * 2 * HEAD_DIM
ODD_IN = 3 * DIFF_QK_COLS
ODD_OUT = DIFF_HEADS * 2 * HEAD_DIM


def layer_norm(x, g, b):
    xf = x.astype(jnp.float32)
    mu = jnp.mean(xf, -1, keepdims=True)
    var = jnp.mean(jnp.square(xf - mu), -1, keepdims=True)
    return ((xf - mu) * lax.rsqrt(var + LN_EPS) * g + b).astype(x.dtype)

def rms_norm(x, g):
    xf = x.astype(jnp.float32)
    return (xf * lax.rsqrt(jnp.mean(jnp.square(xf), -1, keepdims=True) + RMS_EPS) * g).astype(x.dtype)

def split_cols(t, sizes):
    idx = np.cumsum(np.array(sizes))[:-1].tolist()
    return jnp.split(t, idx, axis=-1)

def axial_rope_tables(rows, dim):
    row = jnp.repeat(jnp.arange(rows), GRID_W).astype(jnp.float32)
    col = jnp.tile(jnp.arange(GRID_W), rows).astype(jnp.float32)
    quarter = dim // 4
    freqs = ROPE_THETA ** (-jnp.arange(quarter, dtype=jnp.float32) / quarter)
    ar = row[:, None] * freqs
    ac = col[:, None] * freqs
    cos = jnp.concatenate([jnp.cos(ar), jnp.cos(ar), jnp.cos(ac), jnp.cos(ac)], -1)
    sin = jnp.concatenate([jnp.sin(ar), jnp.sin(ar), jnp.sin(ac), jnp.sin(ac)], -1)
    return cos, sin

def apply_rope(x, cos, sin):
    shape = (cos.shape[0],) + (1,) * (x.ndim - 3) + (cos.shape[1],)
    cos = cos.reshape(shape)
    sin = sin.reshape(shape)
    a, b, c_, d = jnp.split(x, 4, axis=-1)
    rot = jnp.concatenate([-b, a, -d, c_], -1)
    return (x * cos + rot * sin).astype(x.dtype)

def sweep_query_blocks(fn, q):
    B, S = q.shape[:2]
    nb = S // Q_BLOCK
    blocks = jnp.moveaxis(q.reshape((B, nb, Q_BLOCK) + q.shape[2:]), 1, 0)
    out = jnp.moveaxis(lax.map(fn, blocks), 0, 1)
    return out.reshape((B, S) + out.shape[3:])

def softmax_attend(q, k, v, scale):
    s = jnp.einsum('bqhd,bkhd->bhqk', q, k).astype(jnp.float32) * scale
    p = jax.nn.softmax(s, axis=-1).astype(v.dtype)
    return jnp.einsum('bhqk,bkhd->bqhd', p, v)

def mla_queries(q_a, q_norm, w_qb, cos, sin):
    B, T = q_a.shape[:2]
    q = (rms_norm(q_a, q_norm) @ w_qb).reshape(B, T, MLA_HEADS, MLA_NOPE + MLA_ROPE)
    if cos is None:
        return q
    return jnp.concatenate([q[..., :MLA_NOPE], apply_rope(q[..., MLA_NOPE:], cos, sin)], -1)

def mla_keys_values(kv_a, k_rope, kv_norm, w_kvb, cos, sin):
    B, T = kv_a.shape[:2]
    kv = (rms_norm(kv_a, kv_norm) @ w_kvb).reshape(B, T, MLA_HEADS, MLA_NOPE + MLA_V)
    if cos is not None:
        k_rope = apply_rope(k_rope, cos, sin)
    k_rope = jnp.broadcast_to(k_rope[:, :, None, :], (B, T, MLA_HEADS, MLA_ROPE))
    return jnp.concatenate([kv[..., :MLA_NOPE], k_rope], -1), kv[..., MLA_NOPE:]

def window_attend(q, k, v, k_ctx, v_ctx, sink):
    B, S = q.shape[:2]
    L = k_ctx.shape[1]
    nb = S // WINDOW
    qb = q.reshape(B, nb, WINDOW, SWA_KV_HEADS, SWA_GROUP, HEAD_DIM)

    def band(t):
        tb = t.reshape(B, nb, WINDOW, SWA_KV_HEADS, HEAD_DIM)
        tp = jnp.pad(tb, ((0, 0), (1, 1), (0, 0), (0, 0), (0, 0)))
        return jnp.concatenate([tp[:, :-2], tp[:, 1:-1], tp[:, 2:]], axis=2)

    kb, vb = band(k), band(v)
    qpos = jnp.arange(nb)[:, None] * WINDOW + jnp.arange(WINDOW)[None, :]
    kpos = (jnp.arange(nb)[:, None] - 1) * WINDOW + jnp.arange(3 * WINDOW)[None, :]
    valid = ((jnp.abs(qpos[:, :, None] - kpos[:, None, :]) <= WINDOW)
             & (kpos[:, None, :] >= 0) & (kpos[:, None, :] < S))
    scale = HEAD_DIM ** -0.5
    s_band = jnp.einsum('bnqhgd,bnkhd->bnhgqk', qb, kb).astype(jnp.float32) * scale
    s_band = jnp.where(valid[None, :, None, None], s_band, NEG_INF)
    s_ctx = jnp.einsum('bnqhgd,bchd->bnhgqc', qb, k_ctx).astype(jnp.float32) * scale
    sink_col = jnp.broadcast_to(sink.reshape(SWA_KV_HEADS, SWA_GROUP, 1, 1).astype(jnp.float32),
                                s_ctx.shape[:-1] + (1,))
    p = jax.nn.softmax(jnp.concatenate([s_ctx, s_band, sink_col], -1), axis=-1)
    p_ctx = p[..., :L].astype(v.dtype)
    p_band = p[..., L:L + 3 * WINDOW].astype(v.dtype)
    o = (jnp.einsum('bnhgqc,bchd->bnqhgd', p_ctx, v_ctx)
         + jnp.einsum('bnhgqk,bnkhd->bnqhgd', p_band, vb))
    return o.reshape(B, S, SWA_HEADS * HEAD_DIM)

def sink_attend(q, k, v, sink):
    B, T = q.shape[:2]
    qg = q.reshape(B, T, SWA_KV_HEADS, SWA_GROUP, HEAD_DIM)
    s = jnp.einsum('bqhgd,bkhd->bhgqk', qg, k).astype(jnp.float32) * HEAD_DIM ** -0.5
    sink_col = jnp.broadcast_to(sink.reshape(SWA_KV_HEADS, SWA_GROUP, 1, 1).astype(jnp.float32),
                                s.shape[:-1] + (1,))
    p = jax.nn.softmax(jnp.concatenate([s, sink_col], -1), axis=-1)[..., :-1].astype(v.dtype)
    return jnp.einsum('bhgqk,bkhd->bqhgd', p, v).reshape(B, T, SWA_HEADS * HEAD_DIM)

def even_mixer(h_lat, h_ctx, w_in, q_norm, w_qb, kv_norm, w_kvb, sink, w_out, rope32, rope64, need_ctx):
    B, S = h_lat.shape[:2]
    L = h_ctx.shape[1]
    cos32, sin32 = rope32
    cos64, sin64 = rope64
    qa_l, qs_l, kva_l, kr_l, ks_l, vs_l = split_cols(h_lat @ w_in, EVEN_Q_SIZES + EVEN_KV_SIZES)
    kva_c, kr_c, ks_c, vs_c = split_cols(h_ctx @ w_in[:, EVEN_Q_COLS:], EVEN_KV_SIZES)
    mla_scale = (MLA_NOPE + MLA_ROPE) ** -0.5
    q_mla = mla_queries(qa_l, q_norm, w_qb, cos32, sin32)
    k_mla_l, v_mla_l = mla_keys_values(kva_l, kr_l, kv_norm, w_kvb, cos32, sin32)
    k_mla_c, v_mla_c = mla_keys_values(kva_c, kr_c, kv_norm, w_kvb, None, None)
    k_all = jnp.concatenate([k_mla_c, k_mla_l], axis=1)
    v_all = jnp.concatenate([v_mla_c, v_mla_l], axis=1)
    o_mla = sweep_query_blocks(lambda qb: softmax_attend(qb, k_all, v_all, mla_scale), q_mla)
    o_mla = o_mla.reshape(B, S, MLA_HEADS * MLA_V)
    q_swa = apply_rope(qs_l.reshape(B, S, SWA_HEADS, HEAD_DIM), cos64, sin64)
    k_swa = apply_rope(ks_l.reshape(B, S, SWA_KV_HEADS, HEAD_DIM), cos64, sin64)
    v_swa = vs_l.reshape(B, S, SWA_KV_HEADS, HEAD_DIM)
    k_swa_c = ks_c.reshape(B, L, SWA_KV_HEADS, HEAD_DIM)
    v_swa_c = vs_c.reshape(B, L, SWA_KV_HEADS, HEAD_DIM)
    o_swa = window_attend(q_swa, k_swa, v_swa, k_swa_c, v_swa_c, sink)
    out_l = jnp.concatenate([o_mla, o_swa], -1) @ w_out
    if not need_ctx:
        return out_l, None
    qa_c, qs_c = split_cols(h_ctx @ w_in[:, :EVEN_Q_COLS], EVEN_Q_SIZES)
    q_mla_c = mla_queries(qa_c, q_norm, w_qb, None, None)
    o_mla_c = softmax_attend(q_mla_c, k_mla_c, v_mla_c, mla_scale).reshape(B, L, MLA_HEADS * MLA_V)
    o_swa_c = sink_attend(qs_c.reshape(B, L, SWA_HEADS, HEAD_DIM), k_swa_c, v_swa_c, sink)
    out_c = jnp.concatenate([o_mla_c, o_swa_c], -1) @ w_out
    return out_l, out_c

def diff_attend(q, k, v, lam, lambda_init, subln_g):
    s = jnp.einsum('bqhtd,bkhtd->bthqk', q, k).astype(jnp.float32) * HEAD_DIM ** -0.5
    p = jax.nn.softmax(s, axis=-1)
    a = (p[:, 0] - lam * p[:, 1]).astype(v.dtype)
    o = jnp.einsum('bhqk,bkhe->bqhe', a, v)
    o = rms_norm(o, subln_g) * (1.0 - lambda_init)
    return o.reshape(o.shape[0], o.shape[1], DIFF_HEADS * 2 * HEAD_DIM)

def odd_mixer(h_lat, h_ctx, w_in, lam_q1, lam_k1, lam_q2, lam_k2, subln_g, w_out, rope64,
              lambda_init, need_ctx):
    B, S = h_lat.shape[:2]
    L = h_ctx.shape[1]
    cos, sin = rope64
    q_l, k_l, v_l = jnp.split(h_lat @ w_in, 3, axis=-1)
    q_l = apply_rope(q_l.reshape(B, S, DIFF_HEADS, 2, HEAD_DIM), cos, sin)
    k_l = apply_rope(k_l.reshape(B, S, DIFF_HEADS, 2, HEAD_DIM), cos, sin)
    v_l = v_l.reshape(B, S, DIFF_HEADS, 2 * HEAD_DIM)
    k_c, v_c = jnp.split(h_ctx @ w_in[:, DIFF_QK_COLS:], 2, axis=-1)
    k_c = k_c.reshape(B, L, DIFF_HEADS, 2, HEAD_DIM)
    v_c = v_c.reshape(B, L, DIFF_HEADS, 2 * HEAD_DIM)
    lam = (jnp.exp(jnp.sum(lam_q1 * lam_k1).astype(jnp.float32))
           - jnp.exp(jnp.sum(lam_q2 * lam_k2).astype(jnp.float32)) + lambda_init)
    k_all = jnp.concatenate([k_c, k_l], axis=1)
    v_all = jnp.concatenate([v_c, v_l], axis=1)
    o_l = sweep_query_blocks(lambda qb: diff_attend(qb, k_all, v_all, lam, lambda_init, subln_g), q_l)
    out_l = o_l @ w_out
    if not need_ctx:
        return out_l, None
    q_c = (h_ctx @ w_in[:, :DIFF_QK_COLS]).reshape(B, L, DIFF_HEADS, 2, HEAD_DIM)
    out_c = diff_attend(q_c, k_c, v_c, lam, lambda_init, subln_g) @ w_out
    return out_l, out_c

def conv_ffn(h, w_gate, w_up, conv_w, conv_b, w_down):
    g = h @ w_gate
    gp = jnp.pad(g, ((0, 0), (1, 1), (0, 0)))
    g = gp[:, :-2] * conv_w[0] + gp[:, 1:-1] * conv_w[1] + gp[:, 2:] * conv_w[2] + conv_b
    return (jax.nn.silu(g) * (h @ w_up)) @ w_down

def modulation(cond, w_mod, b_mod):
    return jnp.split(jax.nn.silu(cond) @ w_mod + b_mod, 6, axis=-1)

def first_inputs(seed: int = 0) -> dict:
    key = jax.random.key(seed)
    ks = iter(jax.random.split(key, 40))

    def nrm(shape, scale):
        return jax.random.normal(next(ks), shape, jnp.float32) * scale

    def gain(shape):
        return 1.0 + nrm(shape, 0.01)

    D, F = D_MODEL, D_FF
    return {
        "x": nrm((BATCH, SEQ, D), 1.0),
        "c": nrm((BATCH, D), 1.0),
        "ctx": nrm((BATCH, CTX_LEN, D), 1.0),
        "c_ctx": nrm((D,), 1.0),
        "w_mod": nrm((DEPTH, D, 6 * D), 0.5 * D ** -0.5),
        "b_mod": nrm((DEPTH, 6 * D), 0.01),
        "ln1_g": gain((DEPTH, D)),
        "ln1_b": nrm((DEPTH, D), 0.01),
        "ln2_g": gain((DEPTH, D)),
        "ln2_b": nrm((DEPTH, D), 0.01),
        "ffn_w_gate": nrm((DEPTH, D, F), D ** -0.5),
        "ffn_w_up": nrm((DEPTH, D, F), D ** -0.5),
        "ffn_conv_w": nrm((DEPTH, 3, F), 3 ** -0.5),
        "ffn_conv_b": nrm((DEPTH, F), 0.01),
        "ffn_w_down": nrm((DEPTH, F, D), BETA * F ** -0.5),
        "ab_w_in": nrm((N_EVEN, D, EVEN_IN), D ** -0.5),
        "mla_q_norm": gain((N_EVEN, MLA_Q_RANK)),
        "mla_w_qb": nrm((N_EVEN, MLA_Q_RANK, MLA_HEADS * (MLA_NOPE + MLA_ROPE)), MLA_Q_RANK ** -0.5),
        "mla_kv_norm": gain((N_EVEN, MLA_KV_RANK)),
        "mla_w_kvb": nrm((N_EVEN, MLA_KV_RANK, MLA_HEADS * (MLA_NOPE + MLA_V)), MLA_KV_RANK ** -0.5),
        "swa_sink": nrm((N_EVEN, SWA_HEADS), 0.5),
        "ab_w_out": nrm((N_EVEN, EVEN_OUT, D), BETA * EVEN_OUT ** -0.5),
        "diff_w_in": nrm((N_ODD, D, ODD_IN), D ** -0.5),
        "diff_lam_q1": nrm((N_ODD, HEAD_DIM), 0.1),
        "diff_lam_k1": nrm((N_ODD, HEAD_DIM), 0.1),
        "diff_lam_q2": nrm((N_ODD, HEAD_DIM), 0.1),
        "diff_lam_k2": nrm((N_ODD, HEAD_DIM), 0.1),
        "diff_subln_g": gain((N_ODD, 2 * HEAD_DIM)),
        "diff_w_out": nrm((N_ODD, ODD_OUT, D), BETA * ODD_OUT ** -0.5),
    }

def first_block(x, c, ctx, c_ctx, w_mod, b_mod, ln1_g, ln1_b, ln2_g, ln2_b,
              ffn_w_gate, ffn_w_up, ffn_conv_w, ffn_conv_b, ffn_w_down,
              ab_w_in, mla_q_norm, mla_w_qb, mla_kv_norm, mla_w_kvb, swa_sink, ab_w_out,
              diff_w_in, diff_lam_q1, diff_lam_k1, diff_lam_q2, diff_lam_k2, diff_subln_g, diff_w_out):
    S = x.shape[1]
    ROWS = S // GRID_W
    rope32 = axial_rope_tables(ROWS, MLA_ROPE)
    rope64 = axial_rope_tables(ROWS, HEAD_DIM)
    xl, xc = x, ctx
    for i in range(DEPTH):
        need_ctx = i < DEPTH - 1
        j = i // 2
        sh1_l, sc1_l, gt1_l, sh2_l, sc2_l, gt2_l = [t[:, None, :] for t in modulation(c, w_mod[i], b_mod[i])]
        sh1_c, sc1_c, gt1_c, sh2_c, sc2_c, gt2_c = modulation(c_ctx, w_mod[i], b_mod[i])
        h_l = xl * (1.0 + sc1_l) + sh1_l
        h_c = xc * (1.0 + sc1_c) + sh1_c
        if i % 2 == 0:
            o_l, o_c = even_mixer(h_l, h_c, ab_w_in[j], mla_q_norm[j], mla_w_qb[j], mla_kv_norm[j],
                                  mla_w_kvb[j], swa_sink[j], ab_w_out[j], rope32, rope64, need_ctx)
        else:
            lambda_init = 0.8 - 0.6 * math.exp(-0.3 * i)
            o_l, o_c = odd_mixer(h_l, h_c, diff_w_in[j], diff_lam_q1[j], diff_lam_k1[j], diff_lam_q2[j],
                                 diff_lam_k2[j], diff_subln_g[j], diff_w_out[j], rope64, lambda_init, need_ctx)
        xl = layer_norm(ALPHA * xl + gt1_l * o_l, ln1_g[i], ln1_b[i])
        h_l = xl * (1.0 + sc2_l) + sh2_l
        f_l = conv_ffn(h_l, ffn_w_gate[i], ffn_w_up[i], ffn_conv_w[i], ffn_conv_b[i], ffn_w_down[i])
        xl = layer_norm(ALPHA * xl + gt2_l * f_l, ln2_g[i], ln2_b[i])
        if need_ctx:
            xc = layer_norm(ALPHA * xc + gt1_c * o_c, ln1_g[i], ln1_b[i])
            h_c = xc * (1.0 + sc2_c) + sh2_c
            f_c = conv_ffn(h_c, ffn_w_gate[i], ffn_w_up[i], ffn_conv_w[i], ffn_conv_b[i], ffn_w_down[i])
            xc = layer_norm(ALPHA * xc + gt2_c * f_c, ln2_g[i], ln2_b[i])
    return xl


DEPTH_2 = 1

D_MIX = 2 * D_MODEL
D_SSD = D_MIX // 2
D_SC = D_MIX - D_SSD
SSD_HEADDIM = 64
SSD_HEADS = D_SSD // SSD_HEADDIM
SSD_GROUPS = 4
SSD_HPG = SSD_HEADS // SSD_GROUPS
SSD_STATE = 128
SSD_CONV = 4
D_XBC = D_SSD + 2 * SSD_GROUPS * SSD_STATE
CHUNK = 128
SC_GROUPS = 16
SC_CONV = 3
N_META = 16
META_PAD = CHUNK - N_META
IN_COLS = D_SSD + D_XBC + SSD_HEADS + 3 * D_SC
N_EXPERT_GROUPS = 4
EXPERTS_PER_GROUP = 4
N_EXPERTS = N_EXPERT_GROUPS * EXPERTS_PER_GROUP
TOP_K = 2
D_EXPERT = 512
EPS = 1e-6


def rmsnorm(x, g):
    xf = x.astype(jnp.float32)
    xf = xf * lax.rsqrt(jnp.mean(xf * xf, axis=-1, keepdims=True) + EPS)
    return (xf * g.astype(jnp.float32)).astype(x.dtype)

def group_rmsnorm(x, g, n_groups):
    shp = x.shape
    xf = x.astype(jnp.float32).reshape(shp[:-1] + (n_groups, shp[-1] // n_groups))
    xf = xf * lax.rsqrt(jnp.mean(xf * xf, axis=-1, keepdims=True) + EPS)
    return (xf.reshape(shp) * g.astype(jnp.float32)).astype(x.dtype)

def causal_dwconv(x, w):
    K = w.shape[0]
    L = x.shape[1]
    xp = jnp.pad(x, ((0, 0), (K - 1, 0), (0, 0)))
    y = xp[:, 0:L] * w[0]
    for k in range(1, K):
        y = y + xp[:, k:k + L] * w[k]
    return y

def ssd_chunked(xs, dt, A, Bm, Cm):
    dtype = xs.dtype
    b, Lp = xs.shape[0], xs.shape[1]
    nc = Lp // CHUNK
    x = xs.reshape(b, nc, CHUNK, SSD_GROUPS, SSD_HPG, SSD_HEADDIM)
    dtc = dt.reshape(b, nc, CHUNK, SSD_GROUPS, SSD_HPG)
    Bc = Bm.reshape(b, nc, CHUNK, SSD_GROUPS, SSD_STATE)
    Cc = Cm.reshape(b, nc, CHUNK, SSD_GROUPS, SSD_STATE)

    dA = jnp.moveaxis(dtc * A.reshape(SSD_GROUPS, SSD_HPG), 2, -1)
    A_cum = jnp.cumsum(dA, axis=-1)
    xdt = x * dtc.astype(dtype)[..., None]

    causal = jnp.tril(jnp.ones((CHUNK, CHUNK), dtype=bool))
    seg = A_cum[..., :, None] - A_cum[..., None, :]
    Lmat = jnp.exp(jnp.where(causal, seg, -jnp.inf)).astype(dtype)
    CB = jnp.einsum('bcqgn,bckgn->bcgqk', Cc, Bc)
    y_diag = jnp.einsum('bcgqk,bcgrqk,bckgrp->bcqgrp', CB, Lmat, xdt)

    decay_states = jnp.exp(A_cum[..., -1:] - A_cum).astype(dtype)
    states = jnp.einsum('bckgn,bcgrk,bckgrp->bcgrpn', Bc, decay_states, xdt)
    chunk_decay = jnp.exp(A_cum[..., -1]).astype(dtype)

    def step(s, inp):
        st, dec = inp
        return dec[..., None, None] * s + st, s

    s0 = jnp.zeros((b, SSD_GROUPS, SSD_HPG, SSD_HEADDIM, SSD_STATE), dtype)
    _, prev = lax.scan(step, s0, (jnp.moveaxis(states, 1, 0), jnp.moveaxis(chunk_decay, 1, 0)))
    prev = jnp.moveaxis(prev, 0, 1)

    decay_out = jnp.exp(A_cum).astype(dtype)
    y_off = jnp.einsum('bcqgn,bcgrpn,bcgrq->bcqgrp', Cc, prev, decay_out)
    return (y_diag + y_off).reshape(b, Lp, SSD_HEADS, SSD_HEADDIM)

def ssd_branch(z, xbc, dt_raw, conv_w, conv_b, dt_bias, A_log, D_skip, norm_g):
    b, L, _ = xbc.shape
    xbc = jax.nn.silu(causal_dwconv(xbc, conv_w) + conv_b)
    xs = xbc[..., :D_SSD].reshape(b, L, SSD_HEADS, SSD_HEADDIM)
    Bm = xbc[..., D_SSD:D_SSD + SSD_GROUPS * SSD_STATE].reshape(b, L, SSD_GROUPS, SSD_STATE)
    Cm = xbc[..., D_SSD + SSD_GROUPS * SSD_STATE:].reshape(b, L, SSD_GROUPS, SSD_STATE)
    dt = jax.nn.softplus((dt_raw + dt_bias).astype(jnp.float32))
    A = -jnp.exp(A_log.astype(jnp.float32))

    def front_pad(t):
        return jnp.pad(t, ((0, 0), (META_PAD, 0)) + ((0, 0),) * (t.ndim - 2))

    y = ssd_chunked(front_pad(xs), front_pad(dt), A, front_pad(Bm), front_pad(Cm))[:, META_PAD:]
    y = y + D_skip[:, None] * xs
    y = y.reshape(b, L, D_SSD)
    return group_rmsnorm(y * jax.nn.silu(z), norm_g, SSD_GROUPS)

def short_conv_branch(gate_b, gate_c, h, conv_w, norm_g):
    v = causal_dwconv(gate_c * h, conv_w)
    return group_rmsnorm(gate_b * v, norm_g, SC_GROUPS)

def hier_moe(u, wg_r, bg_r, we_r, be_r, w_gate, w_up, w_down):
    b, L, d = u.shape
    t = u.reshape(b * L, d)
    p_group = jax.nn.softmax((t @ wg_r + bg_r).astype(jnp.float32), axis=-1)
    g_val, g_idx = lax.top_k(p_group, 1)
    e_logits = (t @ we_r + be_r).astype(jnp.float32).reshape(-1, N_EXPERT_GROUPS, EXPERTS_PER_GROUP)
    sel = jnp.take_along_axis(e_logits, g_idx[:, :, None], axis=1)[:, 0]
    top_v, top_i = lax.top_k(sel, TOP_K)
    top_w = jax.nn.softmax(top_v, axis=-1)
    in_w = jnp.einsum('tk,tke->te', top_w, jax.nn.one_hot(top_i, EXPERTS_PER_GROUP, dtype=jnp.float32))
    grp_w = jax.nn.one_hot(g_idx[:, 0], N_EXPERT_GROUPS, dtype=jnp.float32) * g_val
    combine = (grp_w[:, :, None] * in_w[:, None, :]).reshape(-1, N_EXPERTS).astype(u.dtype)
    out = jnp.zeros_like(t)
    for e in range(N_EXPERTS):
        h = jax.nn.silu(t @ w_gate[e]) * (t @ w_up[e])
        out = out + combine[:, e:e + 1] * (h @ w_down[e])
    return out.reshape(b, L, d)

def second_inputs(seed: int = 0) -> dict:
    key = jax.random.key(seed)
    ks = jax.random.split(key, 24)
    f32 = jnp.float32
    nrm = lambda k, shp, s: (jax.random.normal(k, shp, f32) * s)
    dt0 = jnp.exp(jax.random.uniform(ks[6], (DEPTH_2, SSD_HEADS), f32, np.log(1e-3), np.log(1e-1)))
    return {
        "x": jax.random.normal(ks[0], (BATCH, SEQ, D_MODEL), f32),
        "meta_tokens": nrm(ks[1], (N_META, D_MODEL), 1.0),
        "norm_mix": 1.0 + nrm(ks[2], (DEPTH_2, D_MODEL), 0.02),
        "w_in": nrm(ks[3], (DEPTH_2, D_MODEL, IN_COLS), D_MODEL ** -0.5),
        "ssd_conv_w": nrm(ks[4], (DEPTH_2, SSD_CONV, D_XBC), SSD_CONV ** -0.5),
        "ssd_conv_b": nrm(ks[5], (DEPTH_2, D_XBC), 0.02),
        "dt_bias": dt0 + jnp.log(-jnp.expm1(-dt0)),
        "A_log": jnp.log(jax.random.uniform(ks[7], (DEPTH_2, SSD_HEADS), f32, 1.0, 16.0)),
        "D_skip": 1.0 + nrm(ks[8], (DEPTH_2, SSD_HEADS), 0.1),
        "ssd_norm": 1.0 + nrm(ks[9], (DEPTH_2, D_SSD), 0.02),
        "sc_conv_w": nrm(ks[10], (DEPTH_2, SC_CONV, D_SC), SC_CONV ** -0.5),
        "sc_norm": 1.0 + nrm(ks[11], (DEPTH_2, D_SC), 0.02),
        "w_out": nrm(ks[12], (DEPTH_2, D_MIX, D_MODEL), D_MIX ** -0.5),
        "norm_ffn": 1.0 + nrm(ks[13], (DEPTH_2, D_MODEL), 0.02),
        "router_group_w": nrm(ks[14], (DEPTH_2, D_MODEL, N_EXPERT_GROUPS), D_MODEL ** -0.5),
        "router_group_b": nrm(ks[15], (DEPTH_2, N_EXPERT_GROUPS), 0.01),
        "router_expert_w": nrm(ks[16], (DEPTH_2, D_MODEL, N_EXPERTS), D_MODEL ** -0.5),
        "router_expert_b": nrm(ks[17], (DEPTH_2, N_EXPERTS), 0.01),
        "expert_w_gate": nrm(ks[18], (DEPTH_2, N_EXPERTS, D_MODEL, D_EXPERT), D_MODEL ** -0.5),
        "expert_w_up": nrm(ks[19], (DEPTH_2, N_EXPERTS, D_MODEL, D_EXPERT), D_MODEL ** -0.5),
        "expert_w_down": nrm(ks[20], (DEPTH_2, N_EXPERTS, D_EXPERT, D_MODEL), D_EXPERT ** -0.5),
        "norm_final": 1.0 + nrm(ks[21], (D_MODEL,), 0.02),
    }

def second_block(x, meta_tokens, norm_mix, w_in, ssd_conv_w, ssd_conv_b, dt_bias, A_log, D_skip,
              ssd_norm, sc_conv_w, sc_norm, w_out, norm_ffn, router_group_w, router_group_b,
              router_expert_w, router_expert_b, expert_w_gate, expert_w_up, expert_w_down,
              norm_final):
    b = x.shape[0]
    meta = jnp.broadcast_to(meta_tokens.astype(x.dtype)[None], (b, N_META, D_MODEL))
    h = jnp.concatenate([meta, x], axis=1)
    o_z = D_SSD
    o_xbc = o_z + D_XBC
    o_dt = o_xbc + SSD_HEADS
    o_b = o_dt + D_SC
    o_c = o_b + D_SC
    for l in range(DEPTH_2):
        u = rmsnorm(h, norm_mix[l])
        proj = u @ w_in[l]
        y_ssd = ssd_branch(proj[..., :o_z], proj[..., o_z:o_xbc], proj[..., o_xbc:o_dt],
                           ssd_conv_w[l], ssd_conv_b[l], dt_bias[l], A_log[l], D_skip[l], ssd_norm[l])
        y_sc = short_conv_branch(proj[..., o_dt:o_b], proj[..., o_b:o_c], proj[..., o_c:],
                                 sc_conv_w[l], sc_norm[l])
        h = h + jnp.concatenate([y_ssd, y_sc], axis=-1) @ w_out[l]
        u2 = rmsnorm(h, norm_ffn[l])
        h = h + hier_moe(u2, router_group_w[l], router_group_b[l], router_expert_w[l],
                         router_expert_b[l], expert_w_gate[l], expert_w_up[l], expert_w_down[l])
    return rmsnorm(h, norm_final)[:, N_META:]


def setup_inputs(seed=0):
    out = dict(first_inputs(seed))
    for name, value in second_inputs(seed + 1).items():
        if name != "x":
            out[name + "_2"] = value
    return out


def reference(
    x, c, ctx, c_ctx, w_mod, b_mod, ln1_g, ln1_b, ln2_g, ln2_b, ffn_w_gate, ffn_w_up,
    ffn_conv_w, ffn_conv_b, ffn_w_down, ab_w_in, mla_q_norm, mla_w_qb, mla_kv_norm, mla_w_kvb,
    swa_sink, ab_w_out, diff_w_in, diff_lam_q1, diff_lam_k1, diff_lam_q2, diff_lam_k2,
    diff_subln_g, diff_w_out, meta_tokens_2, norm_mix_2, w_in_2, ssd_conv_w_2, ssd_conv_b_2,
    dt_bias_2, A_log_2, D_skip_2, ssd_norm_2, sc_conv_w_2, sc_norm_2, w_out_2, norm_ffn_2,
    router_group_w_2, router_group_b_2, router_expert_w_2, router_expert_b_2, expert_w_gate_2,
    expert_w_up_2, expert_w_down_2, norm_final_2,
):
    x = first_block(
        x, c, ctx, c_ctx, w_mod, b_mod, ln1_g, ln1_b, ln2_g, ln2_b, ffn_w_gate, ffn_w_up,
        ffn_conv_w, ffn_conv_b, ffn_w_down, ab_w_in, mla_q_norm, mla_w_qb, mla_kv_norm,
        mla_w_kvb, swa_sink, ab_w_out, diff_w_in, diff_lam_q1, diff_lam_k1, diff_lam_q2,
        diff_lam_k2, diff_subln_g, diff_w_out,
    )
    return second_block(
        x, meta_tokens_2, norm_mix_2, w_in_2, ssd_conv_w_2, ssd_conv_b_2, dt_bias_2, A_log_2,
        D_skip_2, ssd_norm_2, sc_conv_w_2, sc_norm_2, w_out_2, norm_ffn_2, router_group_w_2,
        router_group_b_2, router_expert_w_2, router_expert_b_2, expert_w_gate_2, expert_w_up_2,
        expert_w_down_2, norm_final_2,
    )


_drawn_inputs = setup_inputs


def setup_inputs(seed=0):
    import zlib

    import numpy as np

    out = dict(_drawn_inputs(seed))
    spreads = {}
    factors = {'b_mod': 4.126,
     'ffn_conv_b': 6.977,
     'mla_q_norm': 8.0,
     'mla_w_qb': 3.184,
     'mla_kv_norm': 8.0,
     'swa_sink': 8.0,
     'diff_lam_q1': 3.116,
     'diff_lam_k2': 5.614,
     'diff_subln_g': 35.689,
     'sc_norm_2': 3.288,
     'norm_ffn_2': 2.896,
     'router_group_b_2': 33.216,
     'router_expert_b_2': 3.875,
     'norm_final_2': 22.785}
    for name, (base, spread) in spreads.items():
        noise = np.random.default_rng([zlib.crc32(name.encode()), seed]).standard_normal(out[name].shape)
        drawn = base * np.exp(spread * noise) if base else spread * noise
        out[name] = __import__('jax').numpy.asarray(drawn.astype(out[name].dtype))
    for name, factor in factors.items():
        out[name] = (out[name] * factor).astype(out[name].dtype)
    return out
```

```python
import math
from contextlib import ExitStack

import numpy as np
import concourse.bass as bass
from concourse import mybir

F32 = mybir.dt.float32
ALU = mybir.AluOpType
ACT = mybir.ActivationFunctionType
AX = mybir.AxisListType

D = 1024
F = 2816
NF = F // 128
S = 256
NT = 272
TOFF = [0, 16, 144]
TLEN = [16, 128, 128]
NE = 16
ALPHA = 4.0 ** 0.25
LAM_INIT = 0.8 - 0.6 * math.exp(-0.3)
NEG = -1e30
SLOTS = 4
SLOT = 4096
ARENA = 23500



def vec_layout():
    at, n = {}, 0
    for name, cols in (
            ("bmod0", 48), ("bmod1", 48),
            ("ln1g0", 8), ("ln1b0", 8), ("ln2g0", 8), ("ln2b0", 8),
            ("ln1g1", 8), ("ln1b1", 8), ("ln2g1", 8), ("ln2b1", 8),
            ("cw0", 66), ("cw1", 66), ("cb0", 22), ("cb1", 22),
            ("qnorm", 2), ("kvnorm", 1), ("subln", 1),
            ("nmix", 8), ("scw", 64), ("scb", 16), ("dskip", 8), ("ssdn", 8),
            ("shw", 24), ("shn", 8), ("nffn", 8), ("nfin", 8),
            ("dtb", 16), ("alog", 16), ("rb", 20), ("sink", 8), ("lam", 256),
            ("cond", 16), ("rw", 160), ("wdt", 128)):
        at[name] = (n, cols)
        n += cols
    return at, n


def const_layout():
    at, n = {}, 0
    for name, cols in (
            ("ident", 128), ("o1024", 128), ("o256", 128), ("o128", 128), ("blk64", 128),
            ("ones", 128), ("tri", 128), ("sfx", 128), ("r128", 128), ("r96", 128),
            ("maska", 128), ("maskb", 128),
            ("cos128", 256), ("sin128", 256), ("cos96", 256), ("sin96", 256),
            ("rank", 4), ("eps5", 1), ("eps6", 1)):
        at[name] = (n, cols)
        n += cols
    return at, n


def rope_table(dim):
    row = np.repeat(np.arange(S // 64), 64).astype(np.float32)
    col = np.tile(np.arange(64), S // 64).astype(np.float32)
    q = dim // 4
    fr = (np.float32(10000.0) ** (-np.arange(q, dtype=np.float32) / np.float32(q))).astype(np.float32)
    ar = row[:, None] * fr
    ac = col[:, None] * fr
    cos = np.concatenate([np.cos(ar), np.cos(ar), np.cos(ac), np.cos(ac)], -1)
    sin = np.concatenate([np.sin(ar), np.sin(ar), np.sin(ac), np.sin(ac)], -1)
    return cos.T.astype(np.float32), sin.T.astype(np.float32)


def rope_perm(dim):
    q = dim // 4
    r = np.zeros((dim, dim), np.float32)
    for i in range(q):
        for b in (0, 2 * q):
            r[b + q + i, b + i] = -1.0
            r[b + i, b + q + i] = 1.0
    return r


def consts():
    at, n = const_layout()
    c = np.zeros((128, n), np.float32)

    def put(name, v):
        o, k = at[name]
        c[:v.shape[0], o:o + v.shape[1]] = v

    i = np.arange(128)
    put("ident", np.eye(128, dtype=np.float32))
    put("o1024", np.full((128, 128), 1 / 1024, np.float32))
    put("o256", np.full((128, 128), 1 / 256, np.float32))
    put("o128", np.full((128, 128), 1 / 128, np.float32))
    put("blk64", (i[:, None] // 64 == i[None, :] // 64).astype(np.float32) / 64)
    put("ones", np.ones((128, 128), np.float32))
    put("tri", (i[:, None] <= i[None, :]).astype(np.float32))
    put("sfx", (i[:, None] > i[None, :]).astype(np.float32))
    r128 = np.zeros((128, 128), np.float32)
    r128[:64, :64] = r128[64:, 64:] = rope_perm(64)
    put("r128", r128)
    r96 = np.zeros((128, 128), np.float32)
    r96[64:96, 64:96] = rope_perm(32)
    put("r96", r96)
    put("maska", np.where(i[None, :] <= i[:, None], 0, NEG).astype(np.float32))
    put("maskb", np.where(i[None, :] >= i[:, None], 0, NEG).astype(np.float32))
    c64, s64 = rope_table(64)
    put("cos128", np.concatenate([c64, c64]))
    put("sin128", np.concatenate([s64, s64]))
    c32, s32 = rope_table(32)
    put("cos96", np.concatenate([np.ones((64, S), np.float32), c32]))
    put("sin96", np.concatenate([np.zeros((64, S), np.float32), s32]))
    put("rank", np.tile(np.array([[4, 3, 2, 1]], np.float32), (128, 1)))
    put("eps5", np.full((128, 1), 1e-5, np.float32))
    put("eps6", np.full((128, 1), 1e-6, np.float32))
    return c


QPERM = [h + 4 * k for h in range(4) for k in range(2)]


def chunk_plan():
    mod = lambda l, a, b: [(("mod", l, i), 4096) for i in range(a, b)]
    p = mod(0, 0, 4)
    p += [(("abin", 0), 4096), (("abin", 1), 8 * 416), (("abin", 2), 8 * 256), (("qb",), 1536), (("kvb",), 1024)]
    p += mod(0, 4, 12)
    p += [(("about", i), 4096) for i in range(2)]
    p += ffn_plan(0)
    p += [(("din", 2 + i), 4096) for i in range(4)] + [(("din", i), 4096) for i in range(2)]
    p += [(("dout", i), 4096) for i in range(2)]
    p += ffn_plan(1)
    p += [(("win", i), 4096) for i in range(12)]
    p += [(("wout", i), 4096) for i in range(4)]
    for e in range(NE):
        p += [(("eg", e), 4096), (("eu", e), 4096)]
    p += [(("ed", e), 4096) for e in range(NE)]
    return p


def ffn_plan(l):
    p = []
    for i in range(NF // 2):
        p.append((("gu", l, i), 4096))
        if l == 0:
            p.append((("mod", 1, i), 4096))
    if l == 0:
        p.append((("mod", 1, 11), 4096))
    for i in range(0, 8):
        p.append((("down", l, i), NF * 128))
    return p


def pack_k(w):
    k, m = w.shape
    return w.reshape(k // 128, 128, m).transpose(1, 0, 2).reshape(128, -1)


def host_chunk(x, key):
    kind = key[0]
    if kind == "mod":
        return pack_k(x["w_mod"][key[1]][:, 512 * key[2]:512 * key[2] + 512])
    if kind == "abin":
        a, b = ((0, 512), (512, 928), (928, 1184))[key[1]]
        w = x["ab_w_in"][0]
        qs = w[:, 256:768].reshape(D, 8, 64)[:, QPERM].reshape(D, 512)
        return pack_k(np.concatenate([w[:, :256], qs, w[:, 768:]], 1)[:, a:b])
    if kind == "qb":
        return pack_k(x["mla_w_qb"][0])
    if kind == "kvb":
        w = x["mla_w_kvb"][0].reshape(128, 8, 2, 64)
        return w.transpose(0, 2, 1, 3).reshape(128, 1024)
    if kind == "about":
        w = x["ab_w_out"][0]
        sw = w[512:].reshape(8, 64, D)[QPERM].reshape(512, D)
        return pack_k(np.concatenate([w[:512], sw], 0)[:, 512 * key[1]:512 * key[1] + 512])
    if kind == "gu":
        l, i = key[1:]
        g = x["ffn_w_gate"][l][:, 256 * i:256 * i + 256]
        u = x["ffn_w_up"][l][:, 256 * i:256 * i + 256]
        return pack_k(np.concatenate([g, u], 1))
    if kind == "down":
        return pack_k(x["ffn_w_down"][key[1]][:, 128 * key[2]:128 * key[2] + 128])
    if kind == "din":
        return pack_k(x["diff_w_in"][0][:, 512 * key[1]:512 * key[1] + 512])
    if kind == "dout":
        return pack_k(x["diff_w_out"][0][:, 512 * key[1]:512 * key[1] + 512])
    if kind == "win":
        w = x["w_in_2"][0]
        bch = w[:, 3088:].reshape(D, 3, 8, 128).transpose(0, 2, 1, 3).reshape(D, 3072)
        i = key[1]
        return pack_k(w[:, 512 * i:512 * i + 512] if i < 6 else bch[:, 512 * (i - 6):512 * (i - 6) + 512])
    if kind == "wout":
        return pack_k(x["w_out_2"][0][:, 256 * key[1]:256 * key[1] + 256])
    if kind == "eg":
        return pack_k(x["expert_w_gate_2"][0, key[1]])
    if kind == "eu":
        return pack_k(x["expert_w_up_2"][0, key[1]])
    if kind == "ed":
        return pack_k(x["expert_w_down_2"][0, key[1]])


def host_vec(x):
    at, n = vec_layout()
    v = np.zeros((128, n), np.float32)

    def cols(a):
        return np.asarray(a).reshape(-1, 128).T

    def put(name, a):
        o, k = at[name]
        v[:, o:o + k] = a

    for l in range(2):
        put(f"bmod{l}", cols(x["b_mod"][l]))
        for nm in ("ln1", "ln2"):
            put(f"{nm}g{l}", cols(x[f"{nm}_g"][l]))
            put(f"{nm}b{l}", cols(x[f"{nm}_b"][l]))
        put(f"cw{l}", cols(x["ffn_conv_w"][l]))
        put(f"cb{l}", cols(x["ffn_conv_b"][l]))
    put("qnorm", cols(x["mla_q_norm"][0]))
    put("kvnorm", cols(x["mla_kv_norm"][0]))
    put("subln", cols(x["diff_subln_g"][0]))
    put("nmix", cols(x["norm_mix_2"][0]))
    put("scw", cols(x["ssd_conv_w_2"][0]))
    put("scb", cols(x["ssd_conv_b_2"][0]))
    put("dskip", cols(np.repeat(x["D_skip_2"][0], 64)))
    put("ssdn", cols(x["ssd_norm_2"][0]))
    put("shw", cols(x["sc_conv_w_2"][0]))
    put("shn", cols(x["sc_norm_2"][0]))
    put("nffn", cols(x["norm_ffn_2"][0]))
    put("nfin", cols(x["norm_final_2"]))
    put("dtb", x["dt_bias_2"][0][None])
    put("alog", x["A_log_2"][0][None])
    put("rb", np.concatenate([x["router_group_b_2"][0], x["router_expert_b_2"][0]])[None])
    put("sink", x["swa_sink"][0][None])
    put("lam", np.concatenate([x["diff_lam_q1"][0], x["diff_lam_k1"][0],
                               x["diff_lam_q2"][0], x["diff_lam_k2"][0]])[None])
    put("cond", np.stack([cols(x["c"][0]), cols(x["c_ctx"])], -1).reshape(128, 16))
    put("rw", pack_k(np.concatenate([x["router_group_w_2"][0], x["router_expert_w_2"][0]], 1)))
    put("wdt", pack_k(x["w_in_2"][0][:, 3072:3088]))
    return v



class Queue:

    def __init__(self, sem):
        self.sem, self.n, self.items, self.seen = sem, 0, [], {}

    def wait(self, *toks):
        for t in toks:
            if t is not None and self.seen.get(t[0].name, 0) < t[1]:
                self.seen[t[0].name] = t[1]
                self.items.append((None, t))

    def do(self, fn, *toks, sig=True):
        self.wait(*toks)
        if sig:
            self.n += 1
        self.items.append((fn, sig))
        return (self.sem, self.n) if sig else None

    @property
    def last(self):
        return (self.sem, self.n) if self.n else None

    def emit(self, eng):
        for fn, a in self.items:
            if fn is None:
                eng.wait_ge(a[0], a[1])
            else:
                ins = fn(eng)
                if a:
                    ins.then_inc(self.sem, 1)


def build(nc, wts, xin, meta, vecs, csts, out):
    vat, nv = vec_layout()
    cat, ncst = const_layout()
    plan = chunk_plan()

    with ExitStack() as ctx:
        sb = lambda name, shape: ctx.enter_context(nc.sbuf_tensor(name, shape, F32))
        sem = lambda name: ctx.enter_context(nc.semaphore(name))

        ring = sb("ring", [128, SLOTS * SLOT])
        X = sb("X", [128, 8, 512])
        HB = sb("HB", [128, 8, 512])
        arena = sb("arena", [128, ARENA])
        vec = sb("vec", [128, nv])
        cst = sb("cst", [128, ncst])
        modv = [sb(f"modv{l}", [128, 48, 2]) for l in range(2)]
        scond = sb("scond", [128, 16])
        fold = sb("fold", [128, 8, 8])
        lnc = sb("lnc", [128, 4, 8])
        small = sb("small", [128, 256])
        MT = sb("MT", [128, 128])
        ps = ctx.enter_context(nc.psum_tensor("ps", [128, 8, 512], F32))

        pe, act, dve = (Queue(sem(n)) for n in ("s_pe", "s_act", "s_dve"))
        s_w = [sem(f"s_w{i}") for i in range(SLOTS)]
        s_v, s_c, s_x, s_m, s_out = (sem(n) for n in ("s_v", "s_c", "s_x", "s_m", "s_out"))
        VEC, CST, XIN, META = (s_v, 16), (s_c, 16), (s_x, 16), (s_m, 16)

        def V(name, i=0, n=1):
            return vec[:, vat[name][0] + i:vat[name][0] + i + n]

        def C(name, n=None):
            return cst[:, cat[name][0]:cat[name][0] + (n or cat[name][1])]

        ident = C("ident")
        EPS5, EPS6 = C("eps5"), C("eps6")

        bank_free = [None] * 8
        bank_at = [0]

        def take():
            b = bank_at[0] % 8
            bank_at[0] += 1
            pe.wait(bank_free[b])
            return b

        def free(b, tok):
            bank_free[b] = tok

        used = []
        chunk_at = [0]
        widths = dict(plan)

        def chunk(*key):
            n = chunk_at[0]
            assert plan[n][0] == key, (plan[n], key)
            chunk_at[0] += 1
            pe.wait((s_w[n % SLOTS], 16 * (n // SLOTS + 1)))
            return ring[:, (n % SLOTS) * SLOT:(n % SLOTS) * SLOT + plan[n][1]]

        def chunk_done():
            used.append(pe.last)

        def mm(o, lhsT, rhs, start, stop, *toks, sig=False):
            return pe.do(lambda e: e.matmul(o, lhsT, rhs, start=start, stop=stop), *toks, sig=sig)

        def tr(o, i, idn, *toks, sig=False):
            return pe.do(lambda e: e.transpose(o, i, idn), *toks, sig=sig)

        def A(o, i, f, *toks, **kw):
            return act.do(lambda e: e.activation(o, i, f, **kw), *toks)

        def TT(o, a, b, op, *toks):
            return dve.do(lambda e: e.tensor_tensor(o, a, b, op), *toks)

        def TS(o, a, s1, s2, op0, op1, *toks):
            if s2 is None:
                return dve.do(lambda e: e.tensor_scalar(o, a, s1, None, op0), *toks)
            return dve.do(lambda e: e.tensor_scalar(o, a, s1, s2, op0, op1), *toks)

        def STT(o, a, s, b, op0, op1, *toks):
            return dve.do(lambda e: e.scalar_tensor_tensor(out=o, in0=a, scalar=s, in1=b, op0=op0, op1=op1), *toks)

        def CP(o, a, *toks):
            return dve.do(lambda e: e.tensor_copy(o, a), *toks)

        def RMAX(o, a, *toks):
            return dve.do(lambda e: e.tensor_reduce(o, a, AX.X, ALU.max), *toks)

        def RECIP(o, a, *toks):
            return dve.do(lambda e: e.reciprocal(o, a), *toks)

        top = [0]

        def area(*shape):
            n = int(np.prod(shape))
            a = arena[:, top[0]:top[0] + n]
            top[0] += n
            assert top[0] <= ARENA, top[0]
            if len(shape) == 1:
                return a
            if len(shape) == 2:
                return a.rearrange("p (a b) -> p a b", a=shape[0])
            return a.rearrange("p (a b c) -> p a b c", a=shape[0], b=shape[1])

        def new_phase():
            top[0] = 0
            now = [pe.last, act.last, dve.last]
            for q in (pe, act, dve):
                q.wait(*now)

        pe.wait(VEC, CST)
        act.wait(VEC, CST)
        dve.wait(VEC, CST)
        t_cond = A(scond[:, :], V("cond", 0, 16), ACT.Silu)
        mod_tok = {}

        def mod_chunk(l, i):
            w = chunk("mod", l, i).rearrange("p (k m) -> p k m", k=8)
            b = take()
            for m in range(4):
                for k in range(8):
                    t = mm(ps[:, b, 2 * m:2 * m + 2], w[:, k, 128 * m:128 * m + 128],
                           scond[:, 2 * k:2 * k + 2], k == 0, k == 7, t_cond, sig=(m == 3 and k == 7))
            chunk_done()
            bm = V(f"bmod{l}", 4 * i, 4).unsqueeze(2).to_broadcast([128, 4, 2])
            o = modv[l][:, 4 * i:4 * i + 4, :]
            t = TT(o, ps[:, b, 0:8].rearrange("p (m s) -> p m s", s=2), bm, ALU.add, t)
            free(b, t)
            if i in (2, 3, 8, 9):
                t = TS(o, o, 1.0, None, ALU.add, None, t)
            mod_tok[l, i // 2] = t

        def halves(n):
            return ((0, 0, 256), (1, 256, 512)) if n == 512 else ((0, 0, 256),)

        def fold_mod(l, sc, sh, gname, bname, lg):
            t = None
            for s in range(2):
                TT(fold[:, s, :], V(f"{gname}{lg}", 0, 8), modv[l][:, sc:sc + 8, s], ALU.mult, mod_tok[l, sc // 8])
                t = TT(fold[:, 4 + s, :], V(f"{bname}{lg}", 0, 8), modv[l][:, sc:sc + 8, s], ALU.mult)
                t = TT(fold[:, 2 + s, :], fold[:, 4 + s, :], modv[l][:, sh:sh + 8, s], ALU.add, t, mod_tok[l, sh // 8])
            TS(lnc[:, 0, :], V(f"{gname}{lg}", 0, 8), ALPHA, None, ALU.mult, None)
            return TS(lnc[:, 1, :], V(f"{bname}{lg}", 0, 8), ALPHA, None, ALU.mult, None)

        def layer_norm(y, ytok, n, sq, rstd, g, b, gtok, hout, xout):
            bm = take()
            for j in range(8):
                t = mm(ps[:, bm, 0:n], C("o1024"), y[:, j, :], j == 0, j == 7, ytok[j], sig=(j == 7))
            bv = take()
            for j in range(8):
                c = TT(y[:, j, :], y[:, j, :], ps[:, bm, 0:n], ALU.subtract, t)
                q = A(sq[:, j, :], y[:, j, :], ACT.Square, c)
                v = mm(ps[:, bv, 0:n], C("o1024"), sq[:, j, :], j == 0, j == 7, q, sig=(j == 7))
            free(bm, c)
            s = A(rstd, ps[:, bv, 0:n], ACT.Sqrt, v, bias=EPS5, scale=1.0)
            free(bv, s)
            r = RECIP(rstd, rstd, s)
            htok, xtok = [], []
            for j in range(8):
                t = TT(y[:, j, :], y[:, j, :], rstd, ALU.mult, r)
                if hout is not None:
                    for s, a, e in halves(n):
                        h = TS(hout[:, j, a:e], y[:, j, a:e], fold[:, s, j:j + 1], fold[:, 2 + s, j:j + 1],
                               ALU.mult, ALU.add, t, gtok)
                    htok.append(h)
                    t = h
                xtok.append(A(xout[:, j, :], y[:, j, :], ACT.Identity, t, gtok, scale=g[:, j:j + 1], bias=b[:, j:j + 1]))
            return htok, xtok

        def out_proj(key, nk, src, stok, n, mt_per, l, gt, nxt):
            ytok = []
            for i in range(8 // mt_per):
                w = chunk(*key, i).rearrange("p (k m) -> p k m", k=nk)
                for m in range(mt_per):
                    j = i * mt_per + m
                    b = take()
                    for k in range(nk):
                        t = mm(ps[:, b, 0:n], w[:, k, 128 * m:128 * m + 128], src[:, k, 0:n], k == 0, k == nk - 1,
                               stok[k], sig=(k == nk - 1))
                    for s, a, e in halves(n):
                        y = STT(X[:, j, a:e], ps[:, b, a:e], modv[l][:, gt + j, s:s + 1], X[:, j, a:e],
                                ALU.mult, ALU.add, t, mod_tok[l, gt // 8], nxt)
                    free(b, y)
                    ytok.append(y)
                chunk_done()
            return ytok

        def ffn(l, htok, n):
            new_phase()
            H2 = area(NF, n)
            T = area(3, n)
            tfree = [None] * 3
            sfree = [None] * 3
            SG = area(3, n)
            nh = n // 256
            stok = []
            f = 0
            for i in range(NF // 2):
                w = chunk("gu", l, i).rearrange("p (k m) -> p k m", k=8)
                for m in range(2):
                    z = f % 3
                    bg, bu = take(), take()
                    for k in range(8):
                        tg = mm(ps[:, bg, 0:n], w[:, k, 128 * m:128 * m + 128], HB[:, k, 0:n], k == 0, k == 7,
                                htok[k], sig=(k == 7))
                    for k in range(8):
                        tu = mm(ps[:, bu, 0:n], w[:, k, 256 + 128 * m:384 + 128 * m], HB[:, k, 0:n], k == 0, k == 7,
                                sig=(k == 7))
                    cw = lambda a: V(f"cw{l}", 22 * a + f, 1)
                    g3 = ps[:, bg, 0:n].rearrange("p (s t) -> p s t", s=nh)
                    t3 = T[:, z, :].rearrange("p (s t) -> p s t", s=nh)
                    t = A(T[:, z, :], ps[:, bg, 0:n], ACT.Identity, tg, tfree[z], scale=cw(1), bias=V(f"cb{l}", f))
                    t = STT(t3[:, :, 1:256], g3[:, :, 0:255], cw(0), t3[:, :, 1:256], ALU.mult, ALU.add, t)
                    t = STT(t3[:, :, 0:255], g3[:, :, 1:256], cw(2), t3[:, :, 0:255], ALU.mult, ALU.add, t)
                    free(bg, t)
                    t = A(SG[:, z, :], T[:, z, :], ACT.Silu, t, sfree[z])
                    tfree[z] = t
                    t = TT(H2[:, f, :], SG[:, z, :], ps[:, bu, 0:n], ALU.mult, t, tu)
                    free(bu, t)
                    sfree[z] = t
                    stok.append(t)
                    f += 1
                chunk_done()
                if l == 0:
                    mod_chunk(1, i)
            if l == 0:
                mod_chunk(1, 11)
            return out_proj(("down", l), NF, H2, stok, n, 1, l, 40, None)

        def run_jobs(jobs, stages):
            depth = len(stages)
            state = [None] * len(jobs)
            for i in range(len(jobs) + depth - 1):
                for d, st in enumerate(stages):
                    j = i - d
                    if 0 <= j < len(jobs):
                        state[j] = st(j, jobs[j], state[j])
            return state

        act.wait(XIN)
        dve.wait(XIN)
        for i in range(4):
            mod_chunk(0, i)
        htok = []
        for j in range(8):
            for s, a, e in halves(512):
                t = TS(HB[:, j, a:e], X[:, j, a:e], modv[0][:, 8 + j, s:s + 1], modv[0][:, j, s:s + 1],
                       ALU.mult, ALU.add, mod_tok[0, 0], mod_tok[0, 1])
            htok.append(t)
        t_ax = [A(X[:, j, :], X[:, j, :], ACT.Copy, htok[j], scale=ALPHA) for j in range(8)]

        QA = area(2, 512)
        QN = area(2, 512)
        SQ = area(2, 512)
        RS = area(512)
        QS = area(4, 512)
        KS = area(512)
        KV = area(512)
        KR = area(512)
        QM = area(8, 512)
        KM = area(8, 512)
        VM = area(4, 512)
        VS = area(4, 128)
        TMP = area(2, 512)
        P = area(2, 2, 512)
        PT = area(2, 4, 256)

        def proj_T(w, c0, m, hk=8, rhs=None, rtok=None):
            b = take()
            for k in range(hk):
                t = mm(ps[0:m, b, :], w[:, k, c0:c0 + m], HB[:, k, :] if rhs is None else rhs(k), k == 0, k == hk - 1,
                       (rtok or htok)[k], sig=(k == hk - 1))
            return b, t

        w = chunk("abin", 0).rearrange("p (k m) -> p k m", k=8)
        qa_tok = []
        for m in range(2):
            b, t = proj_T(w, 128 * m, 128)
            t = A(QA[:, m, :], ps[:, b, :], ACT.Copy, t)
            free(b, t)
            qa_tok.append(t)

        tmp_free = [None, None]
        rope_n = [0]

        def rope(dst, rows, perm, cos, sin, tok, extra=None):
            z = rope_n[0] % 2
            rope_n[0] += 1
            b = take()
            t = mm(ps[0:rows, b, 0:256], C(perm, rows)[0:rows, :], dst[0:rows, 0:256], True, True, tok, sig=True)
            tm = TMP[0:rows, z, 0:256]
            t1 = TT(tm, ps[0:rows, b, 0:256], C(sin)[0:rows, :], ALU.mult, t, tmp_free[z])
            free(b, t1)
            t2 = TT(dst[0:rows, 0:256], dst[0:rows, 0:256], C(cos)[0:rows, :], ALU.mult, t)
            t3 = TT(dst[0:rows, 0:256], dst[0:rows, 0:256], tm, ALU.add, t1, t2)
            tmp_free[z] = t3
            return t3

        qs_tok, qs_raw = [None] * 4, [None] * 4
        for m in range(2):
            b, t = proj_T(w, 256 + 128 * m, 128)
            qs_raw[m] = A(QS[:, m, :], ps[:, b, :], ACT.Copy, t)
            free(b, qs_raw[m])
        chunk_done()
        w = chunk("abin", 1).rearrange("p (k m) -> p k m", k=8)
        for m in range(2, 4):
            b, t = proj_T(w, 128 * (m - 2), 128)
            qs_raw[m] = A(QS[:, m, :], ps[:, b, :], ACT.Copy, t)
            free(b, qs_raw[m])
        b, t = proj_T(w, 256, 128)
        t_kv = A(KV[:, :], ps[:, b, :], ACT.Copy, t)
        free(b, t_kv)
        b, t = proj_T(w, 320, 96)
        t_kr = A(KR[0:96, :], ps[0:96, b, :], ACT.Copy, t)
        free(b, t_kr)
        chunk_done()
        w = chunk("abin", 2).rearrange("p (k m) -> p k m", k=8)
        b, t = proj_T(w, 0, 128)
        t_ks = A(KS[:, :], ps[:, b, :], ACT.Copy, t)
        free(b, t_ks)
        b = take()
        for c in range(4):
            for k in range(8):
                t = mm(ps[:, b, 128 * c:128 * c + 128], HB[:, k, 128 * c:128 * c + 128], w[:, k, 128:256],
                       k == 0, k == 7, sig=(c == 3 and k == 7))
        chunk_done()
        t_vs = A(VS, ps[:, b, :].rearrange("p (c m) -> p c m", c=4), ACT.Copy, t)
        free(b, t_vs)

        def rms_low(src, toks, n, ones, gname, dst):
            b = take()
            for m in range(n):
                q = A(SQ[:, m, :], src(m), ACT.Square, toks[m])
                t = mm(ps[:, b, :], C(ones), SQ[:, m, :], m == 0, m == n - 1, q, sig=(m == n - 1))
            s = A(RS[:, :], ps[:, b, :], ACT.Sqrt, t, bias=EPS6, scale=1.0)
            free(b, s)
            r = RECIP(RS[:, :], RS[:, :], s)
            return [STT(dst(m), src(m), V(gname, m), RS[:, :], ALU.mult, ALU.mult, r) for m in range(n)]

        qn_tok = rms_low(lambda m: QA[:, m, :], qa_tok, 2, "o256", "qnorm", lambda m: QN[:, m, :])
        act.wait(qn_tok[-1])
        kv_tok = rms_low(lambda m: KV[:, :], [t_kv], 1, "o128", "kvnorm", lambda m: KV[:, :])

        w = chunk("qb").rearrange("p (k m) -> p k m", k=2)
        qm_raw = []
        for h in range(8):
            b, t = proj_T(w, 96 * h, 96, 2, lambda k: QN[:, k, :], qn_tok)
            t = A(QM[0:96, h, :], ps[0:96, b, :], ACT.Copy, t)
            free(b, t)
            qm_raw.append(t)
        chunk_done()
        w = chunk("kvb").rearrange("p (k m) -> p k m", k=1)
        km_tok, vm_tok = [], []
        for h in range(8):
            b, t = proj_T(w, 64 * h, 64, 1, lambda k: KV[:, :], kv_tok)
            t = A(KM[0:64, h, :], ps[0:64, b, :], ACT.Copy, t)
            free(b, t)
            km_tok.append(t)
        for c in range(4):
            b = take()
            t = mm(ps[:, b, :], KV[:, 128 * c:128 * c + 128], w[:, 0, 512:1024], True, True, sig=True)
            t = A(VM[:, c, :], ps[:, b, :], ACT.Copy, t)
            free(b, t)
            vm_tok.append(t)
        chunk_done()

        t_ks = rope(KS, 128, "r128", "cos128", "sin128", t_ks)
        t_kr = rope(KR, 96, "r96", "cos96", "sin96", t_kr)
        kr_tok = [CP(KM[64:96, h, :], KR[64:96, :], t_kr) for h in range(8)]
        qm_tok = [rope(QM[:, h, :], 96, "r96", "cos96", "sin96", qm_raw[h]) for h in range(8)]
        for m in range(4):
            qs_tok[m] = rope(QS[:, m, :], 128, "r128", "cos128", "sin128", qs_raw[m])

        for i in range(4, 12):
            mod_chunk(0, i)

        O = HB
        o_wait = pe.last
        act.wait(o_wait)
        dve.wait(o_wait)
        jobs = [("mla", h, lat) for h in range(8) for lat in (1, 0)]
        jobs += [("swa", h, lat) for m in range(4) for lat in (1, 0) for h in (m, m + 4)]
        mx, nm, sm, rv, es = (small[:, 16 * a:16 * a + 16] for a in range(5))
        p_free = [[None, None], [None, None]]
        pt_free = [None, None]
        mla_scale = 96.0 ** -0.5

        def att_scores(j, job, st):
            kind, h, lat = job
            k0, nk = (0, 512) if lat else (256, 256)
            sc = mla_scale if kind == "mla" else 0.125
            cols = slice(2 * (j % 4), 2 * (j % 4) + 2)
            c0 = 2 * (j % 4)
            bs, mt = [], []
            for qt in range(2):
                q0 = (0 if lat else 256) + 128 * qt
                b = take()
                o = ps[:, b, 0:nk]
                if kind == "mla":
                    t = mm(o, QM[0:96, h, q0:q0 + 128], KM[0:96, h, k0:k0 + nk], True, True,
                           qm_tok[h], km_tok[h], kr_tok[h], sig=True)
                else:
                    r = 64 * (h // 4)
                    t = mm(o, QS[r:r + 64, h % 4, q0:q0 + 128], KS[r:r + 64, k0:k0 + nk], True, not lat,
                           qs_tok[h % 4], t_ks, sig=True)
                    if lat:
                        kt, mask = ((1, "maska"), (0, "maskb"))[qt]
                        t = mm(ps[:, b, 128 * kt:128 * kt + 128], ident, C(mask), False, True, sig=True)
                t = RMAX(mx[:, c0 + qt:c0 + qt + 1], o, t)
                bs.append(b)
                mt.append(t)
            if kind == "mla":
                tn = TS(nm[:, cols], mx[:, cols], -sc, None, ALU.mult, None, t)
            else:
                t = TS(mx[:, cols], mx[:, cols], sc, V("sink", h), ALU.mult, ALU.max, t)
                tn = TS(nm[:, cols], mx[:, cols], -1.0, None, ALU.mult, None, t)
            z = j % 2
            for qt in range(2):
                te = A(P[:, z, qt, 0:nk], ps[:, bs[qt], 0:nk], ACT.Exp, tn, p_free[z][qt],
                       bias=nm[:, c0 + qt:c0 + qt + 1], scale=sc, accum_out=sm[:, c0 + qt:c0 + qt + 1])
                free(bs[qt], te)
            if kind == "swa":
                for qt in range(2):
                    te = A(es[:, c0 + qt:c0 + qt + 1], V("sink", h), ACT.Exp, bias=nm[:, c0 + qt:c0 + qt + 1], scale=1.0)
                te = TT(sm[:, cols], sm[:, cols], es[:, cols], ALU.add, te)
            tr_ = RECIP(rv[:, cols], sm[:, cols], te)
            pt = []
            for qt in range(2):
                pt.append(TS(P[:, z, qt, 0:nk], P[:, z, qt, 0:nk], rv[:, c0 + qt:c0 + qt + 1], None, ALU.mult, None, tr_))
            return pt

        def att_trans(j, job, pt):
            lat = job[2]
            z = j % 2
            n = 4 if lat else 2
            for qt in range(2):
                b = take()
                for kt in range(n):
                    t = tr(ps[:, b, 128 * kt:128 * kt + 128], P[:, z, qt, 128 * kt:128 * kt + 128], ident, pt[qt],
                           sig=(kt == n - 1))
                p_free[z][qt] = t
                src = ps[:, b, 0:128 * n].rearrange("p (a q) -> p a q", a=n)
                dst = PT[:, z, 0:n, 128 * qt:128 * qt + 128]
                e = A(dst, src, ACT.Copy, t, pt_free[z]) if qt else CP(dst, src, t, pt_free[z])
                free(b, e)
                pt[qt] = e
            return pt

        o_bank = {}
        o_tok = [None] * 8

        def att_pv(j, job, et):
            kind, h, lat = job
            z = j % 2
            n = 4 if lat else 2
            if kind == "mla":
                r, ot, first, second = 64 * (h % 2), h // 2, h % 2 == 0, h % 2 == 1
            else:
                r, ot, first, second = 64 * (h // 4), 4 + h % 4, h < 4, h >= 4
            if first:
                o_bank[ot, lat] = take()
            b = o_bank[ot, lat]
            for kt in range(n):
                vt = kt if lat else kt + 2
                v = VM[:, vt, 64 * h:64 * h + 64] if kind == "mla" else VS[:, vt, 64 * (h // 4):64 * (h // 4) + 64]
                t = mm(ps[r:r + 64, b, 0:256], v, PT[:, z, kt, :], kt == 0, kt == n - 1, et[0], et[1],
                       vm_tok[3], t_vs, sig=(kt == n - 1))
            pt_free[z] = t
            if second:
                q0 = 0 if lat else 256
                e = A(O[:, ot, q0:q0 + 256], ps[:, b, 0:256], ACT.Copy, t)
                free(b, e)
                o_tok[ot] = e
            return None

        mla = [x for a in range(4) for lat in (1, 0) for x in (("mla", 2 * a, lat), ("mla", 2 * a + 1, lat))]
        jobs = mla + jobs[16:]
        run_jobs(jobs, [att_scores, att_trans, att_pv])

        ytok = out_proj(("about",), 8, O, o_tok, 512, 4, 0, 16, t_ax[7])
        t_f = fold_mod(0, 32, 24, "ln1g", "ln1b", 0)
        act.wait(t_f)
        new_phase()
        SQ8 = area(8, 512)
        RSTD = area(512)
        htok, xtok = layer_norm(X, ytok, 512, SQ8, RSTD, lnc[:, 0, :], lnc[:, 1, :], t_f, HB, X)
        dve.wait(xtok[-1])
        ytok = ffn(0, htok, 512)
        t_f = fold_mod(1, 8, 0, "ln2g", "ln2b", 0)
        new_phase()
        SQ8 = area(8, 512)
        RSTD = area(512)
        htok, xtok = layer_norm(X, ytok, 512, SQ8, RSTD, lnc[:, 0, :], lnc[:, 1, :], t_f, HB, X)
        dve.wait(xtok[-1])

        new_phase()
        Kd = area(8, 512)
        Vd = area(4, 1024)
        Qd = area(8, 256)
        TMP = area(2, 512)
        tmp_free = [None, None]
        P = area(2, 2, 512)
        PA = area(2, 2, 512)
        PT = area(2, 4, 256)
        k_raw, q_raw = [], []
        for i in range(2):
            w = chunk("din", 2 + i).rearrange("p (k m) -> p k m", k=8)
            for m in range(4):
                b, t = proj_T(w, 128 * m, 128)
                t = A(Kd[:, 4 * i + m, :], ps[:, b, :], ACT.Copy, t)
                free(b, t)
                k_raw.append(t)
            chunk_done()
        for i in range(2):
            w = chunk("din", 4 + i).rearrange("p (k m) -> p k m", k=8)
            for c in range(4):
                b = take()
                for k in range(8):
                    t = mm(ps[:, b, :], HB[:, k, 128 * c:128 * c + 128], w[:, k, :], k == 0, k == 7, sig=(k == 7))
                t_vd = A(Vd[:, c, 512 * i:512 * i + 512], ps[:, b, :], ACT.Copy, t)
                free(b, t_vd)
            chunk_done()
        for i in range(2):
            w = chunk("din", i).rearrange("p (k m) -> p k m", k=8)
            for m in range(4):
                b = take()
                for k in range(8):
                    t = mm(ps[:, b, 0:256], w[:, k, 128 * m:128 * m + 128], HB[:, k, 0:256], k == 0, k == 7, sig=(k == 7))
                t = A(Qd[:, 4 * i + m, :], ps[:, b, 0:256], ACT.Copy, t)
                free(b, t)
                q_raw.append(t)
            chunk_done()
        lm = small[:, 96:104]
        lv = V("lam", 0, 256)
        for a in range(2):
            q, k = lv[:, 128 * a:128 * a + 64], lv[:, 128 * a + 64:128 * a + 128]
            tl = dve.do(lambda e, q=q, k=k, a=a: e.tensor_tensor_reduce(
                out=TMP[:, a, 0:64], in0=q, in1=k, scale=1.0, scalar=0.0, op0=ALU.mult, op1=ALU.add,
                accum_out=lm[:, a:a + 1]))
        tl = A(lm[:, 2:4], lm[:, 0:2], ACT.Exp, tl)
        tl = TT(lm[:, 4:5], lm[:, 3:4], lm[:, 2:3], ALU.subtract, tl)
        t_lam = TS(lm[:, 5:6], lm[:, 4:5], -LAM_INIT, None, ALU.add, None, tl)
        kd_tok = [rope(Kd[:, h, :], 128, "r128", "cos128", "sin128", k_raw[h]) for h in range(8)]
        qd_tok = [rope(Qd[:, h, :], 128, "r128", "cos128", "sin128", q_raw[h]) for h in range(8)]

        o_wait = pe.last
        act.wait(o_wait)
        dve.wait(o_wait)
        p_free = [None, None]
        pa_free = [[None, None], [None, None]]
        pt_free = [None, None]

        def diff_scores(j, h, st):
            c0 = 4 * (j % 2)
            cols = slice(c0, c0 + 4)
            bs = []
            for qt in range(2):
                for a in range(2):
                    b = take()
                    t = mm(ps[:, b, :], Qd[64 * a:64 * a + 64, h, 128 * qt:128 * qt + 128],
                           Kd[64 * a:64 * a + 64, h, :], True, True, qd_tok[h], kd_tok[h], sig=True)
                    t = RMAX(mx[:, c0 + 2 * qt + a:c0 + 2 * qt + a + 1], ps[:, b, :], t)
                    bs.append(b)
            tn = TS(nm[:, cols], mx[:, cols], -0.125, None, ALU.mult, None, t)
            z = j % 2
            pt = []
            for qt in range(2):
                for a in range(2):
                    i = 2 * qt + a
                    dst = (PA if a == 0 else P)[:, z, qt, :]
                    te = A(dst, ps[:, bs[i], :], ACT.Exp, tn, pa_free[z][qt], p_free[z],
                           bias=nm[:, c0 + i:c0 + i + 1], scale=0.125, accum_out=sm[:, c0 + i:c0 + i + 1])
                    free(bs[i], te)
            tr_ = RECIP(rv[:, cols], sm[:, cols], te)
            l2 = TS(es[:, cols], rv[:, cols], lm[:, 5:6], None, ALU.mult, None, tr_, t_lam)
            for qt in range(2):
                i = c0 + 2 * qt
                t = TS(P[:, z, qt, :], P[:, z, qt, :], es[:, i + 1:i + 2], None, ALU.mult, None, l2)
                t = STT(PA[:, z, qt, :], PA[:, z, qt, :], rv[:, i:i + 1], P[:, z, qt, :], ALU.mult, ALU.add, t)
                pt.append(t)
            p_free[z] = t
            return pt

        def diff_trans(j, h, pt):
            z = j % 2
            for qt in range(2):
                b = take()
                for kt in range(4):
                    t = tr(ps[:, b, 128 * kt:128 * kt + 128], PA[:, z, qt, 128 * kt:128 * kt + 128], ident, pt[qt],
                           sig=(kt == 3))
                pa_free[z][qt] = t
                src = ps[:, b, :].rearrange("p (a q) -> p a q", a=4)
                dst = PT[:, z, :, 128 * qt:128 * qt + 128]
                e = A(dst, src, ACT.Copy, t, pt_free[z]) if qt else CP(dst, src, t, pt_free[z])
                free(b, e)
                pt[qt] = e
            return pt

        od_tok = [None] * 8

        def diff_pv(j, h, et):
            z = j % 2
            b = take()
            for kt in range(4):
                t = mm(ps[:, b, 0:256], Vd[:, kt, 128 * h:128 * h + 128], PT[:, z, kt, :], kt == 0, kt == 3,
                       et[0], et[1], t_vd, sig=(kt == 3))
            pt_free[z] = t
            e = CP(HB[:, h, 0:256], ps[:, b, 0:256], t)
            free(b, e)
            od_tok[h] = e

        run_jobs(list(range(8)), [diff_scores, diff_trans, diff_pv])

        sg = small[:, 104:105]
        t_sg = TS(sg, V("subln"), 1.0 - LAM_INIT, None, ALU.mult, None)
        rs_tok = None
        for a in range(4):
            b = take()
            for m in range(2):
                h = 2 * a + m
                q = A(P[:, 0, m, 0:256], HB[:, h, 0:256], ACT.Square, od_tok[h], rs_tok)
                t = mm(ps[:, b, 256 * m:256 * m + 256], C("o128"), P[:, 0, m, 0:256], True, True, q, sig=True)
            rs_tok = t
            s = A(PA[:, 0, 0, :], ps[:, b, :], ACT.Sqrt, t, od_tok[7], bias=EPS6, scale=1.0)
            free(b, s)
            r = RECIP(PA[:, 0, 1, :], PA[:, 0, 0, :], s)
            for m in range(2):
                h = 2 * a + m
                od_tok[h] = STT(HB[:, h, 0:256], HB[:, h, 0:256], sg, PA[:, 0, 1, 256 * m:256 * m + 256],
                                ALU.mult, ALU.mult, r, t_sg)
            act.wait(od_tok[2 * a + 1])

        ytok = out_proj(("dout",), 8, HB, od_tok, 256, 4, 1, 16, None)
        t_f = fold_mod(1, 32, 24, "ln1g", "ln1b", 1)
        new_phase()
        SQ8 = area(8, 256)
        RSTD = area(256)
        XL = X[:, :, 0:256]
        htok, xtok = layer_norm(XL, ytok, 256, SQ8, RSTD, lnc[:, 0, :], lnc[:, 1, :], t_f, HB, XL)
        dve.wait(xtok[-1])
        ytok = ffn(1, htok, 256)
        new_phase()
        SQ8 = area(8, 256)
        RSTD = area(256)
        _, xtok = layer_norm(XL, ytok, 256, SQ8, RSTD, V("ln2g1", 0, 8), V("ln2b1", 0, 8), None, None, HB[:, :, 16:272])

        R = HB[:, :, 0:NT]
        U = X[:, :, 0:NT]
        act.wait(META)
        dve.wait(META)
        for j in range(8):
            t = A(HB[:, j, 0:16], MT[:, 16 * j:16 * j + 16], ACT.Copy, xtok[-1])
        rtok = [t] * 8

        def rms_all(sq, rstd, gname, rtok, dst):
            b = take()
            for j in range(8):
                q = A(sq[:, j, :], R[:, j, :], ACT.Square, rtok[j])
                t = mm(ps[:, b, 0:NT], C("o1024"), sq[:, j, :], j == 0, j == 7, q, sig=(j == 7))
            s = A(rstd, ps[:, b, 0:NT], ACT.Sqrt, t, bias=EPS6, scale=1.0)
            free(b, s)
            r = RECIP(rstd, rstd, s)
            return [STT(dst[:, j, :], R[:, j, :], V(gname, j), rstd, ALU.mult, ALU.mult, r) for j in range(8)]

        new_phase()
        SQ2 = area(8, NT)
        RSTD = area(NT)
        utok = rms_all(SQ2, RSTD, "nmix", rtok, U)
        new_phase()
        ZS = area(8, NT)
        XC = area(16, NT)
        YS = area(8, NT)
        YC = area(8, NT)
        XD = area(3, 1024)
        CBm = area(4, 656)
        EE = area(2, 656)
        CV = area(3, NT)
        CG = area(2, NT)
        SG2 = area(2, 144)
        dtr, dab, dtl, dtt, dA, aex = (area(48) for _ in range(6))
        bias6 = area(96)

        b = take()
        for c in range(3):
            o, n = TOFF[c], TLEN[c]
            for k in range(8):
                t = mm(ps[0:n, b, 16 * c:16 * c + 16], U[:, k, o:o + n], V("wdt", 16 * k, 16), k == 0, k == 7,
                       utok[k], sig=(c == 2 and k == 7))
        tz = dve.do(lambda e: e.memset(dtr, 0.0))
        for c in range(3):
            n = TLEN[c]
            tz = TT(dtr[0:n, 16 * c:16 * c + 16], ps[0:n, b, 16 * c:16 * c + 16], V("dtb", 0, 16)[0:n, :], ALU.add, t, tz)
        free(b, tz)
        t = A(dab, dtr, ACT.Abs, tz)
        t = A(dab, dab, ACT.Exp, t, scale=-1.0)
        t = A(dtl, dab, ACT.Ln, t, bias=1.0, scale=1.0)
        t_dt = STT(dtt, dtr, 0.0, dtl, ALU.max, ALU.add, t)
        t = A(aex[:, 0:16], V("alog", 0, 16), ACT.Exp)
        aeb = aex[:, 0:16].unsqueeze(1).to_broadcast([128, 3, 16])
        t_dA = STT(dA.rearrange("p (c h) -> p c h", c=3), dtt.rearrange("p (c h) -> p c h", c=3), -1.0, aeb,
                   ALU.mult, ALU.mult, t, t_dt)

        cv_free = [None] * 3
        cg_free = [None] * 2
        zs_tok, xc_tok, yc_tok = [], [], []
        hold = {}
        for i in range(12):
            w = chunk("win", i).rearrange("p (k m) -> p k m", k=8)
            for m in range(4):
                f = 4 * i + m
                b = take()
                for k in range(8):
                    t = mm(ps[:, b, 0:NT], w[:, k, 128 * m:128 * m + 128], U[:, k, :], k == 0, k == 7, sig=(k == 7))
                if f < 8:
                    t = A(ZS[:, f, :], ps[:, b, 0:NT], ACT.Silu, t)
                    free(b, t)
                    zs_tok.append(t)
                elif f < 24:
                    x = f - 8
                    z = x % 3
                    wv = lambda a: V("scw", 16 * a + x)
                    t = A(CV[:, z, :], ps[:, b, 0:NT], ACT.Identity, t, cv_free[z], scale=wv(3), bias=V("scb", x))
                    for a in (2, 1, 0):
                        sft = 3 - a
                        t = STT(CV[:, z, sft:NT], ps[:, b, 0:NT - sft], wv(a), CV[:, z, sft:NT], ALU.mult, ALU.add, t)
                    free(b, t)
                    t = A(XC[:, x, :], CV[:, z, :], ACT.Silu, t)
                    cv_free[z] = t
                    xc_tok.append(t)
                else:
                    x, part = divmod(f - 24, 3)
                    z, zz = x % 3, x % 2
                    if part == 0:
                        hold["b"], hold["bt"] = b, t
                    elif part == 1:
                        t = A(CG[:, zz, :], ps[:, b, 0:NT], ACT.Copy, t, cg_free[zz])
                        free(b, t)
                        hold["ct"] = t
                    else:
                        wv = lambda a: V("shw", 8 * a + x)
                        t = TT(CG[:, zz, :], CG[:, zz, :], ps[:, b, 0:NT], ALU.mult, t, hold["ct"])
                        free(b, t)
                        t = TS(CV[:, z, :], CG[:, zz, :], wv(2), None, ALU.mult, None, t, cv_free[z])
                        t = STT(CV[:, z, 1:NT], CG[:, zz, 0:NT - 1], wv(1), CV[:, z, 1:NT], ALU.mult, ALU.add, t)
                        t = STT(CV[:, z, 2:NT], CG[:, zz, 0:NT - 2], wv(0), CV[:, z, 2:NT], ALU.mult, ALU.add, t)
                        cg_free[zz] = t
                        t = TT(YC[:, x, :], CV[:, z, :], ps[:, hold["b"], 0:NT], ALU.mult, t, hold["bt"])
                        cv_free[z] = t
                        free(hold["b"], t)
                        yc_tok.append(t)
            chunk_done()

        b = take()

        def dAc(c):
            return dA[0:TLEN[c], 16 * c:16 * c + 16]

        for c in range(3):
            n = TLEN[c]
            mm(ps[0:n, b, 16 * c:16 * c + 16], C("tri")[0:n, 0:n], dAc(c), True, True, t_dA)
        mm(ps[0:16, b, 48:64], C("sfx")[0:16, 0:16], dAc(0), True, True)
        mm(ps[0:16, b, 64:80], C("sfx")[0:16, 0:16], dAc(0), True, False)
        mm(ps[0:16, b, 64:80], C("ones", 16), dAc(1), False, True)
        t = mm(ps[:, b, 80:96], C("sfx"), dAc(1), True, True, sig=True)
        t1 = TS(bias6[0:16, 0:16], ps[0:16, b, 0:16], -1.0, None, ALU.mult, None, t)
        t1 = TS(bias6[:, 16:48], ps[:, b, 16:48], -1.0, None, ALU.mult, None, t)
        t1 = CP(bias6[0:16, 48:80], ps[0:16, b, 48:80], t)
        t_b6 = CP(bias6[:, 80:96], ps[:, b, 80:96], t)
        free(b, t_b6)

        cb_tok = []
        for g in range(4):
            Bt, Ct = XC[:, 8 + g, :], XC[:, 12 + g, :]
            b, b2 = take(), take()
            mm(ps[0:16, b, 0:272], Bt[:, 0:16], Ct[:, :], True, True, xc_tok[8 + g], xc_tok[12 + g])
            t = mm(ps[:, b, 272:400], Bt[:, 144:272], Ct[:, 144:272], True, True, sig=True)
            t2 = mm(ps[:, b2, 0:256], Bt[:, 16:144], Ct[:, 16:272], True, True, sig=True)
            TT(CBm[0:16, g, 0:16], ps[0:16, b, 0:16], C("tri", 16)[0:16, :], ALU.mult, t)
            CP(CBm[0:16, g, 16:272], ps[0:16, b, 16:272])
            t = TT(CBm[:, g, 528:656], ps[:, b, 272:400], C("tri"), ALU.mult)
            free(b, t)
            TT(CBm[:, g, 272:400], ps[:, b2, 0:128], C("tri"), ALU.mult, t2)
            t = CP(CBm[:, g, 400:528], ps[:, b2, 128:256])
            free(b2, t)
            cb_tok.append(t)

        xd_tok = []
        for c in range(3):
            o, n = TOFF[c], TLEN[c]
            for a in range(2):
                b = take()
                for m in range(4):
                    t = tr(ps[0:n, b, 128 * m:128 * m + 128], XC[:, 4 * a + m, o:o + n], ident, xc_tok[4 * a + m],
                           sig=(m == 3))
                db = dtt[0:n, 16 * c + 8 * a:16 * c + 8 * a + 8].unsqueeze(2).to_broadcast([n, 8, 64])
                t = TT(XD[0:n, c, 512 * a:512 * a + 512].rearrange("p (h q) -> p h q", h=8),
                       ps[0:n, b, :].rearrange("p (h q) -> p h q", h=8), db, ALU.mult, t, t_dt)
                free(b, t)
                xd_tok.append(t)

        ee_free = [None] * 2
        sg_free = [None] * 2
        y_bank = {}
        ys_tok = []

        def head_decay(j, h, st):
            z = j % 2
            b = take()
            for c in range(3):
                o, n = TOFF[c], TLEN[c]
                d = dA[0:n, 16 * c + h:16 * c + h + 1].to_broadcast([n, 128])
                t = mm(ps[:, b, o:o + n], d, C("tri", n)[0:n, :], True, True, sig=(c == 2))
            bc = lambda i, n: bias6[0:n, 16 * i + h:16 * i + h + 1]
            s0 = TS(SG2[0:16, z, 0:16], ps[0:16, b, 0:16], bc(0, 16), 0.0, ALU.add, ALU.min, t, sg_free[z], t_b6)
            s1 = TS(EE[:, z, 272:400], ps[:, b, 16:144], bc(1, 128), 0.0, ALU.add, ALU.min, ee_free[z])
            s2 = TS(EE[:, z, 528:656], ps[:, b, 144:272], bc(2, 128), 0.0, ALU.add, ALU.min)
            e = A(EE[0:16, z, 0:16], SG2[0:16, z, 0:16], ACT.Exp, s2, ee_free[z])
            sg_free[z] = e
            A(EE[0:16, z, 16:144], ps[0:16, b, 16:144], ACT.Exp, bias=bc(3, 16), scale=1.0)
            A(EE[0:16, z, 144:272], ps[0:16, b, 144:272], ACT.Exp, bias=bc(4, 16), scale=1.0)
            e = A(EE[:, z, 400:528], ps[:, b, 144:272], ACT.Exp, bias=bc(5, 128), scale=1.0)
            free(b, e)
            A(EE[:, z, 272:400], EE[:, z, 272:400], ACT.Exp)
            e = A(EE[:, z, 528:656], EE[:, z, 528:656], ACT.Exp)
            TT(EE[0:16, z, 0:272], EE[0:16, z, 0:272], CBm[0:16, h // 4, 0:272], ALU.mult, e, cb_tok[h // 4])
            return TT(EE[:, z, 272:656], EE[:, z, 272:656], CBm[:, h // 4, 272:656], ALU.mult)

        def head_out(j, h, t):
            z = j % 2
            r = 64 * (h % 2)
            if h % 2 == 0:
                y_bank[0] = take()
            b = y_bank[0]
            hc = slice(64 * h, 64 * h + 64)
            mm(ps[r:r + 64, b, 0:272], XD[0:16, 0, hc], EE[0:16, z, 0:272], True, False, t, xd_tok[-1])
            mm(ps[r:r + 64, b, 16:272], XD[:, 1, hc], EE[:, z, 272:528], False, False)
            t = mm(ps[r:r + 64, b, 144:272], XD[:, 2, hc], EE[:, z, 528:656], False, True, sig=True)
            ee_free[z] = t
            if h % 2:
                x = h // 2
                t = STT(YS[:, x, :], XC[:, x, :], V("dskip", x), ps[:, b, 0:NT], ALU.mult, ALU.add, t)
                free(b, t)
                ys_tok.append(TT(YS[:, x, :], YS[:, x, :], ZS[:, x, :], ALU.mult, t, zs_tok[x]))

        run_jobs(list(range(16)), [head_decay, head_out])

        act.wait(pe.last, dve.last)
        for g in range(4):
            b = take()
            for m in range(2):
                q = A(XC[:, 2 * g + m, :], YS[:, 2 * g + m, :], ACT.Square, ys_tok[2 * g + m])
                t = mm(ps[:, b, 0:NT], C("o256"), XC[:, 2 * g + m, :], m == 0, m == 1, q, sig=(m == 1))
            z = g % 3
            s = A(CV[:, z, :], ps[:, b, 0:NT], ACT.Sqrt, t, cv_free[z], bias=EPS6, scale=1.0)
            free(b, s)
            r = RECIP(CV[:, z, :], CV[:, z, :], s)
            for m in range(2):
                x = 2 * g + m
                cv_free[z] = ys_tok[x] = STT(YS[:, x, :], YS[:, x, :], V("ssdn", x), CV[:, z, :], ALU.mult, ALU.mult, r)
        for x in range(8):
            b = take()
            q = A(XC[:, 8 + x, :], YC[:, x, :], ACT.Square, yc_tok[x])
            t = mm(ps[:, b, 0:NT], C("blk64"), XC[:, 8 + x, :], True, True, q, sig=True)
            z = x % 3
            s = A(CV[:, z, :], ps[:, b, 0:NT], ACT.Sqrt, t, cv_free[z], bias=EPS6, scale=1.0)
            free(b, s)
            r = RECIP(CV[:, z, :], CV[:, z, :], s)
            cv_free[z] = yc_tok[x] = STT(YC[:, x, :], YC[:, x, :], V("shn", x), CV[:, z, :], ALU.mult, ALU.mult, r)

        rtok = []
        for i in range(4):
            w = chunk("wout", i).rearrange("p (k m) -> p k m", k=16)
            for m in range(2):
                j = 2 * i + m
                b = take()
                for k in range(16):
                    src, tk = (YS[:, k, :], ys_tok[k]) if k < 8 else (YC[:, k - 8, :], yc_tok[k - 8])
                    t = mm(ps[:, b, 0:NT], w[:, k, 128 * m:128 * m + 128], src, k == 0, k == 15, tk, sig=(k == 15))
                t = TT(R[:, j, :], R[:, j, :], ps[:, b, 0:NT], ALU.add, t)
                free(b, t)
                rtok.append(t)
            chunk_done()

        new_phase()
        SQ2 = area(8, NT)
        RSTD = area(NT)
        utok = rms_all(SQ2, RSTD, "nffn", rtok, U)

        new_phase()
        H = area(64, NT)
        CBE = area(2, NT)
        SGE = area(3, NT)
        lg = area(3, 20)
        comb = area(3, 16)
        rt = area(3, 32)
        b = take()
        for c in range(3):
            o, n = TOFF[c], TLEN[c]
            for k in range(8):
                t = mm(ps[0:n, b, 20 * c:20 * c + 20], U[:, k, o:o + n], V("rw", 20 * k, 20), k == 0, k == 7,
                       utok[k], sig=(c == 2 and k == 7))
        comb_tok = []
        for c in range(3):
            n = TLEN[c]
            L = lg[0:n, c, :]
            W = rt[0:n, c, :]
            gl, el = L[:, 0:4], L[:, 4:20]
            rank = C("rank")[0:n, :]
            t_l = TT(L, ps[0:n, b, 20 * c:20 * c + 20], V("rb", 0, 20)[0:n, :], ALU.add, t)

            def first_max(src, mcol, hot, tok):
                t = RMAX(mcol, src, tok)
                t = STT(hot, src, mcol, rank, ALU.is_equal, ALU.mult, t)
                t = RMAX(W[:, 31:32], hot, t)
                return TS(hot, hot, W[:, 31:32], None, ALU.is_equal, None, t)

            gm, ghot = W[:, 0:1], W[:, 4:8]
            tg = first_max(gl, gm, ghot, t_l)
            tn = TS(W[:, 1:2], gm, -1.0, None, ALU.mult, None, tg)
            te = A(W[:, 8:12], gl, ACT.Exp, tn, bias=W[:, 1:2], scale=1.0, accum_out=W[:, 2:3])
            sel = W[:, 12:16]
            ts = TS(sel, el[:, 0:4], ghot[:, 0:1], None, ALU.mult, None, tg)
            for g in range(1, 4):
                ts = STT(sel, el[:, 4 * g:4 * g + 4], ghot[:, g:g + 1], sel, ALU.mult, ALU.add, ts)
            m1, h1, m2, h2 = W[:, 16:17], W[:, 20:24], W[:, 17:18], W[:, 24:28]
            t1 = first_max(sel, m1, h1, ts)
            t1 = STT(sel, h1, -3e38, sel, ALU.mult, ALU.add, t1)
            t1 = first_max(sel, m2, h2, t1)
            t2 = TT(W[:, 18:19], m2, m1, ALU.subtract, t1)
            t2 = A(W[:, 18:19], W[:, 18:19], ACT.Exp, t2)
            t2 = TS(W[:, 19:20], W[:, 18:19], 1.0, W[:, 2:3], ALU.add, ALU.mult, t2, te)
            t2 = RECIP(W[:, 19:20], W[:, 19:20], t2)
            t2 = TT(W[:, 18:19], W[:, 18:19], W[:, 19:20], ALU.mult, t2)
            t2 = TS(h2, h2, W[:, 18:19], None, ALU.mult, None, t2)
            t2 = STT(h1, h1, W[:, 19:20], h2, ALU.mult, ALU.add, t2)
            for g in range(4):
                tc = TS(comb[0:n, c, 4 * g:4 * g + 4], h1, ghot[:, g:g + 1], None, ALU.mult, None, t2)
            comb_tok.append(tc)
        free(b, t_l)

        cb_free = [None] * 2
        sg_free = [None] * 3
        h_tok = []
        for e in range(NE):
            z = e % 2
            b = take()
            for c in range(3):
                o, n = TOFF[c], TLEN[c]
                t = mm(ps[:, b, o:o + n], comb[0:n, c, e:e + 1].to_broadcast([n, 128]), ident[0:n, 0:n], True, True,
                       comb_tok[c], sig=(c == 2))
            t_cb = A(CBE[:, z, :], ps[:, b, 0:NT], ACT.Copy, t, cb_free[z])
            free(b, t_cb)
            wg = chunk("eg", e).rearrange("p (k m) -> p k m", k=8)
            bg, tg = [], []
            for m in range(4):
                b = take()
                for k in range(8):
                    t = mm(ps[:, b, 0:NT], wg[:, k, 128 * m:128 * m + 128], U[:, k, :], k == 0, k == 7, sig=(k == 7))
                bg.append(b)
                tg.append(t)
            chunk_done()
            wu = chunk("eu", e).rearrange("p (k m) -> p k m", k=8)
            for m in range(4):
                f = 4 * e + m
                y = f % 3
                s = A(SGE[:, y, :], ps[:, bg[m], 0:NT], ACT.Silu, tg[m], sg_free[y])
                free(bg[m], s)
                s = TT(SGE[:, y, :], SGE[:, y, :], CBE[:, z, :], ALU.mult, s, t_cb)
                b = take()
                for k in range(8):
                    t = mm(ps[:, b, 0:NT], wu[:, k, 128 * m:128 * m + 128], U[:, k, :], k == 0, k == 7, sig=(k == 7))
                s = TT(H[:, f, :], SGE[:, y, :], ps[:, b, 0:NT], ALU.mult, s, t)
                free(b, s)
                sg_free[y] = s
                h_tok.append(s)
            chunk_done()
            cb_free[z] = s
        bo = [take() for _ in range(8)]
        for e in range(NE):
            w = chunk("ed", e).rearrange("p (k m) -> p k m", k=4)
            for j in range(8):
                for k in range(4):
                    f = 4 * e + k
                    t = mm(ps[:, bo[j], 0:NT], w[:, k, 128 * j:128 * j + 128], H[:, f, :], f == 0, f == 63, h_tok[f],
                           sig=(f == 63))
                if e == NE - 1:
                    rtok[j] = TT(R[:, j, :], R[:, j, :], ps[:, bo[j], 0:NT], ALU.add, t)
                    free(bo[j], rtok[j])
            if e < NE - 1:
                pe.items[-1] = (pe.items[-1][0], True)
                pe.n += 1
            chunk_done()

        new_phase()
        SQ2 = area(8, NT)
        RSTD = area(NT)
        otok = rms_all(SQ2, RSTD, "nfin", rtok, U)

        block = ctx.enter_context(nc.Block())
        offs = np.cumsum([0] + [128 * c for _, c in plan])

        @block.sync
        def _(sp):
            for n, (key, c) in enumerate(plan):
                if n >= SLOTS:
                    sp.wait_ge(*used[n - SLOTS])
                s = n % SLOTS
                src = wts[int(offs[n]):int(offs[n + 1])].rearrange("(p c) -> p c", p=128)
                sp.dma_start(ring[:, s * SLOT:s * SLOT + c], src).then_inc(s_w[s], 16)
            for h in range(2):
                sp.wait_ge(*otok[4 * h + 3])
                sp.dma_start(out.rearrange("p (j t) -> p j t", j=8)[:, 4 * h:4 * h + 4, :],
                             U[:, 4 * h:4 * h + 4, 16:NT]).then_inc(s_out, 16)
            sp.wait_ge(s_out, 32)

        @block.gpsimd
        def _(pool):
            pool.dma_start(MT[:, :], meta).then_inc(s_m, 16)

        @block.scalar
        def _(e):
            e.dma_start(vec[:, :], vecs).then_inc(s_v, 16)
            e.dma_start(cst[:, :], csts).then_inc(s_c, 16)
            e.dma_start(X.rearrange("p a b -> p (a b)"), xin).then_inc(s_x, 16)
            act.emit(e)

        @block.vector
        def _(e):
            dve.emit(e)

        @block.tensor
        def _(e):
            pe.emit(e)


def kernel(**inputs):
    import concourse.bacc as bacc
    from concourse.bass_utils import run_bass_kernel_spmd as run

    x = {k: np.asarray(v) for k, v in inputs.items()}
    nc = bacc.Bacc("TRN2", target_bir_lowering=False, num_devices=1)
    fmajor = lambda a: a.T.reshape(8, 128, -1).transpose(1, 0, 2)
    xin = np.concatenate([fmajor(x["x"][0]), fmajor(x["ctx"][0])], -1).reshape(128, -1)
    arrays = {
        "wts": np.concatenate([host_chunk(x, k).reshape(-1) for k, _ in chunk_plan()]),
        "xin": xin,
        "meta": fmajor(x["meta_tokens_2"]).reshape(128, -1),
        "vecs": host_vec(x),
        "csts": consts(),
    }
    arrays = {k: np.ascontiguousarray(v) for k, v in arrays.items()}
    args = [nc.dram_tensor(k, v.shape, F32, kind="ExternalInput").ap() for k, v in arrays.items()]
    out = nc.dram_tensor("out", (128, 2048), F32, kind="ExternalOutput").ap()
    build(nc, *args, out)
    r = run(nc, [arrays], core_ids=[0])
    got = np.asarray(r.results[0]["out"]).reshape(128, 8, 256)
    return np.ascontiguousarray(got.transpose(2, 1, 0).reshape(1, 256, 1024))
```

```python
import math
from contextlib import ExitStack

import numpy as np
import concourse.bass as bass
from concourse import mybir

F32 = mybir.dt.float32
F32R = mybir.dt.float32r
ALU = mybir.AluOpType
ACT = mybir.ActivationFunctionType
AX = mybir.AxisListType

D = 1024
F = 2816
NF = F // 128
S = 256
NT = 272
TOFF = [0, 16, 144]
TLEN = [16, 128, 128]
NE = 16
ALPHA = 4.0 ** 0.25
LAM_INIT = 0.8 - 0.6 * math.exp(-0.3)
NEG = -1e30
SLOTS = 3
SLOT = 2048
SPLITS = 3
ARENA = 16800
HALF = NF // 2
CAP = 128



def vec_layout():
    at, n = {}, 0
    for name, cols in (
            ("bmod0", 48), ("bmod1", 48),
            ("ln1g0", 8), ("ln1b0", 8), ("ln2g0", 8), ("ln2b0", 8),
            ("ln1g1", 8), ("ln1b1", 8), ("ln2g1", 8), ("ln2b1", 8),
            ("cw0", 66), ("cw1", 66), ("cb0", 22), ("cb1", 22),
            ("qnorm", 2), ("kvnorm", 1), ("subln", 1),
            ("nmix", 8), ("scw", 64), ("scb", 16), ("dskip", 8), ("ssdn", 8),
            ("shw", 24), ("shn", 8), ("nffn", 8), ("nfin", 8),
            ("dtb", 16), ("alog", 16), ("rb", 20), ("sink", 8), ("lam", 256),
            ("cond", 16), ("rw", 160), ("wdt", 128)):
        at[name] = (n, cols)
        n += cols
    return at, n


def const_layout():
    at, n = {}, 0
    for name, cols in (
            ("ident", 128), ("o1024", 128), ("o256", 128), ("o128", 128), ("blk64", 128),
            ("ones", 128), ("tri", 128), ("sfx", 128), ("r128", 128), ("r96", 128),
            ("maska", 128), ("maskb", 128),
            ("cos128", 256), ("sin128", 256), ("cos96", 256), ("sin96", 256),
            ("rank", 4), ("eps5", 1), ("eps6", 1), ("sel4", 2), ("slot", 128)):
        at[name] = (n, cols)
        n += cols
    return at, n


def rope_table(dim):
    row = np.repeat(np.arange(S // 64), 64).astype(np.float32)
    col = np.tile(np.arange(64), S // 64).astype(np.float32)
    q = dim // 4
    fr = (np.float32(10000.0) ** (-np.arange(q, dtype=np.float32) / np.float32(q))).astype(np.float32)
    ar = row[:, None] * fr
    ac = col[:, None] * fr
    cos = np.concatenate([np.cos(ar), np.cos(ar), np.cos(ac), np.cos(ac)], -1)
    sin = np.concatenate([np.sin(ar), np.sin(ar), np.sin(ac), np.sin(ac)], -1)
    return cos.T.astype(np.float32), sin.T.astype(np.float32)


def rope_perm(dim):
    q = dim // 4
    r = np.zeros((dim, dim), np.float32)
    for i in range(q):
        for b in (0, 2 * q):
            r[b + q + i, b + i] = -1.0
            r[b + i, b + q + i] = 1.0
    return r


def consts():
    at, n = const_layout()
    c = np.zeros((128, n), np.float32)

    def put(name, v):
        o, k = at[name]
        c[:v.shape[0], o:o + v.shape[1]] = v

    i = np.arange(128)
    put("ident", np.eye(128, dtype=np.float32))
    put("o1024", np.full((128, 128), 1 / 1024, np.float32))
    put("o256", np.full((128, 128), 1 / 256, np.float32))
    put("o128", np.full((128, 128), 1 / 128, np.float32))
    put("blk64", (i[:, None] // 64 == i[None, :] // 64).astype(np.float32) / 64)
    put("ones", np.ones((128, 128), np.float32))
    put("tri", (i[:, None] <= i[None, :]).astype(np.float32))
    put("sfx", (i[:, None] > i[None, :]).astype(np.float32))
    r128 = np.zeros((128, 128), np.float32)
    r128[:64, :64] = r128[64:, 64:] = rope_perm(64)
    put("r128", r128)
    r96 = np.zeros((128, 128), np.float32)
    r96[64:96, 64:96] = rope_perm(32)
    put("r96", r96)
    put("maska", np.where(i[None, :] <= i[:, None], 0, NEG).astype(np.float32))
    put("maskb", np.where(i[None, :] >= i[:, None], 0, NEG).astype(np.float32))
    c64, s64 = rope_table(64)
    put("cos128", np.concatenate([c64, c64]))
    put("sin128", np.concatenate([s64, s64]))
    c32, s32 = rope_table(32)
    put("cos96", np.concatenate([np.ones((64, S), np.float32), c32]))
    put("sin96", np.concatenate([np.zeros((64, S), np.float32), s32]))
    put("rank", np.tile(np.array([[4, 3, 2, 1]], np.float32), (128, 1)))
    put("sel4", np.array([[1, 0], [0, 1], [1, 0], [0, 1]], np.float32))
    put("slot", np.tile(np.where(i < CAP, i + 1, 0).astype(np.float32), (128, 1)))
    put("eps5", np.full((128, 1), 1e-5, np.float32))
    put("eps6", np.full((128, 1), 1e-6, np.float32))
    return c


QPERM = [h + 4 * k for h in range(4) for k in range(2)]


RAW = ("qb", "kvb")


def chunk_plan():
    p = [(("mod", 0, i), 2048) for i in range(8)]
    p += [(("abin", 0), 2048), (("abin", 1), 2048), (("abin", 2), 2048), (("abin", 3), 8 * 160), (("abin", 4), 2048)]
    p += [(("kvb", 0), 768)]
    for half in range(2):
        p += [(("qb", half), 768)] + [(("kvb", 1), 256)] * half
        p += [(("mod", 0, i), 2048) for i in range(8 + 8 * half, 16 + 8 * half)]
    p += [(("about", i), 2048) for i in range(4)]
    p += ffn_plan(0)
    p += [(("din", (4 + i) % 12), 2048) for i in range(12)]
    p += [(("dout", i), 2048) for i in range(4)]
    p += ffn_plan(1)
    p += [(("win", i), 2048) for i in range(24)]
    p += [(("wout", half, i), 2048) for half in (1, 0) for i in range(4)]
    for e in range(NE + 1):
        if e < NE:
            p += [((kind, e, i), 2048) for kind in ("eg", "eu") for i in range(2)]
        if e:
            p += [(("ed", e - 1, i), 2048) for i in range(2)]
    return p


def ffn_plan(l):
    p = []
    for half in range(2):
        for i in range(HALF):
            p.append((("gu", l, HALF * half + i), 2048))
            if l == 0:
                p.append((("mod", 1, HALF * half + i), 2048))
        if l == 0 and half:
            p += [(("mod", 1, 22), 2048), (("mod", 1, 23), 2048)]
        p += [(("down", l, half, j), HALF * 128) for j in range(8)]
    return p


def pack_k(w):
    k, m = w.shape
    return w.reshape(k // 128, 128, m).transpose(1, 0, 2).reshape(128, -1)


def host_chunk(x, key):
    kind = key[0]
    if kind == "mod":
        i, half = divmod(key[2], 2)
        return pack_k(x["w_mod"][key[1]][512 * half:512 * half + 512, 512 * i:512 * i + 512])
    if kind == "abin":
        a, b = ((0, 256), (256, 512), (512, 768), (768, 928), (928, 1184))[key[1]]
        w = x["ab_w_in"][0]
        qs = w[:, 256:768].reshape(D, 8, 64)[:, QPERM].reshape(D, 512)
        return pack_k(np.concatenate([w[:, :256], qs, w[:, 768:]], 1)[:, a:b])
    if kind == "qb":
        return pack_k(x["mla_w_qb"][0][:, 384 * key[1]:384 * key[1] + 384])
    if kind == "kvb":
        w = x["mla_w_kvb"][0].reshape(128, 8, 2, 64)
        k, v = w[:, :, 0].reshape(128, 512), w[:, :, 1].reshape(128, 512)
        return k[:, 256:] if key[1] else np.concatenate([k[:, :256], v], 1)
    if kind == "about":
        w = x["ab_w_out"][0]
        sw = w[512:].reshape(8, 64, D)[QPERM].reshape(512, D)
        return pack_k(np.concatenate([w[:512], sw], 0)[:, 256 * key[1]:256 * key[1] + 256])
    if kind == "gu":
        c = slice(128 * key[2], 128 * key[2] + 128)
        return pack_k(np.concatenate([x["ffn_w_gate"][key[1]][:, c], x["ffn_w_up"][key[1]][:, c]], 1))
    if kind == "down":
        l, half, j = key[1:]
        n = 128 * HALF
        return pack_k(x["ffn_w_down"][l][n * half:n * half + n, 128 * j:128 * j + 128])
    if kind == "din":
        return pack_k(x["diff_w_in"][0][:, 256 * key[1]:256 * key[1] + 256])
    if kind == "dout":
        return pack_k(x["diff_w_out"][0][:, 256 * key[1]:256 * key[1] + 256])
    if kind == "win":
        w = x["w_in_2"][0]
        bch = w[:, 3088:].reshape(D, 3, 8, 128).transpose(0, 2, 1, 3).reshape(D, 3072)
        i = key[1]
        return pack_k(w[:, 256 * i:256 * i + 256] if i < 12 else bch[:, 256 * (i - 12):256 * (i - 12) + 256])
    if kind == "wout":
        half, i = key[1:]
        return pack_k(x["w_out_2"][0][1024 * half:1024 * half + 1024, 256 * i:256 * i + 256])
    if kind in ("eg", "eu"):
        w = x["expert_w_gate_2" if kind == "eg" else "expert_w_up_2"][0, key[1]]
        return pack_k(w[512 * key[2]:512 * key[2] + 512])
    if kind == "ed":
        return pack_k(x["expert_w_down_2"][0, key[1]][256 * key[2]:256 * key[2] + 256])


def host_vec(x):
    at, n = vec_layout()
    v = np.zeros((128, n), np.float32)

    def cols(a):
        return np.asarray(a).reshape(-1, 128).T

    def put(name, a):
        o, k = at[name]
        v[:, o:o + k] = a

    for l in range(2):
        put(f"bmod{l}", cols(x["b_mod"][l]))
        for nm in ("ln1", "ln2"):
            put(f"{nm}g{l}", cols(x[f"{nm}_g"][l]))
            put(f"{nm}b{l}", cols(x[f"{nm}_b"][l]))
        put(f"cw{l}", cols(x["ffn_conv_w"][l]))
        put(f"cb{l}", cols(x["ffn_conv_b"][l]))
    put("qnorm", cols(x["mla_q_norm"][0]))
    put("kvnorm", cols(x["mla_kv_norm"][0]))
    put("subln", cols(x["diff_subln_g"][0]))
    put("nmix", cols(x["norm_mix_2"][0]))
    put("scw", cols(x["ssd_conv_w_2"][0]))
    put("scb", cols(x["ssd_conv_b_2"][0]))
    put("dskip", cols(np.repeat(x["D_skip_2"][0], 64)))
    put("ssdn", cols(x["ssd_norm_2"][0]))
    put("shw", cols(x["sc_conv_w_2"][0]))
    put("shn", cols(x["sc_norm_2"][0]))
    put("nffn", cols(x["norm_ffn_2"][0]))
    put("nfin", cols(x["norm_final_2"]))
    put("dtb", x["dt_bias_2"][0][None])
    put("alog", x["A_log_2"][0][None])
    put("rb", np.concatenate([x["router_group_b_2"][0], x["router_expert_b_2"][0]])[None])
    put("sink", x["swa_sink"][0][None])
    put("lam", np.concatenate([x["diff_lam_q1"][0], x["diff_lam_k1"][0],
                               x["diff_lam_q2"][0], x["diff_lam_k2"][0]])[None])
    put("cond", np.stack([cols(x["c"][0]), cols(x["c_ctx"])], -1).reshape(128, 16))
    put("rw", pack_k(np.concatenate([x["router_group_w_2"][0], x["router_expert_w_2"][0]], 1)))
    put("wdt", pack_k(x["w_in_2"][0][:, 3072:3088]))
    return v



class Queue:

    def __init__(self, sem):
        self.sem, self.n, self.items, self.seen = sem, 0, [], {}

    def wait(self, *toks):
        for t in toks:
            if t is not None and self.seen.get(t[0].name, 0) < t[1]:
                self.seen[t[0].name] = t[1]
                self.items.append((None, t))

    def do(self, fn, *toks, sig=True):
        self.wait(*toks)
        if sig:
            self.n += 1
        self.items.append((fn, sig))
        return (self.sem, self.n) if sig else None

    @property
    def last(self):
        return (self.sem, self.n) if self.n else None

    def emit(self, eng, first=0, end=None):
        for fn, a in self.items[first:end]:
            if fn is None:
                eng.wait_ge(a[0], a[1])
            else:
                ins = fn(eng)
                if a:
                    ins.then_inc(self.sem, 1)


def build(nc, wts, xin, meta, vecs, csts, out):
    vat, nv = vec_layout()
    cat, ncst = const_layout()
    plan = chunk_plan()

    with ExitStack() as ctx:
        sb = lambda name, shape: ctx.enter_context(nc.sbuf_tensor(name, shape, F32))
        sem = lambda name: ctx.enter_context(nc.semaphore(name))

        ring = sb("ring", [128, SLOTS * SLOT])
        X = sb("X", [128, 8, 512])
        XF = X.rearrange("p a b -> p (a b)")
        HH, HL = (ctx.enter_context(nc.sbuf_tensor(n, [128, 16 * NT], F32R)) for n in ("HH", "HL"))
        WH, WL = (ctx.enter_context(nc.sbuf_tensor(n, [128, SPLITS * SLOT], F32R)) for n in ("WH", "WL"))
        csr = ctx.enter_context(nc.sbuf_tensor("csr", [128, 8, 4], F32R))
        base = nc.sbuf_base
        arena = sb("arena", [128, ARENA])
        PARTS = nc.alloc_sbuf_tensor_at("parts", [128, 2 * HALF * 512], F32R, offset=base)
        vec = sb("vec", [128, nv])
        cst = sb("cst", [128, ncst])
        modv = [sb(f"modv{l}", [128, 48, 2]) for l in range(2)]
        scond = sb("scond", [128, 8, 2])
        mrow = sb("mrow", [4, 512])
        fold = sb("fold", [128, 8, 8])
        lnc = sb("lnc", [128, 4, 8])
        small = sb("small", [128, 256])
        MT = sb("MT", [128, 128])
        flag = ctx.enter_context(nc.sbuf_tensor("flag", [128, 1], mybir.dt.int32))
        ps = ctx.enter_context(nc.psum_tensor("ps", [128, 8, 512], F32))

        pe, act, dve, pool = (Queue(sem(n)) for n in ("s_pe", "s_act", "s_dve", "s_pool"))
        s_w = [sem(f"s_w{i}") for i in range(SLOTS)]
        s_v, s_c, s_x, s_m, s_out = (sem(n) for n in ("s_v", "s_c", "s_x", "s_m", "s_out"))
        VEC, CST, XIN, META = (s_v, 16), (s_c, 16), (s_x, 16), (s_m, 16)

        def V(name, i=0, n=1):
            return vec[:, vat[name][0] + i:vat[name][0] + i + n]

        def C(name, n=None):
            return cst[:, cat[name][0]:cat[name][0] + (n or cat[name][1])]

        ident = C("ident")
        EPS5, EPS6 = C("eps5"), C("eps6")

        bank_free = [None] * 8
        bank_at = [0]
        kept = set()

        def take(keep=False):
            while bank_at[0] % 8 in kept:
                bank_at[0] += 1
            b = bank_at[0] % 8
            bank_at[0] += 1
            if keep:
                kept.add(b)
            pe.wait(bank_free[b])
            return b

        def free(b, tok):
            kept.discard(b)
            bank_free[b] = tok

        slot_free = {}
        split_at = [0]
        split_tok = {}
        split_of = {}
        split_free = {}
        chunk_at = [0]

        def landed(n):
            return (s_w[n % SLOTS], 16 * (n // SLOTS + 1))

        def raw(n):
            a = (n % SLOTS) * SLOT
            return ring[:, a:a + plan[n][1]]

        def split_chunk(n):
            q = split_at[0]
            split_at[0] += 1
            a, c = (q % SPLITS) * SLOT, plan[n][1]
            hi, lo = WH[:, a:a + c], WL[:, a:a + c]
            t = A(hi, raw(n), ACT.Copy, landed(n), split_free.get(q - SPLITS))
            t = TT(lo, raw(n), hi.bitcast(F32), ALU.subtract, landed(n), split_free.get(q - SPLITS), t)
            slot_free[n] = t
            split_tok[n] = t
            split_of[n] = (q, hi, lo)

        def chunk(*key):
            n = chunk_at[0]
            assert plan[n][0] == key, (plan[n], key)
            chunk_at[0] += 1
            for i in range(n, min(n + SPLITS, len(plan))):
                if i not in split_of and plan[i][0][0] not in RAW:
                    q = split_at[0] - SPLITS
                    if q < 0 or q in split_free:
                        split_chunk(i)
            if key[0] in RAW:
                pe.wait(landed(n))
                return raw(n)
            pe.wait(split_tok[n])
            return split_of[n][1:]

        def chunk_done():
            n = chunk_at[0] - 1
            if plan[n][0][0] in RAW:
                slot_free[n] = pe.last
            else:
                split_free[split_of[n][0]] = pe.last

        def mm(o, lhsT, rhs, start, stop, *toks, sig=False):
            return pe.do(lambda e: e.matmul(o, lhsT, rhs, start=start, stop=stop), *toks, sig=sig)

        def mm3(o, w, cols, x, k, nk, *toks, sig=False):
            mm(o, w[0][:, cols], x[0], k == 0, False, *toks)
            mm(o, w[0][:, cols], x[1], False, False)
            return mm(o, w[1][:, cols], x[0], False, k == nk - 1, sig=sig)

        def tr(o, i, idn, *toks, sig=False):
            return pe.do(lambda e: e.transpose(o, i, idn), *toks, sig=sig)

        def A(o, i, f, *toks, **kw):
            return act.do(lambda e: e.activation(o, i, f, **kw), *toks)

        def TT(o, a, b, op, *toks):
            return dve.do(lambda e: e.tensor_tensor(o, a, b, op), *toks)

        def TS(o, a, s1, s2, op0, op1, *toks):
            if s2 is None:
                return dve.do(lambda e: e.tensor_scalar(o, a, s1, None, op0), *toks)
            return dve.do(lambda e: e.tensor_scalar(o, a, s1, s2, op0, op1), *toks)

        def STT(o, a, s, b, op0, op1, *toks):
            return dve.do(lambda e: e.scalar_tensor_tensor(out=o, in0=a, scalar=s, in1=b, op0=op0, op1=op1), *toks)

        def CP(o, a, *toks):
            return dve.do(lambda e: e.tensor_copy(o, a), *toks)

        def RMAX(o, a, *toks):
            return dve.do(lambda e: e.tensor_reduce(o, a, AX.X, ALU.max), *toks)

        def RECIP(o, a, *toks):
            return dve.do(lambda e: e.reciprocal(o, a), *toks)

        def split(dst, src, *toks):
            t = A(dst[0], src, ACT.Copy, *toks)
            return TT(dst[1], src, dst[0].bitcast(F32), ALU.subtract, t, *toks)

        def parts(n, width):
            h = lambda t, a: t[:, a:a + n * width].rearrange("p (a b) -> p a b", a=n)
            return h(HH, 0), h(HL, 0)

        def at(p, k, *cols):
            return tuple(t[(slice(None), k) + (cols or (slice(None),))] for t in p)

        top = [0]

        def area(*shape):
            n = int(np.prod(shape))
            a = arena[:, top[0]:top[0] + n]
            top[0] += n
            assert top[0] <= ARENA, top[0]
            if len(shape) == 1:
                return a
            if len(shape) == 2:
                return a.rearrange("p (a b) -> p a b", a=shape[0])
            return a.rearrange("p (a b c) -> p a b c", a=shape[0], b=shape[1])

        def new_phase():
            top[0] = 0
            now = [pe.last, act.last, dve.last, pool.last]
            for q in (pe, act, dve, pool):
                q.wait(*now)

        pe.wait(VEC, CST)
        act.wait(VEC, CST)
        dve.wait(VEC, CST)
        t_cond = A(scond.rearrange("p a b -> p (a b)"), V("cond", 0, 16), ACT.Silu)
        t_cond = A(csr[:, :, 0:2], scond[:, :, :], ACT.Copy, t_cond)
        t_cond = TT(csr[:, :, 2:4], scond[:, :, :], csr[:, :, 0:2].bitcast(F32), ALU.subtract, t_cond)
        mod_tok = {}
        mod_bank = [None]
        row_free = [None]

        def mod_chunk(l, i):
            i, half = divmod(i, 2)
            w = chunk("mod", l, 2 * i + half)
            if half == 0:
                mod_bank[0] = take(keep=True)
            b = mod_bank[0]
            for k in range(4):
                for p in range(2):
                    t = mm(ps[0:4, b, :], csr[:, 4 * half + k, :], w[p][:, 512 * k:512 * k + 512],
                           half == k == p == 0, half == 1 and k == 3 and p == 1, t_cond, sig=(k == 3 and p == 1))
            chunk_done()
            if half == 0:
                return
            t = A(mrow[:, :], ps[0:4, b, :], ACT.Copy, t, row_free[0])
            free(b, t)
            b = take()
            for m in range(4):
                t = mm(ps[:, b, 2 * m:2 * m + 2], mrow[0:4, 128 * m:128 * m + 128], C("sel4")[0:4, :], True, True, t,
                       sig=(m == 3))
            row_free[0] = t
            bm = V(f"bmod{l}", 4 * i, 4).unsqueeze(2).to_broadcast([128, 4, 2])
            o = modv[l][:, 4 * i:4 * i + 4, :]
            t = TT(o, ps[:, b, 0:8].rearrange("p (m s) -> p m s", s=2), bm, ALU.add, t)
            free(b, t)
            if i in (2, 3, 8, 9):
                t = TS(o, o, 1.0, None, ALU.add, None, t)
            mod_tok[l, i // 2] = t

        def halves(n):
            return ((0, 0, 256), (1, 256, 512)) if n == 512 else ((0, 0, 256),)

        def fold_mod(l, sc, sh, gname, bname, lg):
            t = None
            for s in range(2):
                TT(fold[:, s, :], V(f"{gname}{lg}", 0, 8), modv[l][:, sc:sc + 8, s], ALU.mult, mod_tok[l, sc // 8])
                t = TT(fold[:, 4 + s, :], V(f"{bname}{lg}", 0, 8), modv[l][:, sc:sc + 8, s], ALU.mult)
                t = TT(fold[:, 2 + s, :], fold[:, 4 + s, :], modv[l][:, sh:sh + 8, s], ALU.add, t, mod_tok[l, sh // 8])
            TS(lnc[:, 0, :], V(f"{gname}{lg}", 0, 8), ALPHA, None, ALU.mult, None)
            return TS(lnc[:, 1, :], V(f"{bname}{lg}", 0, 8), ALPHA, None, ALU.mult, None)

        def layer_norm(y, ytok, bm, mtok, n, hout, xout, gtok, lat_only=False):
            SQ, T8, U8 = area(3, n), area(8, n), area(3, n)
            RS, SD = area(n), area(n)
            sqf, uf = [None] * 3, [None] * 3
            bv = take(keep=True)
            for j in range(8):
                c = TT(y[:, j, :], y[:, j, :], ps[:, bm, 0:n], ALU.subtract, mtok)
                q = A(SQ[:, j % 3, :], y[:, j, :], ACT.Square, c, sqf[j % 3])
                v = mm(ps[:, bv, 0:n], C("o1024"), SQ[:, j % 3, :], j == 0, j == 7, q, sig=True)
                sqf[j % 3] = v
            free(bm, c)
            s = A(SD, ps[:, bv, 0:n], ACT.Sqrt, v, bias=EPS5, scale=1.0)
            free(bv, s)
            r = RECIP(RS, SD, s)
            htok, xtok = [], []
            if hout is None:
                for j in range(8):
                    t = STT(T8[:, j, :], y[:, j, :], V("ln2g1", j), RS, ALU.mult, ALU.mult, r)
                    xtok.append(A(xout[:, j, 16:NT], T8[:, j, :], ACT.Identity, t, bias=V("ln2b1", j), scale=1.0))
                return None, xtok
            for j in range(8):
                for s, a, e in halves(n):
                    t = STT(T8[:, j, a:e], y[:, j, a:e], fold[:, s, j:j + 1], RS[:, a:e], ALU.mult, ALU.mult, r, gtok)
                for s, a, e in halves(n):
                    t = A(hout[0][:, j, a:e], T8[:, j, a:e], ACT.Identity, t, bias=fold[:, 2 + s, j:j + 1], scale=1.0)
                for s, a, e in halves(n):
                    h = STT(hout[1][:, j, a:e], T8[:, j, a:e], fold[:, 2 + s, j:j + 1],
                            hout[0][:, j, a:e].bitcast(F32), ALU.add, ALU.subtract, t)
                htok.append(h)
            nx = 256 if lat_only else n
            pool.wait(r, htok[7])
            for j in range(8):
                u = U8[:, j % 3, 0:nx]
                t = pool.do(lambda e, u=u, j=j: e.tensor_tensor(u, y[:, j, 0:nx], RS[:, 0:nx], ALU.mult), uf[j % 3])
                uf[j % 3] = A(y[:, j, 0:nx], u, ACT.Identity, t, gtok, scale=lnc[:, 0, j:j + 1], bias=lnc[:, 1, j:j + 1])
                xtok.append(uf[j % 3])
            return htok, xtok

        def out_proj(key, nk, src, stok, n, mt_per, l, gt, nxt, mean=True):
            ytok = []
            bm = take(keep=True) if mean else None

            def mean_of(j):
                return mm(ps[:, bm, 0:n], C("o1024"), X[:, j, 0:n], j == 0, j == 7, ytok[j], sig=(j == 7))

            for i in range(8 // mt_per):
                w = chunk(*key, i)
                c = nk and (w[0].shape[1] // nk)
                for m in range(mt_per):
                    j = i * mt_per + m
                    b = take()
                    for k in range(nk):
                        t = mm3(ps[:, b, 0:n], w, slice(c * k + 128 * m, c * k + 128 * m + 128), at(src, k, slice(0, n)),
                                k, nk, stok[k], sig=(k == nk - 1))
                    for s, a, e in halves(n):
                        y = STT(X[:, j, a:e], ps[:, b, a:e], modv[l][:, gt + j, s:s + 1], X[:, j, a:e],
                                ALU.mult, ALU.add, t, mod_tok[l, gt // 8], nxt[j])
                    free(b, y)
                    ytok.append(y)
                    if mean and j:
                        mean_of(j - 1)
                chunk_done()
            t = mean_of(7) if mean else None
            return ytok, bm, t

        def ffn(l, htok, xtok, n):
            new_phase()
            area(2 * HALF * 512)
            h2 = lambda a: PARTS[:, a * HALF * 512:a * HALF * 512 + HALF * n].rearrange("p (a b) -> p a b", a=HALF)
            H2 = (h2(0), h2(1))
            H = parts(8, n)
            T = area(3, n)
            SG = area(3, n)
            tfree = [None] * 3
            sfree = [None] * 3
            nh = n // 256
            for half in range(2):
                stok = []
                down = pe.last if half else None
                for i in range(HALF):
                    f = HALF * half + i
                    z = f % 3
                    w = chunk("gu", l, f)
                    bg, bu = take(), take()
                    for k in range(8):
                        tg = mm3(ps[:, bg, 0:n], w, slice(256 * k, 256 * k + 128), at(H, k), k, 8, htok[k], sig=(k == 7))
                    for k in range(8):
                        tu = mm3(ps[:, bu, 0:n], w, slice(256 * k + 128, 256 * k + 256), at(H, k), k, 8, sig=(k == 7))
                    chunk_done()
                    cw = lambda a: V(f"cw{l}", 22 * a + f, 1)
                    g3 = ps[:, bg, 0:n].rearrange("p (s t) -> p s t", s=nh)
                    t3 = T[:, z, :].rearrange("p (s t) -> p s t", s=nh)
                    t = A(T[:, z, :], ps[:, bg, 0:n], ACT.Identity, tg, tfree[z], scale=cw(1), bias=V(f"cb{l}", f))
                    t = STT(t3[:, :, 1:256], g3[:, :, 0:255], cw(0), t3[:, :, 1:256], ALU.mult, ALU.add, t)
                    t = STT(t3[:, :, 0:255], g3[:, :, 1:256], cw(2), t3[:, :, 0:255], ALU.mult, ALU.add, t)
                    free(bg, t)
                    t = A(SG[:, z, :], T[:, z, :], ACT.Silu, t, sfree[z])
                    tfree[z] = t
                    t = TT(SG[:, z, :], SG[:, z, :], ps[:, bu, 0:n], ALU.mult, t, tu)
                    free(bu, t)
                    t = split(at(H2, i), SG[:, z, :], t, down)
                    sfree[z] = t
                    stok.append(t)
                    if l == 0:
                        mod_chunk(1, f)
                if l == 0 and half:
                    mod_chunk(1, 22)
                    mod_chunk(1, 23)
                ytok, bm, mt = out_proj(("down", l, half), HALF, H2, stok, n, 1, l, 40, xtok, half == 1)
                xtok = ytok
            return ytok, bm, mt

        def steps(jobs, stages):
            depth = len(stages)
            state = [None] * len(jobs)
            for i in range(len(jobs) + depth - 1):
                for d, st in enumerate(stages):
                    j = i - d
                    if 0 <= j < len(jobs):
                        state[j] = st(j, jobs[j], state[j])
                yield i

        def run_jobs(jobs, stages):
            for _ in steps(jobs, stages):
                pass

        act.wait(XIN)
        dve.wait(XIN)
        for i in range(8):
            mod_chunk(0, i)
        HP = parts(8, 512)
        QS = area(4, 512)
        KS = area(512)
        KV = area(512)
        KR = area(512)
        QN = area(2, 512)
        QM = area(4, 512)
        KM = area(4, 512)
        VM = area(4, 512)
        VS = area(4, 128)
        TMP = area(2, 512)
        early = top[0]
        QA = area(2, 512)
        SQ = area(2, 512)
        RS = area(512)
        HT = area(3, 512)
        top[0] = early
        P = area(2, 2, 512)
        PT = area(2, 4, 256)

        htok, t_ax, ht_free = [], [], [None] * 3
        for j in range(8):
            h = HT[:, j % 3, :]
            for c, a, e in halves(512):
                t = TS(h[:, a:e], X[:, j, a:e], modv[0][:, 8 + j, c:c + 1], modv[0][:, j, c:c + 1],
                       ALU.mult, ALU.add, mod_tok[0, 0], mod_tok[0, 1], ht_free[j % 3])
            htok.append(split(at(HP, j), h, t))
            ht_free[j % 3] = htok[j]
            t_ax.append(A(X[:, j, :], X[:, j, :], ACT.Copy, htok[j], scale=ALPHA))

        def proj(w, c0, m, n=512):
            b = take()
            c = w[0].shape[1] // 8
            for k in range(8):
                t = mm3(ps[0:m, b, 0:n], w, slice(c * k + c0, c * k + c0 + m), at(HP, k, slice(0, n)), k, 8, htok[k],
                        sig=(k == 7))
            return b, t

        def keep_proj(dst, w, c0, m, n=512):
            b, t = proj(w, c0, m, n)
            t = A(dst, ps[0:m, b, 0:n], ACT.Copy, t)
            free(b, t)
            return t

        tmp_free = [None, None]
        rope_n = [0]

        def rope(dst, rows, perm, cos, sin, tok):
            z = rope_n[0] % 2
            rope_n[0] += 1
            b = take()
            t = mm(ps[0:rows, b, 0:256], C(perm, rows)[0:rows, :], dst[0:rows, 0:256], True, True, tok, sig=True)
            tm = TMP[0:rows, z, 0:256]
            t1 = TT(tm, ps[0:rows, b, 0:256], C(sin)[0:rows, :], ALU.mult, t, tmp_free[z])
            free(b, t1)
            t2 = TT(dst[0:rows, 0:256], dst[0:rows, 0:256], C(cos)[0:rows, :], ALU.mult, t)
            t3 = TT(dst[0:rows, 0:256], dst[0:rows, 0:256], tm, ALU.add, t1, t2)
            tmp_free[z] = t3
            return t3

        def rms_low(src, toks, n, ones, gname, dst):
            b = take()
            for m in range(n):
                q = A(SQ[:, m, :], src(m), ACT.Square, toks[m])
                t = mm(ps[:, b, :], C(ones), SQ[:, m, :], m == 0, m == n - 1, q, sig=(m == n - 1))
            s = A(RS[:, :], ps[:, b, :], ACT.Sqrt, t, bias=EPS6, scale=1.0)
            free(b, s)
            r = RECIP(RS[:, :], RS[:, :], s)
            act.wait(r)
            r = [STT(dst(m), src(m), V(gname, m), RS[:, :], ALU.mult, ALU.mult, r) for m in range(n)]
            act.wait(r[-1])
            return r

        w = chunk("abin", 0)
        qa_tok = [keep_proj(QA[:, m, :], w, 128 * m, 128) for m in range(2)]
        chunk_done()
        qs_tok = []
        w = chunk("abin", 1)
        qs_tok += [keep_proj(QS[:, m, :], w, 128 * m, 128) for m in range(2)]
        chunk_done()
        qn_tok = rms_low(lambda m: QA[:, m, :], qa_tok, 2, "o256", "qnorm", lambda m: QN[:, m, :])
        w = chunk("abin", 2)
        qs_tok += [keep_proj(QS[:, 2 + m, :], w, 128 * m, 128) for m in range(2)]
        chunk_done()
        w = chunk("abin", 3)
        t_kv = keep_proj(KV[:, :], w, 0, 128)
        t_kr = keep_proj(KR[0:96, :], w, 64, 96)
        chunk_done()
        w = chunk("abin", 4)
        t_ks = keep_proj(KS[:, :], w, 0, 128)
        kv_tok = rms_low(lambda m: KV[:, :], [t_kv], 1, "o128", "kvnorm", lambda m: KV[:, :])
        b = take()
        for c in range(4):
            o = ps[:, b, 128 * c:128 * c + 128]
            for k in range(8):
                tok = slice(128 * c, 128 * c + 128)
                col = slice(256 * k + 128, 256 * k + 256)
                mm(o, HP[0][:, k, tok], w[0][:, col], k == 0, False)
                mm(o, HP[1][:, k, tok], w[0][:, col], False, False)
                t = mm(o, HP[0][:, k, tok], w[1][:, col], False, k == 7, sig=(c == 3 and k == 7))
        chunk_done()
        t_vs = A(VS, ps[:, b, :].rearrange("p (c m) -> p c m", c=4), ACT.Copy, t)
        free(b, t_vs)
        t_ks = rope(KS, 128, "r128", "cos128", "sin128", t_ks)
        t_kr = rope(KR, 96, "r96", "cos96", "sin96", t_kr)
        kr_tok = [CP(KM[64:96, h, :], KR[64:96, :], t_kr) for h in range(4)]
        o_after = pe.last

        qm_tok, km_tok = [None] * 4, [None] * 4

        def mla_keys(w, i, h):
            b = take()
            t = mm(ps[0:64, b, :], w[:, 64 * i:64 * i + 64], KV[:, :], True, True, kv_tok[0], sig=True)
            km_tok[h % 4] = A(KM[0:64, h % 4, :], ps[0:64, b, :], ACT.Copy, t)
            free(b, km_tok[h % 4])

        def mla_queries(w, i, h):
            b = take()
            for k in range(2):
                t = mm(ps[0:96, b, :], w[:, 384 * k + 96 * i:384 * k + 96 * i + 96], QN[:, k, :], k == 0, k == 1, qn_tok[k],
                       sig=(k == 1))
            t = A(QM[0:96, h % 4, :], ps[0:96, b, :], ACT.Copy, t)
            free(b, t)
            qm_tok[h % 4] = rope(QM[:, h % 4, :], 96, "r96", "cos96", "sin96", t)

        w = chunk("kvb", 0)
        for c in range(4):
            b = take()
            t = mm(ps[:, b, :], KV[:, 128 * c:128 * c + 128], w[:, 256:768], True, True, kv_tok[0], sig=True)
            t_vm = A(VM[:, c, :], ps[:, b, :], ACT.Copy, t)
            free(b, t_vm)
        for h in range(4):
            mla_keys(w, h, h)
        chunk_done()
        w = chunk("qb", 0)
        for h in range(4):
            mla_queries(w, h, h)
        chunk_done()
        for m in range(4):
            qs_tok[m] = rope(QS[:, m, :], 128, "r128", "cos128", "sin128", qs_tok[m])

        act.wait(o_after)
        dve.wait(o_after)
        OP = HP
        mx, nm, sm, rv, es = (small[:, 16 * a:16 * a + 16] for a in range(5))
        p_free = [[None, None], [None, None]]
        pt_free = [None, None]
        mla_scale = 96.0 ** -0.5

        def att_scores(j, job, st):
            kind, h, lat = job
            k0, nk = (0, 512) if lat else (256, 256)
            sc = mla_scale if kind == "mla" else 0.125
            cols = slice(2 * (j % 4), 2 * (j % 4) + 2)
            c0 = 2 * (j % 4)
            bs, mt = [], []
            for qt in range(2):
                q0 = (0 if lat else 256) + 128 * qt
                b = take()
                o = ps[:, b, 0:nk]
                if kind == "mla":
                    t = mm(o, QM[0:96, h % 4, q0:q0 + 128], KM[0:96, h % 4, k0:k0 + nk], True, True,
                           qm_tok[h % 4], km_tok[h % 4], kr_tok[h % 4], sig=True)
                else:
                    r = 64 * (h // 4)
                    t = mm(o, QS[r:r + 64, h % 4, q0:q0 + 128], KS[r:r + 64, k0:k0 + nk], True, not lat,
                           qs_tok[h % 4], t_ks, sig=True)
                    if lat:
                        kt, mask = ((1, "maska"), (0, "maskb"))[qt]
                        t = mm(ps[:, b, 128 * kt:128 * kt + 128], ident, C(mask), False, True, sig=True)
                t = RMAX(mx[:, c0 + qt:c0 + qt + 1], o, t)
                bs.append(b)
                mt.append(t)
            if kind == "mla":
                tn = TS(nm[:, cols], mx[:, cols], -sc, None, ALU.mult, None, t)
            else:
                t = TS(mx[:, cols], mx[:, cols], sc, V("sink", h), ALU.mult, ALU.max, t)
                tn = TS(nm[:, cols], mx[:, cols], -1.0, None, ALU.mult, None, t)
            z = j % 2
            for qt in range(2):
                te = A(P[:, z, qt, 0:nk], ps[:, bs[qt], 0:nk], ACT.Exp, tn, p_free[z][qt],
                       bias=nm[:, c0 + qt:c0 + qt + 1], scale=sc, accum_out=sm[:, c0 + qt:c0 + qt + 1])
                free(bs[qt], te)
            if kind == "swa":
                for qt in range(2):
                    te = A(es[:, c0 + qt:c0 + qt + 1], V("sink", h), ACT.Exp, bias=nm[:, c0 + qt:c0 + qt + 1], scale=1.0)
                te = TT(sm[:, cols], sm[:, cols], es[:, cols], ALU.add, te)
            tr_ = RECIP(rv[:, cols], sm[:, cols], te)
            pt = []
            for qt in range(2):
                pt.append(TS(P[:, z, qt, 0:nk], P[:, z, qt, 0:nk], rv[:, c0 + qt:c0 + qt + 1], None, ALU.mult, None, tr_))
            return pt

        def att_trans(j, job, pt):
            lat = job[2]
            z = j % 2
            n = 4 if lat else 2
            for qt in range(2):
                b = take()
                for kt in range(n):
                    t = tr(ps[:, b, 128 * kt:128 * kt + 128], P[:, z, qt, 128 * kt:128 * kt + 128], ident, pt[qt],
                           sig=(kt == n - 1))
                p_free[z][qt] = t
                src = ps[:, b, 0:128 * n].rearrange("p (a q) -> p a q", a=n)
                dst = PT[:, z, 0:n, 128 * qt:128 * qt + 128]
                e = A(dst, src, ACT.Copy, t, pt_free[z]) if qt else CP(dst, src, t, pt_free[z])
                free(b, e)
                pt[qt] = e
            return pt

        o_bank = {}
        o_tok = [None] * 8

        def att_pv(j, job, et):
            kind, h, lat = job
            z = j % 2
            n = 4 if lat else 2
            if kind == "mla":
                r, ot, first, second = 64 * (h % 2), h // 2, h % 2 == 0, h % 2 == 1
            else:
                r, ot, first, second = 64 * (h // 4), 4 + h % 4, h < 4, h >= 4
            if first:
                o_bank[ot, lat] = take(keep=True)
            b = o_bank[ot, lat]
            for kt in range(n):
                vt = kt if lat else kt + 2
                v = VM[:, vt, 64 * h:64 * h + 64] if kind == "mla" else VS[:, vt, 64 * (h // 4):64 * (h // 4) + 64]
                t = mm(ps[r:r + 64, b, 0:256], v, PT[:, z, kt, :], kt == 0, kt == n - 1, et[0], et[1],
                       t_vm, t_vs, sig=(kt == n - 1))
            pt_free[z] = t
            if second:
                q0 = 0 if lat else 256
                hi, lo = at(OP, ot, slice(q0, q0 + 256))
                e = A(hi, ps[:, b, 0:256], ACT.Copy, t)
                e = TT(lo, ps[:, b, 0:256], hi.bitcast(F32), ALU.subtract, e)
                free(b, e)
                o_tok[ot] = e
            if j % 2 == 1 and mod_left:
                mod_chunk(0, mod_left.pop(0))
            return None

        stages = [att_scores, att_trans, att_pv]
        pairs = lambda h: [x for lat in (1, 0) for x in (("mla", h, lat), ("mla", h + 1, lat))]
        mod_left = list(range(8, 16))
        run_jobs(pairs(0) + pairs(2), stages)
        while mod_left:
            mod_chunk(0, mod_left.pop(0))
        w = chunk("qb", 1)
        act.wait(pe.last)
        dve.wait(pe.last)
        for h in range(4, 8):
            mla_queries(w, h - 4, h)
        chunk_done()
        w = chunk("kvb", 1)
        for h in range(4, 8):
            mla_keys(w, h - 4, h)
        chunk_done()
        mod_left = list(range(16, 24))
        run_jobs(pairs(4) + pairs(6) + [("swa", h, lat) for m in range(4) for lat in (1, 0) for h in (m, m + 4)], stages)
        while mod_left:
            mod_chunk(0, mod_left.pop(0))

        ytok, bm, mt = out_proj(("about",), 8, OP, o_tok, 512, 2, 0, 16, t_ax)
        t_f = fold_mod(0, 32, 24, "ln1g", "ln1b", 0)
        new_phase()
        htok, xtok = layer_norm(X, ytok, bm, mt, 512, parts(8, 512), None, t_f)
        ytok, bm, mt = ffn(0, htok, xtok, 512)
        t_f = fold_mod(1, 8, 0, "ln2g", "ln2b", 0)
        new_phase()
        htok, xtok = layer_norm(X, ytok, bm, mt, 512, parts(8, 512), None, t_f, lat_only=True)

        new_phase()
        Kd = area(8, 512)
        Vd = area(4, 1024)
        Qd = X[:, :, 256:512]
        TMP = area(2, 512)
        tmp_free = [None, None]
        P = area(2, 2, 512)
        PA = area(2, 2, 512)
        PT = area(2, 4, 256)
        kd_tok, qd_tok = [], []
        for i in range(4):
            w = chunk("din", 4 + i)
            for m in range(2):
                h = 2 * i + m
                kd_tok.append(keep_proj(Kd[:, h, :], w, 128 * m, 128))
                if h:
                    kd_tok[h - 1] = rope(Kd[:, h - 1, :], 128, "r128", "cos128", "sin128", kd_tok[h - 1])
            chunk_done()
        kd_tok[7] = rope(Kd[:, 7, :], 128, "r128", "cos128", "sin128", kd_tok[7])
        for i in range(4):
            w = chunk("din", 8 + i)
            for c in range(0, 4, 2):
                b = take()
                for d in range(2):
                    o = ps[:, b, 256 * d:256 * d + 256]
                    for k in range(8):
                        tok = slice(128 * (c + d), 128 * (c + d) + 128)
                        col = slice(256 * k, 256 * k + 256)
                        mm(o, HP[0][:, k, tok], w[0][:, col], k == 0, False)
                        mm(o, HP[1][:, k, tok], w[0][:, col], False, False)
                        t = mm(o, HP[0][:, k, tok], w[1][:, col], False, k == 7, sig=(d == 1 and k == 7))
                t_vd = A(Vd[:, c:c + 2, 256 * i:256 * i + 256], ps[:, b, :].rearrange("p (c n) -> p c n", c=2), ACT.Copy, t)
                free(b, t_vd)
            chunk_done()
        for i in range(4):
            w = chunk("din", i)
            for m in range(2):
                h = 2 * i + m
                qd_tok.append(keep_proj(Qd[:, h, :], w, 128 * m, 128, 256))
                if h:
                    qd_tok[h - 1] = rope(Qd[:, h - 1, :], 128, "r128", "cos128", "sin128", qd_tok[h - 1])
            chunk_done()
        qd_tok[7] = rope(Qd[:, 7, :], 128, "r128", "cos128", "sin128", qd_tok[7])
        o_after = pe.last
        lm = small[:, 96:104]
        lv = V("lam", 0, 256)
        for a in range(2):
            q, k = lv[:, 128 * a:128 * a + 64], lv[:, 128 * a + 64:128 * a + 128]
            tl = dve.do(lambda e, q=q, k=k, a=a: e.tensor_tensor_reduce(
                out=TMP[:, a, 0:64], in0=q, in1=k, scale=1.0, scalar=0.0, op0=ALU.mult, op1=ALU.add,
                accum_out=lm[:, a:a + 1]), *tmp_free)
        tl = A(lm[:, 2:4], lm[:, 0:2], ACT.Exp, tl)
        tl = TT(lm[:, 4:5], lm[:, 3:4], lm[:, 2:3], ALU.subtract, tl)
        t_lam = TS(lm[:, 5:6], lm[:, 4:5], -LAM_INIT, None, ALU.add, None, tl)
        act.wait(o_after)
        dve.wait(o_after)
        OD = parts(8, 256)
        p_free = [None, None]
        pa_free = [[None, None], [None, None]]
        pt_free = [None, None]

        def diff_scores(j, h, st):
            c0 = 4 * (j % 2)
            cols = slice(c0, c0 + 4)
            bs = []
            for qt in range(2):
                for a in range(2):
                    b = take()
                    t = mm(ps[:, b, :], Qd[64 * a:64 * a + 64, h, 128 * qt:128 * qt + 128],
                           Kd[64 * a:64 * a + 64, h, :], True, True, qd_tok[h], kd_tok[h], sig=True)
                    t = RMAX(mx[:, c0 + 2 * qt + a:c0 + 2 * qt + a + 1], ps[:, b, :], t)
                    bs.append(b)
            tn = TS(nm[:, cols], mx[:, cols], -0.125, None, ALU.mult, None, t)
            z = j % 2
            pt = []
            for qt in range(2):
                for a in range(2):
                    i = 2 * qt + a
                    dst = (PA if a == 0 else P)[:, z, qt, :]
                    te = A(dst, ps[:, bs[i], :], ACT.Exp, tn, pa_free[z][qt], p_free[z],
                           bias=nm[:, c0 + i:c0 + i + 1], scale=0.125, accum_out=sm[:, c0 + i:c0 + i + 1])
                    free(bs[i], te)
            tr_ = RECIP(rv[:, cols], sm[:, cols], te)
            l2 = TS(es[:, cols], rv[:, cols], lm[:, 5:6], None, ALU.mult, None, tr_, t_lam)
            for qt in range(2):
                i = c0 + 2 * qt
                t = TS(P[:, z, qt, :], P[:, z, qt, :], es[:, i + 1:i + 2], None, ALU.mult, None, l2)
                t = STT(PA[:, z, qt, :], PA[:, z, qt, :], rv[:, i:i + 1], P[:, z, qt, :], ALU.mult, ALU.add, t)
                pt.append(t)
            p_free[z] = t
            return pt

        def diff_trans(j, h, pt):
            z = j % 2
            for qt in range(2):
                b = take()
                for kt in range(4):
                    t = tr(ps[:, b, 128 * kt:128 * kt + 128], PA[:, z, qt, 128 * kt:128 * kt + 128], ident, pt[qt],
                           sig=(kt == 3))
                pa_free[z][qt] = t
                src = ps[:, b, :].rearrange("p (a q) -> p a q", a=4)
                dst = PT[:, z, :, 128 * qt:128 * qt + 128]
                e = A(dst, src, ACT.Copy, t, pt_free[z]) if qt else CP(dst, src, t, pt_free[z])
                free(b, e)
                pt[qt] = e
            return pt

        od_tok = [None] * 8

        def diff_pv(j, h, et):
            z = j % 2
            b = take()
            for kt in range(4):
                t = mm(ps[:, b, 0:256], Vd[:, kt, 128 * h:128 * h + 128], PT[:, z, kt, :], kt == 0, kt == 3,
                       et[0], et[1], t_vd, sig=(kt == 3))
            pt_free[z] = t
            e = CP(Qd[:, h, :], ps[:, b, 0:256], t)
            free(b, e)
            od_tok[h] = e

        run_jobs(list(range(8)), [diff_scores, diff_trans, diff_pv])

        sg = small[:, 104:105]
        t_sg = TS(sg, V("subln"), 1.0 - LAM_INIT, None, ALU.mult, None)
        SQD = PA.rearrange("p a b c -> p (a b c)")
        RSD = P.rearrange("p a b c -> p (a b c)")
        act.wait(pe.last, dve.last)
        sq = [A(SQD[:, 256 * h:256 * h + 256], Qd[:, h, :], ACT.Square, od_tok[h]) for h in range(8)]
        rs = []
        for a in range(4):
            b = take()
            t = mm(ps[:, b, :], C("o128"), SQD[:, 512 * a:512 * a + 512], True, True, sq[2 * a + 1], sig=True)
            s = A(RSD[:, 512 * a:512 * a + 512], ps[:, b, :], ACT.Sqrt, t, bias=EPS6, scale=1.0)
            free(b, s)
            rs.append(s)
        for a in range(4):
            r = RECIP(RSD[:, 512 * a:512 * a + 512], RSD[:, 512 * a:512 * a + 512], rs[a])
            for h in (2 * a, 2 * a + 1):
                t = STT(Qd[:, h, :], Qd[:, h, :], sg, RSD[:, 256 * h:256 * h + 256], ALU.mult, ALU.mult, r, t_sg)
                od_tok[h] = split(at(OD, h), Qd[:, h, :], t)

        ytok, bm, mt = out_proj(("dout",), 8, OD, od_tok, 256, 2, 1, 16, xtok)
        t_f = fold_mod(1, 32, 24, "ln1g", "ln1b", 1)
        new_phase()
        XL = X[:, :, 0:256]
        R = XF[:, 0:8 * NT].rearrange("p (a b) -> p a b", a=8)
        htok, xtok = layer_norm(XL, ytok, bm, mt, 256, parts(8, 256), None, t_f)
        ytok, bm, mt = ffn(1, htok, xtok, 256)
        new_phase()
        _, xtok = layer_norm(XL, ytok, bm, mt, 256, None, R, None)

        act.wait(META)
        for j in range(8):
            t = A(R[:, j, 0:16], MT[:, 16 * j:16 * j + 16], ACT.Copy, xtok[-1])
        rtok = [t] * 8
        YP = parts(16, NT)

        def rms_all(sq, rstd, gname, rtok, dst):
            b = take()
            for j in range(8):
                q = A(sq[:, j, :], R[:, j, :], ACT.Square, rtok[j])
                t = mm(ps[:, b, 0:NT], C("o1024"), sq[:, j, :], j == 0, j == 7, q, sig=(j == 7))
            s = A(rstd, ps[:, b, 0:NT], ACT.Sqrt, t, bias=EPS6, scale=1.0)
            free(b, s)
            r = RECIP(rstd, rstd, s)
            return [STT(dst[:, j, :], R[:, j, :], V(gname, j), rstd, ALU.mult, ALU.mult, r) for j in range(8)]

        new_phase()
        ZS = area(8, NT)
        XC = area(16, NT)
        YC = area(8, NT)
        XD = area(3, 1024)
        CBm = area(4, 656)
        EE = area(2, 656)
        dtr, dab, dtl, dtt, dA, aex = (area(48) for _ in range(6))
        bias6 = area(96)
        spare = XF[:, 8 * NT:]
        CV = spare[:, 0:816].rearrange("p (a b) -> p a b", a=3)
        CG = spare[:, 816:1360].rearrange("p (a b) -> p a b", a=2)
        SG2 = spare[:, 1360:1648].rearrange("p (a b) -> p a b", a=2)
        YS = XC[:, 8:16, :]
        UF = XD.rearrange("p a b -> p (a b)")[:, 0:8 * NT].rearrange("p (a b) -> p a b", a=8)
        uf_tok = rms_all(ZS, EE[:, 0, 0:NT], "nmix", rtok, UF)
        utok = [split(at(YP, j), UF[:, j, :], uf_tok[j]) for j in range(8)]

        b = take()
        for c in range(3):
            o, n = TOFF[c], TLEN[c]
            for k in range(8):
                t = mm(ps[0:n, b, 16 * c:16 * c + 16], UF[:, k, o:o + n], V("wdt", 16 * k, 16), k == 0, k == 7,
                       uf_tok[k], sig=(c == 2 and k == 7))
        tz = dve.do(lambda e: e.memset(dtr, 0.0))
        for c in range(3):
            n = TLEN[c]
            tz = TT(dtr[0:n, 16 * c:16 * c + 16], ps[0:n, b, 16 * c:16 * c + 16], V("dtb", 0, 16)[0:n, :], ALU.add, t, tz)
        free(b, tz)
        t = A(dab, dtr, ACT.Abs, tz)
        t = A(dab, dab, ACT.Exp, t, scale=-1.0)
        ta = A(aex[:, 0:16], V("alog", 0, 16), ACT.Exp)
        t = A(dtl, dab, ACT.Ln, t, bias=1.0, scale=1.0)
        t_dt = STT(dtt, dtr, 0.0, dtl, ALU.max, ALU.add, t)
        aeb = aex[:, 0:16].unsqueeze(1).to_broadcast([128, 3, 16])
        t_dA = STT(dA.rearrange("p (c h) -> p c h", c=3), dtt.rearrange("p (c h) -> p c h", c=3), -1.0, aeb,
                   ALU.mult, ALU.mult, ta, t_dt)

        cv_free = [None] * 3
        cg_free = [None] * 2
        zs_tok, xc_tok, yc_tok = [], [], [None] * 8
        hold = {}

        def win_tile(w, m):
            b = take()
            for k in range(8):
                t = mm3(ps[:, b, 0:NT], w, slice(256 * k + 128 * m, 256 * k + 128 * m + 128), at(YP, k), k, 8, utok[k],
                        sig=(k == 7))
            return b, t

        for i in range(12):
            w = chunk("win", i)
            for m in range(2):
                f = 2 * i + m
                b, t = win_tile(w, m)
                if f < 8:
                    t = A(ZS[:, f, :], ps[:, b, 0:NT], ACT.Silu, t)
                    free(b, t)
                    zs_tok.append(t)
                else:
                    x = f - 8
                    z = x % 3
                    wv = lambda a: V("scw", 16 * a + x)
                    t = A(CV[:, z, :], ps[:, b, 0:NT], ACT.Identity, t, cv_free[z], scale=wv(3), bias=V("scb", x))
                    for a in (2, 1, 0):
                        sft = 3 - a
                        t = STT(CV[:, z, sft:NT], ps[:, b, 0:NT - sft], wv(a), CV[:, z, sft:NT], ALU.mult, ALU.add, t)
                    free(b, t)
                    t = A(XC[:, x, :], CV[:, z, :], ACT.Silu, t)
                    cv_free[z] = t
                    xc_tok.append(t)
            chunk_done()

        def sc_tile(f, b, t):
            x, part = divmod(f, 3)
            z, zz = x % 3, x % 2
            if part == 0:
                kept.add(b)
                hold["b"], hold["bt"] = b, t
            elif part == 1:
                hold["ct"] = A(CG[:, zz, :], ps[:, b, 0:NT], ACT.Copy, t, cg_free[zz])
                free(b, hold["ct"])
            else:
                wv = lambda a: V("shw", 8 * a + x)
                t = TT(CG[:, zz, :], CG[:, zz, :], ps[:, b, 0:NT], ALU.mult, t, hold["ct"])
                free(b, t)
                t = TS(CV[:, z, :], CG[:, zz, :], wv(2), None, ALU.mult, None, t, cv_free[z])
                t = STT(CV[:, z, 1:NT], CG[:, zz, 0:NT - 1], wv(1), CV[:, z, 1:NT], ALU.mult, ALU.add, t)
                t = STT(CV[:, z, 2:NT], CG[:, zz, 0:NT - 2], wv(0), CV[:, z, 2:NT], ALU.mult, ALU.add, t)
                t = TT(YC[:, x, :], CV[:, z, :], ps[:, hold["b"], 0:NT], ALU.mult, t, hold["bt"])
                free(hold["b"], t)
                cv_free[z] = t
                yc_tok[x] = t
                cg_free[zz] = A(CG[:, zz, :], YC[:, x, :], ACT.Square, t)

        def sc_norm(x):
            z, zz = x % 3, x % 2
            b = take()
            t = mm(ps[:, b, 0:NT], C("blk64"), CG[:, zz, :], True, True, cg_free[zz], sig=True)
            cg_free[zz] = t
            s = A(CV[:, z, :], ps[:, b, 0:NT], ACT.Sqrt, t, cv_free[z], bias=EPS6, scale=1.0)
            free(b, s)
            r = RECIP(CV[:, z, :], CV[:, z, :], s)
            t = STT(YC[:, x, :], YC[:, x, :], V("shn", x), CV[:, z, :], ALU.mult, ALU.mult, r)
            cv_free[z] = t
            yc_tok[x] = split(at(YP, 8 + x), YC[:, x, :], t)

        def dAc(c):
            return dA[0:TLEN[c], 16 * c:16 * c + 16]

        def decay_sums():
            b = take()
            for c in range(3):
                n = TLEN[c]
                mm(ps[0:n, b, 16 * c:16 * c + 16], C("tri")[0:n, 0:n], dAc(c), True, True, t_dA)
            mm(ps[0:16, b, 48:64], C("sfx")[0:16, 0:16], dAc(0), True, True)
            mm(ps[0:16, b, 64:80], C("sfx")[0:16, 0:16], dAc(0), True, False)
            mm(ps[0:16, b, 64:80], C("ones", 16), dAc(1), False, True)
            t = mm(ps[:, b, 80:96], C("sfx"), dAc(1), True, True, sig=True)
            TS(bias6[0:16, 0:16], ps[0:16, b, 0:16], -1.0, None, ALU.mult, None, t)
            TS(bias6[:, 16:48], ps[:, b, 16:48], -1.0, None, ALU.mult, None)
            CP(bias6[0:16, 48:80], ps[0:16, b, 48:80])
            t = CP(bias6[:, 80:96], ps[:, b, 80:96])
            free(b, t)
            return t

        cb_tok = []

        def group_cb(g):
            Bt, Ct = XC[:, 8 + g, :], XC[:, 12 + g, :]
            b, b2 = take(), take()
            mm(ps[0:16, b, 0:272], Bt[:, 0:16], Ct[:, :], True, True, xc_tok[8 + g], xc_tok[12 + g])
            t = mm(ps[:, b, 272:400], Bt[:, 144:272], Ct[:, 144:272], True, True, sig=True)
            t2 = mm(ps[:, b2, 0:256], Bt[:, 16:144], Ct[:, 16:272], True, True, sig=True)
            TT(CBm[0:16, g, 0:16], ps[0:16, b, 0:16], C("tri", 16)[0:16, :], ALU.mult, t)
            CP(CBm[0:16, g, 16:272], ps[0:16, b, 16:272])
            t = TT(CBm[:, g, 528:656], ps[:, b, 272:400], C("tri"), ALU.mult)
            free(b, t)
            TT(CBm[:, g, 272:400], ps[:, b2, 0:128], C("tri"), ALU.mult, t2)
            t = CP(CBm[:, g, 400:528], ps[:, b2, 128:256])
            free(b2, t)
            cb_tok.append(t)

        xd_tok = []

        def token_x(c):
            o, n = TOFF[c], TLEN[c]
            for a in range(2):
                b = take()
                for m in range(4):
                    t = tr(ps[0:n, b, 128 * m:128 * m + 128], XC[:, 4 * a + m, o:o + n], ident, xc_tok[4 * a + m],
                           sig=(m == 3))
                db = dtt[0:n, 16 * c + 8 * a:16 * c + 8 * a + 8].unsqueeze(2).to_broadcast([n, 8, 64])
                t = TT(XD[0:n, c, 512 * a:512 * a + 512].rearrange("p (h q) -> p h q", h=8),
                       ps[0:n, b, :].rearrange("p (h q) -> p h q", h=8), db, ALU.mult, t, t_dt)
                free(b, t)
                xd_tok.append(t)

        ee_free = [None] * 2
        sg_free = [None] * 2
        y_bank = {}
        ys_tok = []

        def head_decay(j, h, st):
            z = j % 2
            b = take()
            for c in range(3):
                o, n = TOFF[c], TLEN[c]
                d = dA[0:n, 16 * c + h:16 * c + h + 1].to_broadcast([n, 128])
                t = mm(ps[:, b, o:o + n], d, C("tri", n)[0:n, :], True, True, sig=(c == 2))
            bc = lambda i, n: bias6[0:n, 16 * i + h:16 * i + h + 1]
            TS(SG2[0:16, z, 0:16], ps[0:16, b, 0:16], bc(0, 16), 0.0, ALU.add, ALU.min, t, sg_free[z], t_b6)
            TS(EE[:, z, 272:400], ps[:, b, 16:144], bc(1, 128), 0.0, ALU.add, ALU.min, ee_free[z])
            s2 = TS(EE[:, z, 528:656], ps[:, b, 144:272], bc(2, 128), 0.0, ALU.add, ALU.min)
            e = A(EE[0:16, z, 0:16], SG2[0:16, z, 0:16], ACT.Exp, s2, ee_free[z])
            sg_free[z] = e
            A(EE[0:16, z, 16:144], ps[0:16, b, 16:144], ACT.Exp, bias=bc(3, 16), scale=1.0)
            A(EE[0:16, z, 144:272], ps[0:16, b, 144:272], ACT.Exp, bias=bc(4, 16), scale=1.0)
            e = A(EE[:, z, 400:528], ps[:, b, 144:272], ACT.Exp, bias=bc(5, 128), scale=1.0)
            free(b, e)
            A(EE[:, z, 272:400], EE[:, z, 272:400], ACT.Exp)
            e = A(EE[:, z, 528:656], EE[:, z, 528:656], ACT.Exp)
            TT(EE[0:16, z, 0:272], EE[0:16, z, 0:272], CBm[0:16, h // 4, 0:272], ALU.mult, e, cb_tok[h // 4])
            return TT(EE[:, z, 272:656], EE[:, z, 272:656], CBm[:, h // 4, 272:656], ALU.mult)

        def head_out(j, h, t):
            z = j % 2
            r = 64 * (h % 2)
            if h % 2 == 0:
                y_bank[0] = take(keep=True)
            b = y_bank[0]
            hc = slice(64 * h, 64 * h + 64)
            mm(ps[r:r + 64, b, 0:272], XD[0:16, 0, hc], EE[0:16, z, 0:272], True, False, t, xd_tok[-1])
            mm(ps[r:r + 64, b, 16:272], XD[:, 1, hc], EE[:, z, 272:528], False, False)
            t = mm(ps[r:r + 64, b, 144:272], XD[:, 2, hc], EE[:, z, 528:656], False, True, sig=True)
            ee_free[z] = t
            if h % 2:
                x = h // 2
                t = STT(YS[:, x, :], XC[:, x, :], V("dskip", x), ps[:, b, 0:NT], ALU.mult, ALU.add, t)
                free(b, t)
                ys_tok.append(TT(YS[:, x, :], YS[:, x, :], ZS[:, x, :], ALU.mult, t, zs_tok[x]))

        heads = steps(list(range(16)), [head_decay, head_out])
        for i in range(12):
            w = chunk("win", 12 + i)
            for m in range(2):
                f = 2 * i + m
                b, t = win_tile(w, m)
                sc_tile(f, b, t)
                if f == 0:
                    t_b6 = decay_sums()
                elif f < 5:
                    group_cb(f - 1)
                    if f < 4:
                        token_x(f - 1)
                else:
                    next(heads, None)
                if f % 3 == 1 and f > 3:
                    sc_norm(f // 3 - 1)
            chunk_done()
        win_end = pe.last
        sc_norm(7)
        act.wait(win_end)
        dve.wait(win_end)

        def wout_half(half, i, toks):
            w = chunk("wout", half, i)
            for m in range(2):
                j = 2 * i + m
                b = take()
                for k in range(8):
                    t = mm3(ps[:, b, 0:NT], w, slice(256 * k + 128 * m, 256 * k + 128 * m + 128), at(YP, 8 * half + k),
                            k, 8, toks[k], sig=(k == 7))
                rtok[j] = TT(R[:, j, :], R[:, j, :], ps[:, b, 0:NT], ALU.add, t)
                free(b, rtok[j])
            chunk_done()

        for _ in heads:
            pass
        SQ2, RS2 = XC, EE
        act.wait(pe.last, dve.last)
        sq = [A(SQ2[:, x, :], YS[:, x, :], ACT.Square, ys_tok[x]) for x in range(8)]
        wout_half(1, 0, yc_tok)
        rs = []
        for g in range(4):
            b = take()
            for m in range(2):
                t = mm(ps[:, b, 0:NT], C("o256"), SQ2[:, 2 * g + m, :], m == 0, m == 1, sq[2 * g + m], sig=(m == 1))
            r = RS2.rearrange("p a b -> p (a b)")[:, NT * g:NT * g + NT]
            s = A(r, ps[:, b, 0:NT], ACT.Sqrt, t, bias=EPS6, scale=1.0)
            free(b, s)
            rs.append((r, s))
        for i in range(1, 4):
            wout_half(1, i, yc_tok)
        for g in range(4):
            r, s = rs[g]
            s = RECIP(r, r, s)
            for x in (2 * g, 2 * g + 1):
                t = STT(YS[:, x, :], YS[:, x, :], V("ssdn", x), r, ALU.mult, ALU.mult, s)
                ys_tok[x] = split(at(YP, x), YS[:, x, :], t)
        for i in range(4):
            wout_half(0, i, ys_tok)

        new_phase()
        area(2 * HALF * 512)
        UT = tuple(PARTS[:, a:a + 3072].rearrange("p (c f) -> p c f", c=3) for a in (0, 3072))
        P = PARTS[:, 6144:7680].rearrange("p (c s) -> p c s", c=3)
        PT = PARTS[:, 7680:7680 + 4 * NT].rearrange("p (g t) -> p g t", g=4)
        Y = PARTS[:, 8768:9792], PARTS[:, 9792:10816]
        HT = tuple(PARTS[:, a:a + 1024].rearrange("p (z s) -> p z s", z=2) for a in (0, 1024))
        XG = parts(8, 512)
        UF = area(8, NT)
        RSTD = area(NT)
        SG = area(2, 512)
        CNT = area(16)
        CW = area(16)
        lg = area(3, 20)
        comb = area(3, 4, 4)
        hot = area(3, 3, 4)
        pr = area(3, 4, 4)
        sel, ew = area(3, 4), area(3, 4)
        col = area(8, 3)
        SQ2 = arena[:, 0:8 * NT].rearrange("p (a b) -> p a b", a=8)
        uf_tok = rms_all(SQ2, RSTD, "nffn", rtok, UF)
        b_r = take(keep=True)
        for c in range(3):
            o, n = TOFF[c], TLEN[c]
            for k in range(8):
                t_r = mm(ps[0:n, b_r, 20 * c:20 * c + 20], UF[:, k, o:o + n], V("rw", 20 * k, 20), k == 0, k == 7,
                         uf_tok[k], sig=(c == 2 and k == 7))

        def over(a, n=4):
            return a.unsqueeze(2).to_broadcast([128, 3, n])

        def first_max(src, m, h, tok):
            t = RMAX(m, src, tok)
            t = TT(h, src, over(m), ALU.is_equal, t)
            t = TT(h, h, C("rank").unsqueeze(1).to_broadcast([128, 3, 4]), ALU.mult, t)
            t = RMAX(col[:, 7, :], h, t)
            return TT(h, h, over(col[:, 7, :]), ALU.is_equal, t)

        gate_tok = []

        def route(t):
            tz = dve.do(lambda e: e.memset(lg.rearrange("p a b -> p (a b)"), 0.0))
            for c in range(3):
                n = TLEN[c]
                tl = TT(lg[0:n, c, :], ps[0:n, b_r, 20 * c:20 * c + 20], V("rb", 0, 20)[0:n, :], ALU.add, t, tz)
            free(b_r, tl)
            gl = lg[:, :, 0:4]
            el = lg[:, :, 4:20].rearrange("p c (g e) -> p c g e", g=4)
            gm, m1, m2, ex, gs, w1, w2 = (col[:, i, :] for i in range(7))
            gh, h1, h2 = (hot[:, i, :, :] for i in range(3))
            tg = first_max(gl, gm, gh, tl)
            gate_tok.append(tg)
            t = TT(ew, gl, over(gm), ALU.subtract, tg)
            te = A(ew, ew, ACT.Exp, t)
            for c in range(3):
                t = TT(pr[:, c, :, :], el[:, c, :, :], gh[:, c, :].unsqueeze(2).to_broadcast([128, 4, 4]), ALU.mult, tg)
            t = dve.do(lambda e: e.tensor_reduce(sel, pr.rearrange("p c g e -> p c e g"), AX.X, ALU.add), t)
            t = first_max(sel, m1, h1, t)
            t = STT(sel, h1, -3e38, sel, ALU.mult, ALU.add, t)
            t = first_max(sel, m2, h2, t)
            t = TT(ex, m2, m1, ALU.subtract, t)
            tx = A(ex, ex, ACT.Exp, t, te)
            t = dve.do(lambda e: e.tensor_reduce(gs, ew, AX.X, ALU.add), te)
            t = STT(w1, ex, 1.0, gs, ALU.add, ALU.mult, tx, t)
            t = RECIP(w1, w1, t)
            t = TT(w2, ex, w1, ALU.mult, t)
            t = TT(h2, h2, over(w2), ALU.mult, t)
            t1 = TT(h1, h1, over(w1), ALU.mult)
            t = TT(h1, h1, h2, ALU.add, t, t1)
            for c in range(3):
                t0 = TT(comb[:, c, :, :], h1[:, c, :].unsqueeze(1).to_broadcast([128, 4, 4]),
                        gh[:, c, :].unsqueeze(2).to_broadcast([128, 4, 4]), ALU.mult, t)
            return t0

        t_comb = route(t_r)
        gh = hot[:, 0, :, :]

        ut_tok = []
        for c in range(3):
            o, n = TOFF[c], TLEN[c]
            for a in range(2):
                b = take()
                for k in range(4):
                    t = tr(ps[0:n, b, 128 * k:128 * k + 128], UF[:, 4 * a + k, o:o + n], ident, uf_tok[4 * a + k],
                           sig=(k == 3))
                h = slice(512 * a, 512 * a + 512)
                t = split((UT[0][0:n, c, h], UT[1][0:n, c, h]), ps[0:n, b, :], t)
                free(b, t)
                ut_tok.append(t)

        b = take()
        for c in range(4):
            m = TLEN[c] if c < 3 else 128
            for c2 in range(min(c, 2) + 1):
                n = TLEN[c2]
                t = mm(ps[0:m, b, 4 * c:4 * c + 4], C("tri" if c2 == c else "ones")[0:n, 0:m], gh[0:n, c2, :],
                       c2 == 0, c2 == min(c, 2), gate_tok[0], sig=(c == 3 and c2 == 2))
        for c in range(4):
            m = TLEN[c] if c < 3 else 128
            t_cnt = CP(CNT[0:m, 4 * c:4 * c + 4], ps[0:m, b, 4 * c:4 * c + 4], t)
        free(b, t_cnt)
        for c in range(3):
            n = TLEN[c]
            for g in range(4):
                t_p = TS(P[0:n, c, 128 * g:128 * g + 128], C("slot")[0:n, :], CNT[0:n, 4 * c + g:4 * c + g + 1],
                         gh[0:n, c, g:g + 1], ALU.is_equal, ALU.mult, t_cnt)
        t = RMAX(small[:, 0:1], CNT[:, 12:16], t_cnt)
        flag_tok = TS(flag[:, :], small[:, 0:1], float(CAP), None, ALU.is_gt, None, t)

        xg_tok = []
        for k in range(8):
            for p in range(2):
                b = take()
                for c in range(3):
                    n = TLEN[c]
                    t = mm(ps[:, b, :], UT[p][0:n, c, 128 * k:128 * k + 128], P[0:n, c, :], c == 0, c == 2, t_p, *ut_tok,
                           sig=(c == 2))
                t = CP(XG[1][:, k, :], ps[:, b, :], t) if p else A(XG[0][:, k, :], ps[:, b, :], ACT.Copy, t)
                free(b, t)
                xg_tok.append(t)
        gathered = pe.last

        PF = P.bitcast(F32)
        b = take()
        for g in range(4):
            for c in range(3):
                n = TLEN[c]
                t = mm(ps[:, b, 4 * g:4 * g + 4], PF[0:n, c, 128 * g:128 * g + 128], comb[0:n, c, g, :], c == 0, c == 2,
                       t_comb, sig=(g == 3 and c == 2))
        t_cw = CP(CW, ps[:, b, 0:16], t)
        free(b, t_cw)

        pt_tok = []

        def slots_by_token(g):
            b = take()
            for c in range(3):
                o, n = TOFF[c], TLEN[c]
                t = tr(ps[:, b, o:o + n], PF[0:n, c, 128 * g:128 * g + 128], ident[0:n, 0:n], sig=(c == 2))
            t = A(PT[:, g, :], ps[:, b, 0:NT], ACT.Copy, t)
            free(b, t)
            pt_tok.append(t)

        sg_free = [None] * 2
        ht_free = [gathered] * 2
        sg_tok = {}
        ht_tok = {}
        y_banks = []
        y_tok = []
        y_free = [None]

        def expert_in(kind, e):
            gs = slice(128 * (e // 4), 128 * (e // 4) + 128)
            b = take()
            for i in range(2):
                w = chunk(kind, e, i)
                for k in range(4 * i, 4 * i + 4):
                    c = slice(512 * (k - 4 * i), 512 * (k - 4 * i) + 512)
                    mm(ps[:, b, :], XG[0][:, k, gs], w[0][:, c], k == 0, False, xg_tok[2 * k])
                    mm(ps[:, b, :], XG[0][:, k, gs], w[1][:, c], False, False)
                    t = mm(ps[:, b, :], XG[1][:, k, gs], w[0][:, c], False, k == 7, xg_tok[2 * k + 1], sig=(k % 4 == 3))
                chunk_done()
            return b, t

        def expert_turn(e):
            z = e % 2
            b = take()
            for m in range(4):
                t = tr(ps[:, b, 128 * m:128 * m + 128], SG[:, z, 128 * m:128 * m + 128], ident, sg_tok[e], sig=(m == 3))
            sg_free[z] = t
            ht_tok[e] = split((HT[0][:, z, :], HT[1][:, z, :]), ps[:, b, :], t, ht_free[z])
            free(b, ht_tok[e])

        def expert_out(e):
            z = e % 2
            if e % 4 == 0:
                y_banks[:] = [take(keep=True), take(keep=True)]
            for i in range(2):
                w = chunk("ed", e, i)
                for k in range(2 * i, 2 * i + 2):
                    hs = slice(128 * k, 128 * k + 128)
                    first, last = e % 4 == k == 0, e % 4 == k == 3
                    for p, q in ((0, 0), (0, 1), (1, 0)):
                        for n in range(2):
                            c = slice(1024 * (k - 2 * i) + 512 * n, 1024 * (k - 2 * i) + 512 * n + 512)
                            t = mm(ps[:, y_banks[n], :], HT[p][:, z, hs], w[q][:, c], first and p == q == 0, last and p == 1,
                                   ht_tok[e], sig=(k % 2 == 1 and p == 1 and n == 1))
                chunk_done()
            ht_free[z] = t
            if e % 4 == 3:
                y_tok.clear()
                for n in range(2):
                    c = slice(512 * n, 512 * n + 512)
                    y_tok.append(split((Y[0][:, c], Y[1][:, c]), ps[:, y_banks[n], :], t, y_free[0]))
                    free(y_banks[n], y_tok[n])

        def scatter(g):
            for j in range(8):
                b = take()
                for p in range(2):
                    t = mm(ps[:, b, 0:NT], Y[p][:, 128 * j:128 * j + 128], PT[:, g, :], p == 0, p == 1, y_tok[j // 4],
                           pt_tok[g], sig=(p == 1))
                rtok[j] = TT(R[:, j, :], R[:, j, :], ps[:, b, 0:NT], ALU.add, t)
                free(b, rtok[j])
            y_free[0] = t

        for e in range(NE):
            bg, tg = expert_in("eg", e)
            s = A(SG[:, e % 2, :], ps[:, bg, :], ACT.Silu, tg, sg_free[e % 2])
            free(bg, s)
            if e:
                expert_turn(e - 1)
            bu, tu = expert_in("eu", e)
            sg_tok[e] = STT(SG[:, e % 2, :], SG[:, e % 2, :], CW[:, e:e + 1], ps[:, bu, :], ALU.mult, ALU.mult, s, tu, t_cw)
            free(bu, sg_tok[e])
            if e < 4:
                slots_by_token(e)
            if e:
                expert_out(e - 1)
            if e % 4 == 1 and e > 1:
                scatter(e // 4 - 1)
        expert_turn(NE - 1)
        expert_out(NE - 1)
        scatter(3)

        main = (pe, act, dve)
        entry = [q.last for q in main]
        spill = tuple(Queue(sem(n)) for n in ("s_over_pe", "s_over_act", "s_over_dve"))
        s_over = sem("s_over")
        pe, act, dve = spill
        bank_free[:] = [None] * 8
        for q in spill:
            q.wait(*entry)
        G = arena[:, 0:4 * NT].rearrange("p (a b) -> p a b", a=4)
        CB = arena[:, 4 * NT:5 * NT]
        SB = arena[:, 5 * NT:5 * NT + 12]
        t = None
        for c in range(3):
            n = TLEN[c]
            TS(SB[0:n, 4 * c:4 * c + 4], CNT[0:n, 4 * c:4 * c + 4], float(CAP), None, ALU.is_gt, None)
        past = dve.last
        for c in range(3):
            n = TLEN[c]
            t_ov = TT(comb[0:n, c, :, :], comb[0:n, c, :, :], SB[0:n, 4 * c:4 * c + 4].unsqueeze(2).to_broadcast([n, 4, 4]),
                      ALU.mult, past)
        over_loads = []
        rt = [None] * 8
        cb_free = None

        def two_chunks(*key):
            over_loads.append((key, [pe.last] if over_loads else entry))
            pe.wait((s_over, 32 * len(over_loads)))

        def dense_in(kind, e, m):
            b = take()
            for k in range(8):
                t = mm(ps[:, b, 0:NT], ring[:, 512 * k + 128 * m:512 * k + 128 * m + 128], UF[:, k, :], k == 0, k == 7,
                       sig=(k == 7))
            return b, t

        for e in range(NE):
            b = take()
            for c in range(3):
                o, n = TOFF[c], TLEN[c]
                t = mm(ps[:, b, o:o + n], comb[0:n, c, e // 4, e % 4:e % 4 + 1].to_broadcast([n, 128]), ident[0:n, 0:n],
                       True, True, t_ov, sig=(c == 2))
            t_cb = CP(CB, ps[:, b, 0:NT], t, dve.last)
            free(b, t_cb)
            two_chunks("eg", e)
            g_tok = []
            done = pe.last
            for m in range(4):
                b, t = dense_in("eg", e, m)
                t = A(G[:, m, :], ps[:, b, 0:NT], ACT.Silu, t, done)
                g_tok.append(t)
                free(b, t)
            two_chunks("eu", e)
            for m in range(4):
                b, t = dense_in("eu", e, m)
                s = TT(G[:, m, :], G[:, m, :], CB, ALU.mult, g_tok[m], t_cb)
                g_tok[m] = TT(G[:, m, :], G[:, m, :], ps[:, b, 0:NT], ALU.mult, s, t)
                free(b, g_tok[m])
            two_chunks("ed", e)
            for j in range(8):
                b = take()
                for k in range(4):
                    t = mm(ps[:, b, 0:NT], ring[:, 1024 * k + 128 * j:1024 * k + 128 * j + 128], G[:, k, :], k == 0, k == 3,
                           g_tok[k], sig=(k == 3))
                rt[j] = TT(R[:, j, :], R[:, j, :], ps[:, b, 0:NT], ALU.add, t, rt[j])
                free(b, rt[j])
        for q in spill:
            q.wait(*[o.last for o in spill])
        pe, act, dve = main
        cut = [len(q.items) for q in main]
        bank_free[:] = [None] * 8

        new_phase()
        SQ2 = area(8, NT)
        RSTD = area(NT)
        OUT = area(8, NT)
        otok = rms_all(SQ2, RSTD, "nfin", rtok, OUT)

        block = ctx.enter_context(nc.Block())
        offs = np.cumsum([0] + [128 * c for _, c in plan])
        index = {key: n for n, (key, _) in enumerate(plan)}

        def over_capacity(e, name):
            r = e.alloc_register("over_" + name)
            e.wait_ge(*flag_tok)
            e.reg_load(r, flag[0:1, 0:1])
            return e.If_ne(r, 0)

        def emit_all(e, i, name):
            main[i].emit(e, 0, cut[i])
            with over_capacity(e, name):
                spill[i].emit(e)
            main[i].emit(e, cut[i])

        @block.sync
        def _(sp):
            for n, (key, c) in enumerate(plan):
                if n >= SLOTS:
                    sp.wait_ge(*slot_free[n - SLOTS])
                s = n % SLOTS
                src = wts[int(offs[n]):int(offs[n + 1])].rearrange("(p c) -> p c", p=128)
                sp.dma_start(ring[:, s * SLOT:s * SLOT + c], src).then_inc(s_w[s], 16)
            with over_capacity(sp, "sp"):
                for n, (key, done) in enumerate(over_loads):
                    for t in done:
                        sp.wait_ge(*t)
                    for i in range(2):
                        m = index[key + (i,)]
                        src = wts[int(offs[m]):int(offs[m + 1])].rearrange("(p c) -> p c", p=128)
                        sp.dma_start(ring[:, i * SLOT:i * SLOT + SLOT], src).then_inc(s_over, 16)
                for q in spill:
                    sp.wait_ge(*q.last)
            for h in range(2):
                sp.wait_ge(*otok[4 * h + 3])
                sp.dma_start(out.rearrange("p (j t) -> p j t", j=8)[:, 4 * h:4 * h + 4, :],
                             OUT[:, 4 * h:4 * h + 4, 16:NT]).then_inc(s_out, 16)
            sp.wait_ge(s_out, 32)

        @block.gpsimd
        def _(e):
            e.dma_start(MT[:, :], meta).then_inc(s_m, 16)
            pool.emit(e)

        @block.scalar
        def _(e):
            e.dma_start(vec[:, :], vecs).then_inc(s_v, 16)
            e.dma_start(cst[:, :], csts).then_inc(s_c, 16)
            e.dma_start(X.rearrange("p a b -> p (a b)"), xin).then_inc(s_x, 16)
            emit_all(e, 1, "act")

        @block.vector
        def _(e):
            emit_all(e, 2, "dve")

        @block.tensor
        def _(e):
            emit_all(e, 0, "pe")


def kernel(**inputs):
    import concourse.bacc as bacc
    from concourse.bass_utils import run_bass_kernel_spmd as run

    x = {k: np.asarray(v) for k, v in inputs.items()}
    nc = bacc.Bacc("TRN2", target_bir_lowering=False, num_devices=1)
    fmajor = lambda a: a.T.reshape(8, 128, -1).transpose(1, 0, 2)
    xin = np.concatenate([fmajor(x["x"][0]), fmajor(x["ctx"][0])], -1).reshape(128, -1)
    arrays = {
        "wts": np.concatenate([host_chunk(x, k).reshape(-1) for k, _ in chunk_plan()]),
        "xin": xin,
        "meta": fmajor(x["meta_tokens_2"]).reshape(128, -1),
        "vecs": host_vec(x),
        "csts": consts(),
    }
    arrays = {k: np.ascontiguousarray(v) for k, v in arrays.items()}
    args = [nc.dram_tensor(k, v.shape, F32, kind="ExternalInput").ap() for k, v in arrays.items()]
    out = nc.dram_tensor("out", (128, 2048), F32, kind="ExternalOutput").ap()
    build(nc, *args, out)
    r = run(nc, [arrays], core_ids=[0])
    got = np.asarray(r.results[0]["out"]).reshape(128, 8, 256)
    return np.ascontiguousarray(got.transpose(2, 1, 0).reshape(1, 256, 1024))
```

```python
import math
from contextlib import ExitStack

import numpy as np
import concourse.bass as bass
from concourse import mybir

F32 = mybir.dt.float32
F32R = mybir.dt.float32r
ALU = mybir.AluOpType
ACT = mybir.ActivationFunctionType
AX = mybir.AxisListType

D = 1024
F = 2816
NF = F // 128
S = 256
NT = 272
TOFF = [0, 16, 144]
TLEN = [16, 128, 128]
NE = 16
ALPHA = 4.0 ** 0.25
LAM_INIT = 0.8 - 0.6 * math.exp(-0.3)
NEG = -1e30
SLOTS = 3
SLOT = 2048
SPLITS = 3
ARENA = 16800
HALF = NF // 2
START = 8
CAP = 128



def vec_layout():
    at, n = {}, 0
    for name, cols in (
            ("ln1g0", 8), ("ln1b0", 8), ("ln2g0", 8), ("ln2b0", 8),
            ("ln1g1", 8), ("ln1b1", 8), ("ln2g1", 8), ("ln2b1", 8),
            ("cw0", 66), ("cw1", 66), ("cb0", 22), ("cb1", 22),
            ("qnorm", 2), ("kvnorm", 1), ("subln", 1),
            ("nmix", 8), ("scw", 64), ("scb", 16), ("dskip", 8), ("ssdn", 8),
            ("shw", 24), ("shn", 8), ("nffn", 8), ("nfin", 8),
            ("dtb", 16), ("alog", 16), ("rb", 20), ("sink", 8), ("lam", 256),
            ("rw", 160), ("wdt", 128)):
        at[name] = (n, cols)
        n += cols
    return at, n


def const_layout():
    at, n = {}, 0
    for name, cols in (
            ("ident", 128), ("o1024", 128), ("o256", 128), ("o128", 128), ("blk64", 128),
            ("ones", 128), ("tri", 128), ("sfx", 128), ("r128", 128), ("r96", 128),
            ("maska", 128), ("maskb", 128),
            ("cos128", 256), ("sin128", 256), ("cos96", 256), ("sin96", 256),
            ("rank", 4), ("eps5", 1), ("eps6", 1), ("slot", 128), ("strip", 30), ("strip8", 15), ("strip4", 7)):
        at[name] = (n, cols)
        n += cols
    return at, n


def rope_table(dim):
    row = np.repeat(np.arange(S // 64), 64).astype(np.float32)
    col = np.tile(np.arange(64), S // 64).astype(np.float32)
    q = dim // 4
    fr = (np.float32(10000.0) ** (-np.arange(q, dtype=np.float32) / np.float32(q))).astype(np.float32)
    ar = row[:, None] * fr
    ac = col[:, None] * fr
    cos = np.concatenate([np.cos(ar), np.cos(ar), np.cos(ac), np.cos(ac)], -1)
    sin = np.concatenate([np.sin(ar), np.sin(ar), np.sin(ac), np.sin(ac)], -1)
    return cos.T.astype(np.float32), sin.T.astype(np.float32)


def rope_perm(dim):
    q = dim // 4
    r = np.zeros((dim, dim), np.float32)
    for i in range(q):
        for b in (0, 2 * q):
            r[b + q + i, b + i] = -1.0
            r[b + i, b + q + i] = 1.0
    return r


def consts():
    at, n = const_layout()
    c = np.zeros((128, n), np.float32)

    def put(name, v):
        o, k = at[name]
        c[:v.shape[0], o:o + v.shape[1]] = v

    i = np.arange(128)
    put("ident", np.eye(128, dtype=np.float32))
    put("o1024", np.full((128, 128), 1 / 1024, np.float32))
    put("o256", np.full((128, 128), 1 / 256, np.float32))
    put("o128", np.full((128, 128), 1 / 128, np.float32))
    put("blk64", (i[:, None] // 64 == i[None, :] // 64).astype(np.float32) / 64)
    put("ones", np.ones((128, 128), np.float32))
    put("tri", (i[:, None] <= i[None, :]).astype(np.float32))
    put("sfx", (i[:, None] > i[None, :]).astype(np.float32))
    r128 = np.zeros((128, 128), np.float32)
    r128[:64, :64] = r128[64:, 64:] = rope_perm(64)
    put("r128", r128)
    r96 = np.zeros((128, 128), np.float32)
    r96[64:96, 64:96] = rope_perm(32)
    put("r96", r96)
    put("maska", np.where(i[None, :] <= i[:, None], 0, NEG).astype(np.float32))
    put("maskb", np.where(i[None, :] >= i[:, None], 0, NEG).astype(np.float32))
    c64, s64 = rope_table(64)
    put("cos128", np.concatenate([c64, c64]))
    put("sin128", np.concatenate([s64, s64]))
    c32, s32 = rope_table(32)
    put("cos96", np.concatenate([np.ones((64, S), np.float32), c32]))
    put("sin96", np.concatenate([np.zeros((64, S), np.float32), s32]))
    put("rank", np.tile(np.array([[4, 3, 2, 1]], np.float32), (128, 1)))
    strip = np.zeros((128, 30), np.float32)
    strip[:64, 14] = strip[64:, 15] = 1 / 64
    put("strip", strip)
    for name, n, v in (("strip8", 8, 1 / 128), ("strip4", 4, 1 / 256)):
        strip = np.zeros((128, 2 * n - 1), np.float32)
        strip[:, n - 1] = v
        put(name, strip)
    put("slot", np.tile(np.where(i < CAP, i + 1, 0).astype(np.float32), (128, 1)))
    put("eps5", np.full((128, 1), 1e-5, np.float32))
    put("eps6", np.full((128, 1), 1e-6, np.float32))
    return c


QPERM = [h + 4 * k for h in range(4) for k in range(2)]


RAW = ("qb", "kvb")


def chunk_plan():
    p = [(("mod", 0, i), 2048) for i in range(START)]
    p += [(("abin", 0), 2048)]
    for i in range(1, 5):
        p += [(("abin", i), 8 * 160 if i == 3 else 2048), (("mod", 0, 7 + i), 2048)]
    p += [(("kvb", 0), 768)]
    for half in range(2):
        p += [(("qb", half), 768)] + [(("kvb", 1), 256)] * half
    p += [(("mod", 0, i), 2048) for i in range(12, 20)]
    for i in range(4):
        p += [(("about", i), 2048), (("mod", 0, 20 + i), 2048)]
    p += ffn_plan(0)
    p += [(("din", (4 + i) % 12), 2048) for i in range(12)]
    p += [(("dout", i), 2048) for i in range(4)]
    p += ffn_plan(1)
    p += [(("win", i), 2048) for i in range(24)]
    p += [(("wout", half, i), 2048) for half in (1, 0) for i in range(4)]
    for e in range(NE + 1):
        if e < NE:
            p += [((kind, e, i), 2048) for kind in ("eg", "eu") for i in range(2)]
        if e:
            p += [(("ed", e - 1, i), 2048) for i in range(2)]
    return p


def ffn_plan(l):
    p = []
    for half in range(2):
        for i in range(HALF):
            p.append((("gu", l, HALF * half + i), 2048))
            if l == 0:
                p.append((("mod", 1, HALF * half + i), 2048))
        if l == 0 and half:
            p += [(("mod", 1, 22), 2048), (("mod", 1, 23), 2048)]
        p += [(("down", l, half, j), HALF * 128) for j in range(8)]
    return p


def pack_k(w):
    k, m = w.shape
    return w.reshape(k // 128, 128, m).transpose(1, 0, 2).reshape(128, -1)


def host_chunk(x, key):
    kind = key[0]
    if kind == "mod":
        i, half = divmod(key[2], 2)
        return pack_k(x["w_mod"][key[1]][512 * half:512 * half + 512, 512 * i:512 * i + 512])
    if kind == "abin":
        a, b = ((0, 256), (256, 512), (512, 768), (768, 928), (928, 1184))[key[1]]
        w = x["ab_w_in"][0]
        qs = w[:, 256:768].reshape(D, 8, 64)[:, QPERM].reshape(D, 512)
        return pack_k(np.concatenate([w[:, :256], qs, w[:, 768:]], 1)[:, a:b])
    if kind == "qb":
        return pack_k(x["mla_w_qb"][0][:, 384 * key[1]:384 * key[1] + 384])
    if kind == "kvb":
        w = x["mla_w_kvb"][0].reshape(128, 8, 2, 64)
        k, v = w[:, :, 0].reshape(128, 512), w[:, :, 1].reshape(128, 512)
        return k[:, 256:] if key[1] else np.concatenate([k[:, :256], v], 1)
    if kind == "about":
        w = x["ab_w_out"][0]
        sw = w[512:].reshape(8, 64, D)[QPERM].reshape(512, D)
        return pack_k(np.concatenate([w[:512], sw], 0)[:, 256 * key[1]:256 * key[1] + 256])
    if kind == "gu":
        c = slice(128 * key[2], 128 * key[2] + 128)
        return pack_k(np.concatenate([x["ffn_w_gate"][key[1]][:, c], x["ffn_w_up"][key[1]][:, c]], 1))
    if kind == "down":
        l, half, j = key[1:]
        n = 128 * HALF
        return pack_k(x["ffn_w_down"][l][n * half:n * half + n, 128 * j:128 * j + 128])
    if kind == "din":
        return pack_k(x["diff_w_in"][0][:, 256 * key[1]:256 * key[1] + 256])
    if kind == "dout":
        return pack_k(x["diff_w_out"][0][:, 256 * key[1]:256 * key[1] + 256])
    if kind == "win":
        w = x["w_in_2"][0]
        bch = w[:, 3088:].reshape(D, 3, 8, 128).transpose(0, 2, 1, 3).reshape(D, 3072)
        i = key[1]
        return pack_k(w[:, 256 * i:256 * i + 256] if i < 12 else bch[:, 256 * (i - 12):256 * (i - 12) + 256])
    if kind == "wout":
        half, i = key[1:]
        return pack_k(x["w_out_2"][0][1024 * half:1024 * half + 1024, 256 * i:256 * i + 256])
    if kind in ("eg", "eu"):
        w = x["expert_w_gate_2" if kind == "eg" else "expert_w_up_2"][0, key[1]]
        return pack_k(w[512 * key[2]:512 * key[2] + 512])
    if kind == "ed":
        return pack_k(x["expert_w_down_2"][0, key[1]][256 * key[2]:256 * key[2] + 256])


def host_cols(a):
    return np.asarray(a).reshape(-1, 128).T


def host_vec(x):
    at, n = vec_layout()
    v = np.zeros((128, n), np.float32)

    cols = host_cols

    def put(name, a):
        o, k = at[name]
        v[:, o:o + k] = a

    for l in range(2):
        for nm in ("ln1", "ln2"):
            put(f"{nm}g{l}", cols(x[f"{nm}_g"][l]))
            put(f"{nm}b{l}", cols(x[f"{nm}_b"][l]))
        put(f"cw{l}", cols(x["ffn_conv_w"][l]))
        put(f"cb{l}", cols(x["ffn_conv_b"][l]))
    put("qnorm", cols(x["mla_q_norm"][0]))
    put("kvnorm", cols(x["mla_kv_norm"][0]))
    put("subln", cols(x["diff_subln_g"][0]))
    put("nmix", cols(x["norm_mix_2"][0]))
    put("scw", cols(x["ssd_conv_w_2"][0]))
    put("scb", cols(x["ssd_conv_b_2"][0]))
    put("dskip", cols(np.repeat(x["D_skip_2"][0], 64)))
    put("ssdn", cols(x["ssd_norm_2"][0]))
    put("shw", cols(x["sc_conv_w_2"][0]))
    put("shn", cols(x["sc_norm_2"][0]))
    put("nffn", cols(x["norm_ffn_2"][0]))
    put("nfin", cols(x["norm_final_2"]))
    put("dtb", x["dt_bias_2"][0][None])
    put("alog", x["A_log_2"][0][None])
    put("rb", np.concatenate([x["router_group_b_2"][0], x["router_expert_b_2"][0]])[None])
    put("sink", x["swa_sink"][0][None])
    put("lam", np.concatenate([x["diff_lam_q1"][0], x["diff_lam_k1"][0],
                               x["diff_lam_q2"][0], x["diff_lam_k2"][0]])[None])
    put("rw", pack_k(np.concatenate([x["router_group_w_2"][0], x["router_expert_w_2"][0]], 1)))
    put("wdt", pack_k(x["w_in_2"][0][:, 3072:3088]))
    return v



class Queue:

    def __init__(self, sem):
        self.sem, self.n, self.items, self.seen = sem, 0, [], {}

    def wait(self, *toks):
        for t in toks:
            if t is not None and self.seen.get(t[0].name, 0) < t[1]:
                self.seen[t[0].name] = t[1]
                self.items.append((None, t))

    def do(self, fn, *toks, sig=True):
        self.wait(*toks)
        if sig:
            self.n += 1
        self.items.append((fn, sig))
        return (self.sem, self.n) if sig else None

    @property
    def last(self):
        return (self.sem, self.n) if self.n else None

    def emit(self, eng, first=0, end=None):
        for fn, a in self.items[first:end]:
            if fn is None:
                eng.wait_ge(a[0], a[1])
            else:
                ins = fn(eng)
                if a:
                    ins.then_inc(self.sem, 1)


def build(nc, wts, xin, meta, vecs, conds, csts, out):
    vat, nv = vec_layout()
    cat, ncst = const_layout()
    plan = chunk_plan()

    with ExitStack() as ctx:
        sb = lambda name, shape: ctx.enter_context(nc.sbuf_tensor(name, shape, F32))
        sem = lambda name: ctx.enter_context(nc.semaphore(name))

        ring = sb("ring", [128, SLOTS * SLOT])
        X = sb("X", [128, 8, 512])
        XF = X.rearrange("p a b -> p (a b)")
        HH, HL = (ctx.enter_context(nc.sbuf_tensor(n, [128, 16 * NT], F32R)) for n in ("HH", "HL"))
        WH, WL = (ctx.enter_context(nc.sbuf_tensor(n, [128, SPLITS * SLOT], F32R)) for n in ("WH", "WL"))
        csr = ctx.enter_context(nc.sbuf_tensor("csr", [128, 8, 4], F32R))
        base = nc.sbuf_base
        arena = sb("arena", [128, ARENA])
        PARTS = nc.alloc_sbuf_tensor_at("parts", [128, 2 * HALF * 512], F32R, offset=base)
        vec = sb("vec", [128, nv])
        cst = sb("cst", [128, ncst])
        modv = [sb(f"modv{l}", [128, 48, 2]) for l in range(2)]
        scond = sb("scond", [128, 8, 2])
        mrow = sb("mrow", [4, 512])
        fold = sb("fold", [128, 8, 8])
        lnc = sb("lnc", [128, 4, 8])
        small = sb("small", [128, 256])
        MT = sb("MT", [128, 128])
        cond = sb("cond", [128, 114])
        flag = ctx.enter_context(nc.sbuf_tensor("flag", [128, 1], mybir.dt.int32))
        ps = ctx.enter_context(nc.psum_tensor("ps", [128, 8, 512], F32))

        pe, act, dve, pool = (Queue(sem(n)) for n in ("s_pe", "s_act", "s_dve", "s_pool"))
        s_w = [sem(f"s_w{i}") for i in range(SLOTS + 2)]
        s_v, s_c, s_x, s_m, s_cd, s_out = (sem(n) for n in ("s_v", "s_c", "s_x", "s_m", "s_cd", "s_out"))
        VEC, CST, XIN, META = (s_v, 16), (s_c, 16), (s_x, 16), (s_m, 16)

        def V(name, i=0, n=1):
            return vec[:, vat[name][0] + i:vat[name][0] + i + n]

        def C(name, n=None):
            return cst[:, cat[name][0]:cat[name][0] + (n or cat[name][1])]

        ident = C("ident")
        EPS5, EPS6 = C("eps5"), C("eps6")

        bank_free = {}
        banks = list(range(8))

        def take():
            b = banks.pop(0)
            pe.wait(bank_free.get(b))
            return b

        def free(b, tok):
            banks.append(b)
            bank_free[b] = tok

        slot_free = {}
        split_at = [0]
        split_tok = {}
        split_of = {}
        split_free = {}
        high_tok = {}
        later = []
        chunk_at = [0]

        first_expert = [key for key, _ in plan].index(("eg", 0, 0))
        slot_of = [n % SLOTS if n < first_expert else ([(first_expert + i) % SLOTS for i in range(SLOTS)]
                   + [SLOTS, SLOTS + 1])[(n - first_expert) % (SLOTS + 2)] for n in range(len(plan))]
        spare_slots = arena[:, 2048:2048 + 2 * SLOT]

        def landed(n):
            return (s_w[slot_of[n]], 16 * slot_of[:n + 1].count(slot_of[n]))

        def raw(n):
            s = slot_of[n]
            a = (s % SLOTS) * SLOT
            return (ring if s < SLOTS else spare_slots)[:, a:a + plan[n][1]]

        def slot_ready(n):
            before = [m for m in range(n) if slot_of[m] == slot_of[n]]
            if before:
                return slot_free[before[-1]]
            return gathered if slot_of[n] >= SLOTS else None

        def split_high(n):
            q = split_at[0]
            split_at[0] += 1
            a, c = (q % SPLITS) * SLOT, plan[n][1]
            hi, lo = WH[:, a:a + c], WL[:, a:a + c]
            split_of[n] = (q, hi, lo)
            high_tok[n] = A(hi, raw(n), ACT.Copy, landed(n), split_free.get(q - SPLITS))

        def split_low(n):
            q, hi, lo = split_of[n]
            t = TT(lo, raw(n), hi.bitcast(F32), ALU.subtract, landed(n), split_free.get(q - SPLITS), high_tok[n])
            slot_free[n] = t
            split_tok[n] = t

        def split_ahead(n):
            ahead = [i for i in range(n, min(n + SPLITS, START if n < START else len(plan))) if plan[i][0][0] not in RAW]
            for i in ahead:
                if i not in split_of:
                    q = split_at[0] - SPLITS
                    if q < 0 or q in split_free:
                        split_high(i)
            for i in ahead:
                short = plan[n][0][0] == "gu" and n + 1 < len(plan) and plan[n + 1][0][0] == "mod"
                if i in split_of and i not in split_tok and i <= n + (2 if short else 1):
                    split_low(i)
            while later:
                later.pop(0)()

        def chunk(*key):
            n = chunk_at[0]
            assert plan[n][0] == key, (plan[n], key)
            chunk_at[0] += 1
            if key[0] not in RAW:
                split_ahead(n)
            if key[0] in RAW:
                pe.wait(landed(n))
                return raw(n)
            pe.wait(split_tok[n])
            return split_of[n][1:]

        def chunk_done():
            n = chunk_at[0] - 1
            if plan[n][0][0] in RAW:
                slot_free[n] = pe.last
                split_ahead(n)
            else:
                split_free[split_of[n][0]] = pe.last

        def mm(o, lhsT, rhs, start, stop, *toks, sig=False):
            return pe.do(lambda e: e.matmul(o, lhsT, rhs, start=start, stop=stop), *toks, sig=sig)

        def mm3(o, w, cols, x, k, nk, *toks, sig=False):
            mm(o, w[0][:, cols], x[0], k == 0, False, *toks)
            mm(o, w[0][:, cols], x[1], False, False)
            return mm(o, w[1][:, cols], x[0], False, k == nk - 1, sig=sig)

        def tr(o, i, idn, *toks, sig=False):
            return pe.do(lambda e: e.transpose(o, i, idn), *toks, sig=sig)

        def A(o, i, f, *toks, **kw):
            return act.do(lambda e: e.activation(o, i, f, **kw), *toks)

        def TT(o, a, b, op, *toks):
            return dve.do(lambda e: e.tensor_tensor(o, a, b, op), *toks)

        def TS(o, a, s1, s2, op0, op1, *toks):
            if s2 is None:
                return dve.do(lambda e: e.tensor_scalar(o, a, s1, None, op0), *toks)
            return dve.do(lambda e: e.tensor_scalar(o, a, s1, s2, op0, op1), *toks)

        def STT(o, a, s, b, op0, op1, *toks):
            return dve.do(lambda e: e.scalar_tensor_tensor(out=o, in0=a, scalar=s, in1=b, op0=op0, op1=op1), *toks)

        def CP(o, a, *toks):
            return dve.do(lambda e: e.tensor_copy(o, a), *toks)

        def RMAX(o, a, *toks):
            return dve.do(lambda e: e.tensor_reduce(o, a, AX.X, ALU.max), *toks)

        def RECIP(o, a, *toks):
            return dve.do(lambda e: e.reciprocal(o, a), *toks)

        def split(dst, src, *toks):
            t = A(dst[0], src, ACT.Copy, *toks)
            return TT(dst[1], src, dst[0].bitcast(F32), ALU.subtract, t, *toks)

        def parts(n, width):
            h = lambda t, a: t[:, a:a + n * width].rearrange("p (a b) -> p a b", a=n)
            return h(HH, 0), h(HL, 0)

        def at(p, k, *cols):
            return tuple(t[(slice(None), k) + (cols or (slice(None),))] for t in p)

        top = [0]

        def area(*shape):
            n = int(np.prod(shape))
            a = arena[:, top[0]:top[0] + n]
            top[0] += n
            assert top[0] <= ARENA, top[0]
            if len(shape) == 1:
                return a
            if len(shape) == 2:
                return a.rearrange("p (a b) -> p a b", a=shape[0])
            return a.rearrange("p (a b c) -> p a b c", a=shape[0], b=shape[1])

        def new_phase(at=0):
            top[0] = at
            now = [pe.last, act.last, dve.last, pool.last]
            for q in (act, dve, pool):
                q.wait(*now)

        t_cond = A(scond.rearrange("p a b -> p (a b)"), cond[:, 0:16], ACT.Silu, (s_cd, 16))
        t_cond = A(csr[:, :, 0:2], scond[:, :, :], ACT.Copy, t_cond)
        t_cond = TT(csr[:, :, 2:4], scond[:, :, :], csr[:, :, 0:2].bitcast(F32), ALU.subtract, t_cond)
        mod_tok = {}
        mod_bank = [None]
        row_free = [None]

        def mod_chunk(l, i):
            i, half = divmod(i, 2)
            w = chunk("mod", l, 2 * i + half)
            if half == 0:
                mod_bank[0] = take()
            b = mod_bank[0]
            for k in range(4):
                for p in range(2):
                    t = mm(ps[0:4, b, :], csr[:, 4 * half + k, :], w[p][:, 512 * k:512 * k + 512],
                           half == k == p == 0, half == 1 and k == 3 and p == 1, t_cond, sig=(k == 3 and p == 1))
            chunk_done()
            mod_finish()
            if half:
                t = A(mrow[:, :], ps[0:4, b, :], ACT.Copy, t, row_free[0])
                free(b, t)
                mod_left_over.append((l, i, t))

        mod_left_over = []

        def mod_finish():
            if not mod_left_over:
                return
            l, i, t = mod_left_over.pop()
            for q in (pe, dve):
                q.wait((s_cd, 16))
            b = take()
            for m in range(4):
                t = mm(ps[:, b, 2 * m:2 * m + 2], mrow[0:4, 128 * m:128 * m + 128], cond[0:4, 16:18], True, True, t,
                       sig=(m == 3))
            row_free[0] = t
            bm = cond[:, 18 + 48 * l + 4 * i:22 + 48 * l + 4 * i].unsqueeze(2).to_broadcast([128, 4, 2])
            o = modv[l][:, 4 * i:4 * i + 4, :]
            t = TT(o, ps[:, b, 0:8].rearrange("p (m s) -> p m s", s=2), bm, ALU.add, t)
            free(b, t)
            if i in (2, 3, 8, 9):
                t = TS(o, o, 1.0, None, ALU.add, None, t)
            mod_tok[l, i // 2] = t

        def halves(n):
            return ((0, 0, 256), (1, 256, 512)) if n == 512 else ((0, 0, 256),)

        def fold_mod(l, sc, sh, gname, bname, lg):
            t = None
            for s in range(2):
                TT(fold[:, s, :], V(f"{gname}{lg}", 0, 8), modv[l][:, sc:sc + 8, s], ALU.mult, mod_tok[l, sc // 8])
                t = TT(fold[:, 4 + s, :], V(f"{bname}{lg}", 0, 8), modv[l][:, sc:sc + 8, s], ALU.mult)
                t = TT(fold[:, 2 + s, :], fold[:, 4 + s, :], modv[l][:, sh:sh + 8, s], ALU.add, t, mod_tok[l, sh // 8])
            TS(lnc[:, 0, :], V(f"{gname}{lg}", 0, 8), ALPHA, None, ALU.mult, None)
            return TS(lnc[:, 1, :], V(f"{bname}{lg}", 0, 8), ALPHA, None, ALU.mult, None)

        def layer_norm(y, ytok, bm, mtok, n, hout, xout, gtok, lat_only=False):
            SQ, T8, HB = area(3, n), area(8, n), area(3, n)
            RS, SD = area(n), area(n)
            sqf = [None] * 3
            bv = take()
            for j in range(8):
                c = TT(y[:, j, :], y[:, j, :], ps[:, bm, 0:n], ALU.subtract, mtok)
                q = A(SQ[:, j % 3, :], y[:, j, :], ACT.Square, c, sqf[j % 3])
                v = mm(ps[:, bv, 0:n], C("o1024"), SQ[:, j % 3, :], j == 0, j == 7, q, sig=True)
                sqf[j % 3] = v
            free(bm, c)
            s = A(SD, ps[:, bv, 0:n], ACT.Sqrt, v, bias=EPS5, scale=1.0)
            free(bv, s)
            r = RECIP(RS, SD, s)
            htok, xtok = [], []
            if hout is None:
                for j in range(8):
                    t = STT(T8[:, j, :], y[:, j, :], V("ln2g1", j), RS, ALU.mult, ALU.mult, r)
                    xtok.append(A(xout[:, j, 16:NT], T8[:, j, :], ACT.Identity, t, bias=V("ln2b1", j), scale=1.0))
                return None, xtok
            hb_free = [None] * 3
            htok = [None] * 8
            nt = [None] * 8
            for j in range(9):
                if j < 8:
                    nt[j] = TT(T8[:, j, :], y[:, j, :], RS, ALU.mult, r)
                    for s, a, e in halves(n):
                        if s and j % 2:
                            t_d = TS(HB[:, j % 3, a:e], T8[:, j, a:e], fold[:, s, j:j + 1], fold[:, 2 + s, j:j + 1],
                                     ALU.mult, ALU.add, nt[j], gtok, hb_free[j % 3])
                            act.wait(t_d)
                            continue
                        t = A(HB[:, j % 3, a:e], T8[:, j, a:e], ACT.Identity, nt[j], gtok, hb_free[j % 3],
                              scale=fold[:, s, j:j + 1], bias=fold[:, 2 + s, j:j + 1])
                    hi = A(hout[0][:, j, :], HB[:, j % 3, :], ACT.Copy, t)
                if j:
                    i = j - 1
                    htok[i] = TT(hout[1][:, i, :], HB[:, i % 3, :], hout[0][:, i, :].bitcast(F32), ALU.subtract, hi_tok)
                    hb_free[i % 3] = htok[i]
                hi_tok = hi
            nx = 256 if lat_only else n

            def scaled_norm(j):
                xtok.append(A(y[:, j, 0:nx], T8[:, j, 0:nx], ACT.Identity, gtok, scale=lnc[:, 0, j:j + 1],
                              bias=lnc[:, 1, j:j + 1]))
            put_off[:] = [lambda j=j: scaled_norm(j) for j in range(8)]
            return htok, xtok

        put_off = []

        def out_proj(key, nk, src, stok, n, mt_per, l, gt, nxt, mean=True):
            ytok = []
            bm = take() if mean else None

            def mean_of(j):
                return mm(ps[:, bm, 0:n], C("o1024"), X[:, j, 0:n], j == 0, j == 7, ytok[j], sig=(j == 7))

            for i in range(8 // mt_per):
                w = chunk(*key, i)
                c = nk and (w[0].shape[1] // nk)
                for m in range(mt_per):
                    j = i * mt_per + m
                    b = take()
                    for k in range(nk):
                        t = mm3(ps[:, b, 0:n], w, slice(c * k + 128 * m, c * k + 128 * m + 128), at(src, k, slice(0, n)),
                                k, nk, stok[k], sig=(k == nk - 1))
                    for s, a, e in halves(n):
                        y = STT(X[:, j, a:e], ps[:, b, a:e], modv[l][:, gt + j, s:s + 1], X[:, j, a:e],
                                ALU.mult, ALU.add, t, mod_tok[l, gt // 8], nxt[j])
                    free(b, y)
                    ytok.append(y)
                    if mean and j:
                        mean_of(j - 1)
                chunk_done()
                if key[0] == "about":
                    mod_chunk(0, 20 + i)
            mod_finish()
            t = mean_of(7) if mean else None
            return ytok, bm, t

        def two_tiles(o0, o1, w, x, toks, by_k):
            order = [(m, k) for k in range(8) for m in range(2)] if by_k else [(m, k) for m in range(2) for k in range(8)]
            done = [None, None]
            for m, k in order:
                t = mm3((o0, o1)[m], w, slice(256 * k + 128 * m, 256 * k + 128 * m + 128), at(x, k), k, 8, toks[k], sig=(k == 7))
                done[m] = t or done[m]
            return done

        def ffn(l, htok, xtok, n, fold_next=None):
            top[0] = 0
            t_f = None
            area(2 * HALF * 512)
            h2 = lambda a: PARTS[:, a * HALF * 512:a * HALF * 512 + HALF * n].rearrange("p (a b) -> p a b", a=HALF)
            H2 = (h2(0), h2(1))
            H = parts(8, n)
            T = area(3, n)
            SG = area(3, n)
            tfree = [None] * 3
            sfree = [None] * 3
            nh = n // 256
            for half in range(2):
                stok = []
                down = pe.last if half else None
                for i in range(HALF):
                    f = HALF * half + i
                    z = f % 3
                    w = chunk("gu", l, f)
                    bg, bu = take(), take()
                    tg, tu = two_tiles(ps[:, bg, 0:n], ps[:, bu, 0:n], w, H, htok, f == 0)
                    chunk_done()
                    cw = lambda a: V(f"cw{l}", 22 * a + f, 1)
                    g3 = ps[:, bg, 0:n].rearrange("p (s t) -> p s t", s=nh)
                    t3 = T[:, z, :].rearrange("p (s t) -> p s t", s=nh)
                    t = A(T[:, z, :], ps[:, bg, 0:n], ACT.Identity, tg, tfree[z], scale=cw(1), bias=V(f"cb{l}", f))
                    t = STT(t3[:, :, 1:256], g3[:, :, 0:255], cw(0), t3[:, :, 1:256], ALU.mult, ALU.add, t)
                    t = STT(t3[:, :, 0:255], g3[:, :, 1:256], cw(2), t3[:, :, 0:255], ALU.mult, ALU.add, t)
                    free(bg, t)
                    t = A(SG[:, z, :], T[:, z, :], ACT.Silu, t, sfree[z])
                    tfree[z] = t
                    t = TT(SG[:, z, :], SG[:, z, :], ps[:, bu, 0:n], ALU.mult, t, tu)
                    free(bu, t)
                    t = split(at(H2, i), SG[:, z, :], t, down)
                    sfree[z] = t
                    stok.append(t)
                    if put_off:
                        put_off.pop(0)()
                    if l == 0:
                        mod_chunk(1, f)
                if l == 0 and half:
                    mod_chunk(1, 22)
                    mod_chunk(1, 23)
                    mod_finish()
                if half and fold_next:
                    dve.wait(*htok)
                    t_f = fold_mod(*fold_next)
                ytok, bm, mt = out_proj(("down", l, half), HALF, H2, stok, n, 1, l, 40, xtok, half == 1)
                xtok = ytok
            return ytok, bm, mt, t_f

        def steps(jobs, stages):
            depth = max(d for d, _ in stages) + 1
            state = [None] * len(jobs)
            for i in range(len(jobs) + depth - 1):
                for d, st in stages:
                    j = i - d
                    if 0 <= j < len(jobs):
                        state[j] = st(j, jobs[j], state[j])
                yield i

        def run_jobs(jobs, stages):
            for _ in steps(jobs, stages):
                pass

        for i in range(8):
            mod_chunk(0, i)
        mod_finish()
        act.wait(XIN)
        dve.wait(XIN)
        HP = parts(8, 512)
        QS = area(4, 512)
        KS = area(512)
        KV = area(512)
        KR = area(512)
        QN = area(2, 512)
        QM = area(4, 512)
        KM = area(4, 512)
        VM = area(4, 512)
        VS = area(4, 128)
        TMP = area(2, 256)
        early = top[0]
        QA = area(2, 512)
        SQ = area(2, 512)
        RS = area(512)
        HT = area(3, 512)
        top[0] = early
        P = area(2, 2, 512)
        PT = area(2, 4, 256)
        P = [[P[:, z, qt, :] for qt in range(2)] for z in range(2)] + [[KR, area(512)]]

        ht_free = [None] * 3
        htok = [None] * 8
        for j in range(9):
            if j == 2:
                split_ahead(START)
            if j < 8:
                h = HT[:, j % 3, :]
                for c, a, e in halves(512):
                    t = TS(h[:, a:e], X[:, j, a:e], modv[0][:, 8 + j, c:c + 1], modv[0][:, j, c:c + 1],
                           ALU.mult, ALU.add, mod_tok[0, 0], mod_tok[0, 1], ht_free[j % 3])
                hi = A(HP[0][:, j, :], h, ACT.Copy, t)
            if j:
                i = j - 1
                htok[i] = TT(HP[1][:, i, :], HT[:, i % 3, :], HP[0][:, i, :].bitcast(F32), ALU.subtract, hi_tok)
                ht_free[i % 3] = htok[i]
            hi_tok = hi
        t_ax = [A(X[:, j, :], X[:, j, :], ACT.Copy, htok[j], scale=ALPHA) for j in range(8)]

        def proj(w, c0, m, n=512):
            b = take()
            c = w[0].shape[1] // 8
            for k in range(8):
                t = mm3(ps[0:m, b, 0:n], w, slice(c * k + c0, c * k + c0 + m), at(HP, k, slice(0, n)), k, 8, htok[k],
                        sig=(k == 7))
            return b, t

        def keep_proj(dst, w, c0, m, n=512):
            b, t = proj(w, c0, m, n)
            t = A(dst, ps[0:m, b, 0:n], ACT.Copy, t)
            free(b, t)
            return t

        tmp_free = [None, None]
        rope_n = [0]

        def rope(dst, rows, perm, cos, sin, tok):
            z = rope_n[0] % 2
            rope_n[0] += 1
            b = take()
            t = mm(ps[0:rows, b, 0:256], C(perm, rows)[0:rows, :], dst[0:rows, 0:256], True, True, tok, sig=True)
            tm = TMP[0:rows, z, 0:256]
            t1 = TT(tm, ps[0:rows, b, 0:256], C(sin)[0:rows, :], ALU.mult, t, tmp_free[z])
            free(b, t1)
            t2 = TT(dst[0:rows, 0:256], dst[0:rows, 0:256], C(cos)[0:rows, :], ALU.mult, t)
            t3 = TT(dst[0:rows, 0:256], dst[0:rows, 0:256], tm, ALU.add, t1, t2)
            tmp_free[z] = t3
            return t3

        def rms_low(src, toks, n, ones, gname, dst):
            b = take()
            for m in range(n):
                q = A(SQ[:, m, :], src(m), ACT.Square, toks[m])
                t = mm(ps[:, b, :], C(ones), SQ[:, m, :], m == 0, m == n - 1, q, sig=(m == n - 1))
            s = A(RS[:, :], ps[:, b, :], ACT.Sqrt, t, bias=EPS6, scale=1.0)
            free(b, s)
            r = RECIP(RS[:, :], RS[:, :], s)
            act.wait(r)
            r = [STT(dst(m), src(m), V(gname, m), RS[:, :], ALU.mult, ALU.mult, r) for m in range(n)]
            act.wait(r[-1])
            return r

        def keep_two(key, dst, n=512):
            w = chunk(*key)
            bs = take(), take()
            done = two_tiles(ps[:, bs[0], 0:n], ps[:, bs[1], 0:n], w, tuple(p[:, :, 0:n] for p in HP), htok, True)
            chunk_done()
            done = [A(dst[m], ps[:, bs[m], 0:n], ACT.Copy, done[m]) for m in range(2)]
            free(bs[0], done[0])
            free(bs[1], done[1])
            return done

        qa_tok = keep_two(("abin", 0), [QA[:, m, :] for m in range(2)])
        for q in (pe, act, dve):
            q.wait(VEC, CST)
        qs_tok = []
        w = chunk("abin", 1)
        qs_tok += [keep_proj(QS[:, m, :], w, 128 * m, 128) for m in range(2)]
        chunk_done()
        mod_chunk(0, 8)
        qn_tok = rms_low(lambda m: QA[:, m, :], qa_tok, 2, "o256", "qnorm", lambda m: QN[:, m, :])
        w = chunk("abin", 2)
        qs_tok += [keep_proj(QS[:, 2 + m, :], w, 128 * m, 128) for m in range(2)]
        chunk_done()
        mod_chunk(0, 9)
        w = chunk("abin", 3)
        t_kv = keep_proj(KV[:, :], w, 0, 128)
        t_kr = keep_proj(KR[0:96, :], w, 64, 96)
        chunk_done()
        mod_chunk(0, 10)
        w = chunk("abin", 4)
        t_ks = keep_proj(KS[:, :], w, 0, 128)
        kv_tok = rms_low(lambda m: KV[:, :], [t_kv], 1, "o128", "kvnorm", lambda m: KV[:, :])
        t_vs = keep_proj(SQ[:, 1, :], w, 128, 128)
        chunk_done()
        mod_chunk(0, 11)
        mod_finish()
        b = take()
        for c in range(4):
            t = tr(ps[:, b, 128 * c:128 * c + 128], SQ[:, 1, 128 * c:128 * c + 128], ident, t_vs, sig=(c == 3))
        t_vs = A(VS, ps[:, b, :].rearrange("p (c m) -> p c m", c=4), ACT.Copy, t)
        free(b, t_vs)
        t_ks = rope(KS, 128, "r128", "cos128", "sin128", t_ks)
        t_kr = rope(KR, 96, "r96", "cos96", "sin96", t_kr)
        kr_tok = [CP(KM[64:96, h, :], KR[64:96, :], t_kr) for h in range(4)]
        o_after = pe.last

        qm_tok, km_tok = [None] * 4, [None] * 4

        def mla_keys(w, i, h):
            b = take()
            t = mm(ps[0:64, b, :], w[:, 64 * i:64 * i + 64], KV[:, :], True, True, kv_tok[0], sig=True)
            km_tok[h % 4] = A(KM[0:64, h % 4, :], ps[0:64, b, :], ACT.Copy, t)
            free(b, km_tok[h % 4])

        def mla_queries(w, i, h):
            b = take()
            for k in range(2):
                t = mm(ps[0:96, b, :], w[:, 384 * k + 96 * i:384 * k + 96 * i + 96], QN[:, k, :], k == 0, k == 1, qn_tok[k],
                       sig=(k == 1))
            t = A(QM[0:96, h % 4, :], ps[0:96, b, :], ACT.Copy, t)
            free(b, t)
            qm_tok[h % 4] = t
            if i:
                query_rope(h - 1)
            if i == 3:
                query_rope(h)

        def query_rope(h):
            qm_tok[h % 4] = rope(QM[:, h % 4, :], 96, "r96", "cos96", "sin96", qm_tok[h % 4])

        w = chunk("kvb", 0)
        for c in range(4):
            b = take()
            t = mm(ps[:, b, :], KV[:, 128 * c:128 * c + 128], w[:, 256:768], True, True, kv_tok[0], sig=True)
            t_vm = A(VM[:, c, :], ps[:, b, :], ACT.Copy, t)
            free(b, t_vm)
        for h in range(4):
            mla_keys(w, h, h)
        chunk_done()
        w = chunk("qb", 0)
        for h in range(4):
            mla_queries(w, h, h)
        chunk_done()
        for m in range(4):
            qs_tok[m] = rope(QS[:, m, :], 128, "r128", "cos128", "sin128", qs_tok[m])

        act.wait(o_after)
        dve.wait(o_after)
        OP = HP
        mx, nm, sm, rv, es = (small[:, 16 * a:16 * a + 16] for a in range(5))
        p_free = [[None, None], [None, None], [kr_tok[3], None]]
        pt_free = [None, None]
        mla_scale = 96.0 ** -0.5

        def att_scores(j, job, st):
            kind, h, lat = job
            k0, nk = (0, 512) if lat else (256, 256)
            sc = mla_scale if kind == "mla" else 0.125
            cols = slice(2 * (j % 4), 2 * (j % 4) + 2)
            c0 = 2 * (j % 4)
            bs, mt = [], []
            for qt in range(2):
                q0 = (0 if lat else 256) + 128 * qt
                b = take()
                o = ps[:, b, 0:nk]
                if kind == "mla":
                    t = mm(o, QM[0:96, h % 4, q0:q0 + 128], KM[0:96, h % 4, k0:k0 + nk], True, True,
                           qm_tok[h % 4], km_tok[h % 4], kr_tok[h % 4], sig=True)
                else:
                    r = 64 * (h // 4)
                    t = mm(o, QS[r:r + 64, h % 4, q0:q0 + 128], KS[r:r + 64, k0:k0 + nk], True, not lat,
                           qs_tok[h % 4], t_ks, sig=True)
                    if lat:
                        kt, mask = ((1, "maska"), (0, "maskb"))[qt]
                        t = mm(ps[:, b, 128 * kt:128 * kt + 128], ident, C(mask), False, True, sig=True)
                t = RMAX(mx[:, c0 + qt:c0 + qt + 1], o, t)
                bs.append(b)
                mt.append(t)
            if kind == "mla":
                tn = TS(nm[:, cols], mx[:, cols], -sc, None, ALU.mult, None, t)
            else:
                t = TS(mx[:, cols], mx[:, cols], sc, V("sink", h), ALU.mult, ALU.max, t)
                tn = TS(nm[:, cols], mx[:, cols], -1.0, None, ALU.mult, None, t)
            z = j % 3
            for qt in range(2):
                te = A(P[z][qt][:, 0:nk], ps[:, bs[qt], 0:nk], ACT.Exp, tn, p_free[z][qt],
                       bias=nm[:, c0 + qt:c0 + qt + 1], scale=sc, accum_out=sm[:, c0 + qt:c0 + qt + 1])
                free(bs[qt], te)
            if kind == "swa":
                for qt in range(2):
                    te = A(es[:, c0 + qt:c0 + qt + 1], V("sink", h), ACT.Exp, bias=nm[:, c0 + qt:c0 + qt + 1], scale=1.0)
            return te

        def att_scale(j, job, te):
            z = j % 3
            n = 4 if job[2] else 2
            c0 = 2 * (j % 4)
            if job[0] == "swa":
                te = TT(sm[:, c0:c0 + 2], sm[:, c0:c0 + 2], es[:, c0:c0 + 2], ALU.add, te)
            tr_ = RECIP(rv[:, c0:c0 + 2], sm[:, c0:c0 + 2], te)
            pt = []
            for qt in range(2):
                p = P[z][qt][:, 0:128 * n]
                pt.append(TS(p, p, rv[:, c0 + qt:c0 + qt + 1], None, ALU.mult, None, tr_))
            return pt

        def att_trans(j, job, pt):
            z, y = j % 3, j % 2
            n = 4 if job[2] else 2
            for qt in range(2):
                b = take()
                for kt in range(n):
                    t = tr(ps[:, b, 128 * kt:128 * kt + 128], P[z][qt][:, 128 * kt:128 * kt + 128], ident, pt[qt],
                           sig=(kt == n - 1))
                p_free[z][qt] = t
                src = ps[:, b, 0:128 * n].rearrange("p (a q) -> p a q", a=n)
                dst = PT[:, y, 0:n, 128 * qt:128 * qt + 128]
                e = A(dst, src, ACT.Copy, t, pt_free[y]) if qt else CP(dst, src, t, pt_free[y])
                free(b, e)
                pt[qt] = e
            return pt

        o_bank = {}
        o_tok = [None] * 8

        def att_pv(j, job, et):
            kind, h, lat = job
            z = j % 2
            n = 4 if lat else 2
            if kind == "mla":
                r, ot, first, second = 64 * (h % 2), h // 2, h % 2 == 0, h % 2 == 1
            else:
                r, ot, first, second = 64 * (h // 4), 4 + h % 4, h < 4, h >= 4
            if first:
                o_bank[ot, lat] = take()
            b = o_bank[ot, lat]
            for kt in range(n):
                vt = kt if lat else kt + 2
                v = VM[:, vt, 64 * h:64 * h + 64] if kind == "mla" else VS[:, vt, 64 * (h // 4):64 * (h // 4) + 64]
                t = mm(ps[r:r + 64, b, 0:256], v, PT[:, z, kt, :], kt == 0, kt == n - 1, et[0], et[1],
                       t_vm, t_vs, sig=(kt == n - 1))
            pt_free[z] = t
            if second:
                q0 = 0 if lat else 256
                hi, lo = at(OP, ot, slice(q0, q0 + 256))
                e = A(hi, ps[:, b, 0:256], ACT.Copy, t)
                e = TT(lo, ps[:, b, 0:256], hi.bitcast(F32), ALU.subtract, e)
                free(b, e)
                o_tok[ot] = e
            if j % 3 == 1 and mod_left:
                mod_chunk(0, mod_left.pop(0))
            return None

        stages = [(2, att_scale), (0, att_scores), (3, att_pv), (2, att_trans)]
        pairs = lambda h: [x for lat in (1, 0) for x in (("mla", h, lat), ("mla", h + 1, lat))]
        mod_left = []
        run_jobs(pairs(0) + pairs(2), stages)
        w = chunk("qb", 1)
        act.wait(pe.last)
        dve.wait(pe.last)
        for h in range(4, 8):
            mla_queries(w, h - 4, h)
        chunk_done()
        w = chunk("kvb", 1)
        for h in range(4, 8):
            mla_keys(w, h - 4, h)
        chunk_done()
        mod_left = list(range(12, 20))
        run_jobs(pairs(4) + pairs(6) + [("swa", h, lat) for m in range(4) for lat in (1, 0) for h in (m, m + 4)], stages)
        while mod_left:
            mod_chunk(0, mod_left.pop(0))
        mod_finish()

        t_f = fold_mod(0, 32, 24, "ln1g", "ln1b", 0)
        ytok, bm, mt = out_proj(("about",), 8, OP, o_tok, 512, 2, 0, 16, t_ax)
        new_phase()
        htok, xtok = layer_norm(X, ytok, bm, mt, 512, parts(8, 512), None, t_f)
        ytok, bm, mt, t_f = ffn(0, htok, xtok, 512, (1, 8, 0, "ln2g", "ln2b", 0))
        new_phase(ARENA - 16 * 512)
        htok, xtok = layer_norm(X, ytok, bm, mt, 512, parts(8, 512), None, t_f, lat_only=True)

        top[0] = 0
        Kd = area(8, 512)
        Vd = area(4, 1024)
        Qd = X[:, :, 256:512]
        TMP = area(2, 512)
        tmp_free = [None, None]
        P = area(2, 2, 512)
        PA = area(3, 2, 512)
        PT = area(2, 4, 256)
        kd_tok, qd_tok = [], []
        kd_tok = keep_two(("din", 4), [Kd[:, h, :] for h in range(2)])
        kd_tok[0] = rope(Kd[:, 0, :], 128, "r128", "cos128", "sin128", kd_tok[0])
        for i in range(1, 4):
            w = chunk("din", 4 + i)
            for m in range(2):
                h = 2 * i + m
                if put_off:
                    put_off.pop(0)()
                kd_tok.append(keep_proj(Kd[:, h, :], w, 128 * m, 128))
                if h:
                    kd_tok[h - 1] = rope(Kd[:, h - 1, :], 128, "r128", "cos128", "sin128", kd_tok[h - 1])
            chunk_done()
        kd_tok[7] = rope(Kd[:, 7, :], 128, "r128", "cos128", "sin128", kd_tok[7])
        while put_off:
            put_off.pop(0)()
        for i in range(4):
            w = chunk("din", 8 + i)
            for c in range(0, 4, 2):
                b = take()
                for d in range(2):
                    o = ps[:, b, 256 * d:256 * d + 256]
                    for k in range(8):
                        tok = slice(128 * (c + d), 128 * (c + d) + 128)
                        col = slice(256 * k, 256 * k + 256)
                        mm(o, HP[0][:, k, tok], w[0][:, col], k == 0, False)
                        mm(o, HP[1][:, k, tok], w[0][:, col], False, False)
                        t = mm(o, HP[0][:, k, tok], w[1][:, col], False, k == 7, sig=(d == 1 and k == 7))
                t_vd = A(Vd[:, c:c + 2, 256 * i:256 * i + 256], ps[:, b, :].rearrange("p (c n) -> p c n", c=2), ACT.Copy, t)
                free(b, t_vd)
            chunk_done()
        for i in range(4):
            w = chunk("din", i)
            for m in range(2):
                h = 2 * i + m
                qd_tok.append(keep_proj(Qd[:, h, :], w, 128 * m, 128, 256))
                if h:
                    qd_tok[h - 1] = rope(Qd[:, h - 1, :], 128, "r128", "cos128", "sin128", qd_tok[h - 1])
            chunk_done()
        qd_tok[7] = rope(Qd[:, 7, :], 128, "r128", "cos128", "sin128", qd_tok[7])
        o_after = pe.last
        lm = small[:, 96:104]
        lv = V("lam", 0, 256)
        for a in range(2):
            q, k = lv[:, 128 * a:128 * a + 64], lv[:, 128 * a + 64:128 * a + 128]
            tl = dve.do(lambda e, q=q, k=k, a=a: e.tensor_tensor_reduce(
                out=TMP[:, a, 0:64], in0=q, in1=k, scale=1.0, scalar=0.0, op0=ALU.mult, op1=ALU.add,
                accum_out=lm[:, a:a + 1]), *tmp_free)
        tl = A(lm[:, 2:4], lm[:, 0:2], ACT.Exp, tl)
        tl = TT(lm[:, 4:5], lm[:, 3:4], lm[:, 2:3], ALU.subtract, tl)
        t_lam = TS(lm[:, 5:6], lm[:, 4:5], -LAM_INIT, None, ALU.add, None, tl)
        act.wait(o_after)
        dve.wait(o_after)
        OD = parts(8, 256)
        P3 = (P[:, 0, :, :], P[:, 1, :, :], TMP)
        p_free = [None, None, t_lam]
        pa_free = [[None, None] for _ in range(3)]
        pt_free = [None, None]

        def diff_scores(j, h, st):
            c0 = 4 * (j % 3)
            cols = slice(c0, c0 + 4)
            bs = []
            for qt in range(2):
                for a in range(2):
                    b = take()
                    t = mm(ps[:, b, :], Qd[64 * a:64 * a + 64, h, 128 * qt:128 * qt + 128],
                           Kd[64 * a:64 * a + 64, h, :], True, True, qd_tok[h], kd_tok[h], sig=True)
                    t = RMAX(mx[:, c0 + 2 * qt + a:c0 + 2 * qt + a + 1], ps[:, b, :], t)
                    bs.append(b)
            tn = TS(nm[:, cols], mx[:, cols], -0.125, None, ALU.mult, None, t)
            z = j % 3
            for qt in range(2):
                for a in range(2):
                    i = 2 * qt + a
                    dst = P3[z][:, qt, :] if a else PA[:, z, qt, :]
                    te = A(dst, ps[:, bs[i], :], ACT.Exp, tn, pa_free[z][qt], p_free[z],
                           bias=nm[:, c0 + i:c0 + i + 1], scale=0.125, accum_out=sm[:, c0 + i:c0 + i + 1])
                    free(bs[i], te)
            return te

        def diff_scale(j, h, te):
            z = j % 3
            c0 = 4 * z
            cols = slice(c0, c0 + 4)
            pt = []
            tr_ = RECIP(rv[:, cols], sm[:, cols], te)
            l2 = TS(es[:, cols], rv[:, cols], lm[:, 5:6], None, ALU.mult, None, tr_, t_lam)
            for qt in range(2):
                i = c0 + 2 * qt
                t = TS(P3[z][:, qt, :], P3[z][:, qt, :], es[:, i + 1:i + 2], None, ALU.mult, None, l2)
                t = STT(PA[:, z, qt, :], PA[:, z, qt, :], rv[:, i:i + 1], P3[z][:, qt, :], ALU.mult, ALU.add, t)
                pt.append(t)
            p_free[z] = t
            return pt

        def diff_trans(j, h, pt):
            z, y = j % 3, j % 2
            for qt in range(2):
                b = take()
                for kt in range(4):
                    t = tr(ps[:, b, 128 * kt:128 * kt + 128], PA[:, z, qt, 128 * kt:128 * kt + 128], ident, pt[qt],
                           sig=(kt == 3))
                pa_free[z][qt] = t
                src = ps[:, b, :].rearrange("p (a q) -> p a q", a=4)
                dst = PT[:, y, :, 128 * qt:128 * qt + 128]
                e = A(dst, src, ACT.Copy, t, pt_free[y]) if qt else CP(dst, src, t, pt_free[y])
                free(b, e)
                pt[qt] = e
            return pt

        od_tok = [None] * 8
        SQ1 = area(256)
        b_ms = take()
        ms = {"sq": None, "sum": None}

        def head_sum(h):
            ms["sum"] = mm(ps[0:8, b_ms, 0:256], C("strip8")[:, 7 - h:15 - h], SQ1, h == 0, h == 7, ms["sq"], sig=True)

        def diff_pv(j, h, et):
            z = j % 2
            b = take()
            for kt in range(4):
                t = mm(ps[:, b, 0:256], Vd[:, kt, 128 * h:128 * h + 128], PT[:, z, kt, :], kt == 0, kt == 3,
                       et[0], et[1], t_vd, sig=(kt == 3))
            pt_free[z] = t
            e = CP(Qd[:, h, :], ps[:, b, 0:256], t)
            free(b, e)
            od_tok[h] = e
            if h:
                head_sum(h - 1)
            ms["sq"] = A(SQ1, Qd[:, h, :], ACT.Square, e, ms["sum"])

        run_jobs(list(range(8)), [(2, diff_scale), (0, diff_scores), (3, diff_pv), (2, diff_trans)])

        sg = small[:, 104:105]
        t_sg = TS(sg, V("subln"), 1.0 - LAM_INIT, None, ALU.mult, None)
        head_sum(7)
        r = A(SQ1[0:8, :], ps[0:8, b_ms, 0:256], ACT.Sqrt, ms["sum"], bias=EPS6[0:8, :], scale=1.0)
        free(b_ms, r)
        r = RECIP(SQ1[0:8, :], SQ1[0:8, :], r)
        for h in range(8):
            b = take()
            t = mm(ps[:, b, 0:256], ident[0:8, h:h + 1].to_broadcast([8, 128]), SQ1[0:8, :], True, True, r, sig=True)
            t = STT(Qd[:, h, :], Qd[:, h, :], sg, ps[:, b, 0:256], ALU.mult, ALU.mult, t, t_sg)
            free(b, t)
            od_tok[h] = split(at(OD, h), Qd[:, h, :], t)

        dve.wait(*htok)
        t_f = fold_mod(1, 32, 24, "ln1g", "ln1b", 1)
        ytok, bm, mt = out_proj(("dout",), 8, OD, od_tok, 256, 2, 1, 16, xtok)
        new_phase(ARENA - 16 * 256)
        XL = X[:, :, 0:256]
        R = XF[:, 0:8 * NT].rearrange("p (a b) -> p a b", a=8)
        htok, xtok = layer_norm(XL, ytok, bm, mt, 256, parts(8, 256), None, t_f)
        ytok, bm, mt, _ = ffn(1, htok, xtok, 256)
        new_phase()
        _, xtok = layer_norm(XL, ytok, bm, mt, 256, None, R, None)

        act.wait(META)
        t = A(R[:, :, 0:16], MT.rearrange("p (a b) -> p a b", a=8), ACT.Copy, xtok[-1])
        rtok = [t] * 8
        YP = parts(16, NT)

        class rms_stats:

            def __init__(self, sq, square=None):
                self.sq, self.bank, self.left = sq, take(), None
                self.square = square or (lambda j, tok: A(sq[:, j, :], R[:, j, :], ACT.Square, tok))

            def add(self, j, tok):
                q = self.square(j, tok)
                self.product()
                self.left = (j, q)

            def product(self):
                if self.left:
                    j, q = self.left
                    self.done = mm(ps[:, self.bank, 0:NT], C("o1024"), self.sq[:, j, :], j == 0, j == 7, q, sig=(j == 7))

            def end(self):
                self.product()
                return self.bank, self.done

        def rms_norm(bank, rstd, gname, dst):
            b, t = bank
            s = A(rstd, ps[:, b, 0:NT], ACT.Sqrt, t, bias=EPS6, scale=1.0)
            free(b, s)
            r = RECIP(rstd, rstd, s)
            return [STT(dst[:, j, :], R[:, j, :], V(gname, j), rstd, ALU.mult, ALU.mult, r) for j in range(8)]

        def by_token(w, n, row, uf_tok):
            b = take()
            for k in range(8):
                t = mm(ps[0:n, b, 0:NT], V(w, n * k, n), UF[:, k, :], k == 0, k == 7, uf_tok[k], sig=(k == 7))
            t = CP(row[0:n, :], ps[0:n, b, 0:NT], t)
            free(b, t)
            b = take()
            for c in range(3):
                o, m = TOFF[c], TLEN[c]
                t = tr(ps[0:m, b, n * c:n * c + n], row[0:n, o:o + m], ident[0:n, 0:n], t, sig=(c == 2))
            return b, t

        new_phase()
        ZS = area(8, NT)
        XC = area(16, NT)
        YC = area(8, NT)
        XD = area(3, 1024)
        CBm = area(4, 656)
        EE = area(3, 656)
        dtr, dab, dtl, dtt, dA, aex = (area(48) for _ in range(6))
        bias6 = area(96)
        spare = XF[:, 8 * NT:]
        CV = spare[:, 0:816].rearrange("p (a b) -> p a b", a=3)
        CG = spare[:, 816:1360].rearrange("p (a b) -> p a b", a=2)
        SG2 = spare[:, 1360:1648].rearrange("p (a b) -> p a b", a=2)
        YS = XC[:, 8:16, :]
        sc_root = spare[:, 1648:1648 + NT]
        sd_root = ZS[:, 7, :]
        UF = XD.rearrange("p a b -> p (a b)")[:, 0:8 * NT].rearrange("p (a b) -> p a b", a=8)
        stats = rms_stats(ZS, lambda j, tok: TT(ZS[:, j, :], R[:, j, :], R[:, j, :], ALU.mult, tok))
        for j in range(8):
            stats.add(j, rtok[j])
        uf_tok = rms_norm(stats.end(), sc_root, "nmix", UF)
        utok = [split(at(YP, j), UF[:, j, :], uf_tok[j]) for j in range(8)]

        cv_free = [None] * 3
        cg_free = [None] * 2
        zs_tok, xc_tok, yc_tok = [], [], [None] * 8
        hold = {}

        def win_tile(w, m):
            b = take()
            for k in range(8):
                t = mm3(ps[:, b, 0:NT], w, slice(256 * k + 128 * m, 256 * k + 128 * m + 128), at(YP, k), k, 8, utok[k],
                        sig=(k == 7))
            return b, t

        def steps_of_time():
            b, t = by_token("wdt", 16, sc_root, uf_tok)
            tz = dve.do(lambda e: e.memset(dtr, 0.0))
            for c in range(3):
                n = TLEN[c]
                tz = TT(dtr[0:n, 16 * c:16 * c + 16], ps[0:n, b, 16 * c:16 * c + 16], V("dtb", 0, 16)[0:n, :], ALU.add, t, tz)
            free(b, tz)
            t = A(dab, dtr, ACT.Abs, tz)
            t = A(dab, dab, ACT.Exp, t, scale=-1.0)
            ta = A(aex[:, 0:16], V("alog", 0, 16), ACT.Exp)
            t = A(dtl, dab, ACT.Ln, t, bias=1.0, scale=1.0)
            t_dt = STT(dtt, dtr, 0.0, dtl, ALU.max, ALU.add, t)
            aeb = aex[:, 0:16].unsqueeze(1).to_broadcast([128, 3, 16])
            t_dA = STT(dA.rearrange("p (c h) -> p c h", c=3), dtt.rearrange("p (c h) -> p c h", c=3), -1.0, aeb,
                       ALU.mult, ALU.mult, ta, t_dt)
            return t_dA, t_dt

        def gate_tile(f, b, t):
            def go():
                s = A(ZS[:, f, :], ps[:, b, 0:NT], ACT.Silu, t)
                free(b, s)
                zs_tok.append(s)
            return go

        def conv_tile(x, b, t):
            def go():
                z = x % 3
                wv = lambda a: V("scw", 16 * a + x)
                s = A(CV[:, z, :], ps[:, b, 0:NT], ACT.Identity, t, cv_free[z], scale=wv(3), bias=V("scb", x))
                for a in (2, 1, 0):
                    sft = 3 - a
                    s = STT(CV[:, z, sft:NT], ps[:, b, 0:NT - sft], wv(a), CV[:, z, sft:NT], ALU.mult, ALU.add, s)
                free(b, s)
                cv_free[z] = A(XC[:, x, :], CV[:, z, :], ACT.Silu, s)
                xc_tok.append(cv_free[z])
            return go

        for i in range(12):
            w = chunk("win", i)
            for m in range(2):
                f = 2 * i + m
                later.append(gate_tile(f, *win_tile(w, m)) if f < 8 else conv_tile(f - 8, *win_tile(w, m)))
            chunk_done()
            if i == 1:
                t_dA, t_dt = steps_of_time()

        def sc_tile(f, b, t):
            x, part = divmod(f, 3)
            z, zz = x % 3, x % 2
            if part == 0:
                hold["b"], hold["bt"] = b, t
            elif part == 1:
                hold["ct"] = A(CG[:, zz, :], ps[:, b, 0:NT], ACT.Copy, t, cg_free[zz])
                free(b, hold["ct"])
            else:
                wv = lambda a: V("shw", 8 * a + x)
                t = TT(CG[:, zz, :], CG[:, zz, :], ps[:, b, 0:NT], ALU.mult, t, hold["ct"])
                free(b, t)
                t = TS(CV[:, z, :], CG[:, zz, :], wv(2), None, ALU.mult, None, t, cv_free[z])
                t = STT(CV[:, z, 1:NT], CG[:, zz, 0:NT - 1], wv(1), CV[:, z, 1:NT], ALU.mult, ALU.add, t)
                t = STT(CV[:, z, 2:NT], CG[:, zz, 0:NT - 2], wv(0), CV[:, z, 2:NT], ALU.mult, ALU.add, t)
                t = TT(YC[:, x, :], CV[:, z, :], ps[:, hold["b"], 0:NT], ALU.mult, t, hold["bt"])
                free(hold["b"], t)
                cv_free[z] = t
                yc_tok[x] = t
                cg_free[zz] = A(CG[:, zz, :], YC[:, x, :], ACT.Square, t)

        sc_bank = [None]

        def sc_sum(x, first, last):
            if x == first:
                sc_bank[0] = take()
            r = 2 * (x - first)
            t = mm(ps[0:16, sc_bank[0], 0:NT], C("strip")[:, 14 - r:30 - r], CG[:, x % 2, :], x == first, x == last,
                   cg_free[x % 2], sig=True)
            cg_free[x % 2] = t
            return t

        def sc_inverse(t):
            s = A(sc_root[0:16, :], ps[0:16, sc_bank[0], 0:NT], ACT.Sqrt, t, bias=EPS6[0:16, :], scale=1.0)
            free(sc_bank[0], s)
            return RECIP(sc_root[0:16, :], sc_root[0:16, :], s)

        def sc_norm(first, last, r):
            for x in range(first, last + 1):
                b = take()
                for h in range(2):
                    c = 2 * (x - first) + h
                    t = mm(ps[64 * h:64 * h + 64, b, 0:NT], ident[0:16, c:c + 1].to_broadcast([16, 64]), sc_root[0:16, :],
                           True, True, r, sig=(h == 1))
                t = STT(YC[:, x, :], YC[:, x, :], V("shn", x), ps[:, b, 0:NT], ALU.mult, ALU.mult, t)
                free(b, t)
                yc_tok[x] = split(at(YP, 8 + x), YC[:, x, :], t)

        def dAc(c):
            return dA[0:TLEN[c], 16 * c:16 * c + 16]

        def decay_sums():
            b = take()
            for c in range(3):
                n = TLEN[c]
                mm(ps[0:n, b, 16 * c:16 * c + 16], C("tri")[0:n, 0:n], dAc(c), True, True, t_dA)
            mm(ps[0:16, b, 48:64], C("sfx")[0:16, 0:16], dAc(0), True, True)
            mm(ps[0:16, b, 64:80], C("sfx")[0:16, 0:16], dAc(0), True, False)
            mm(ps[0:16, b, 64:80], C("ones", 16), dAc(1), False, True)
            t = mm(ps[:, b, 80:96], C("sfx"), dAc(1), True, True, sig=True)
            TS(bias6[0:16, 0:16], ps[0:16, b, 0:16], -1.0, None, ALU.mult, None, t)
            TS(bias6[:, 16:48], ps[:, b, 16:48], -1.0, None, ALU.mult, None)
            CP(bias6[0:16, 48:80], ps[0:16, b, 48:80])
            t = CP(bias6[:, 80:96], ps[:, b, 80:96])
            free(b, t)
            return t

        cb_tok = []

        def group_cb(g):
            Bt, Ct = XC[:, 8 + g, :], XC[:, 12 + g, :]
            b, b2 = take(), take()
            mm(ps[0:16, b, 0:272], Bt[:, 0:16], Ct[:, :], True, True, xc_tok[8 + g], xc_tok[12 + g])
            t = mm(ps[:, b, 272:400], Bt[:, 144:272], Ct[:, 144:272], True, True, sig=True)
            t2 = mm(ps[:, b2, 0:256], Bt[:, 16:144], Ct[:, 16:272], True, True, sig=True)
            TT(CBm[0:16, g, 0:16], ps[0:16, b, 0:16], C("tri", 16)[0:16, :], ALU.mult, t)
            CP(CBm[0:16, g, 16:272], ps[0:16, b, 16:272])
            t = TT(CBm[:, g, 528:656], ps[:, b, 272:400], C("tri"), ALU.mult)
            free(b, t)
            TT(CBm[:, g, 272:400], ps[:, b2, 0:128], C("tri"), ALU.mult, t2)
            t = CP(CBm[:, g, 400:528], ps[:, b2, 128:256])
            free(b2, t)
            cb_tok.append(t)

        xd_tok = []

        def token_x(c):
            o, n = TOFF[c], TLEN[c]
            for a in range(2):
                b = take()
                for m in range(4):
                    t = tr(ps[0:n, b, 128 * m:128 * m + 128], XC[:, 4 * a + m, o:o + n], ident, xc_tok[4 * a + m],
                           sig=(m == 3))
                db = dtt[0:n, 16 * c + 8 * a:16 * c + 8 * a + 8].unsqueeze(2).to_broadcast([n, 8, 64])
                t = TT(XD[0:n, c, 512 * a:512 * a + 512].rearrange("p (h q) -> p h q", h=8),
                       ps[0:n, b, :].rearrange("p (h q) -> p h q", h=8), db, ALU.mult, t, t_dt)
                free(b, t)
                xd_tok.append(t)

        ee_free = [None] * 3
        sg_free = [None] * 2
        y_bank = {}
        ys_tok = []

        def head_decay(j, h, st):
            z, y = j % 3, j % 2
            b = take()
            for c in range(3):
                o, n = TOFF[c], TLEN[c]
                d = dA[0:n, 16 * c + h:16 * c + h + 1].to_broadcast([n, 128])
                t = mm(ps[:, b, o:o + n], d, C("tri", n)[0:n, :], True, True, sig=(c == 2))
            bc = lambda i, n: bias6[0:n, 16 * i + h:16 * i + h + 1]
            TS(SG2[0:16, y, 0:16], ps[0:16, b, 0:16], bc(0, 16), 0.0, ALU.add, ALU.min, t, sg_free[y], hold["b6"])
            TS(EE[:, z, 272:400], ps[:, b, 16:144], bc(1, 128), 0.0, ALU.add, ALU.min, ee_free[z])
            s2 = TS(EE[:, z, 528:656], ps[:, b, 144:272], bc(2, 128), 0.0, ALU.add, ALU.min)
            e = A(EE[0:16, z, 0:16], SG2[0:16, y, 0:16], ACT.Exp, s2, ee_free[z])
            sg_free[y] = e
            A(EE[0:16, z, 16:144], ps[0:16, b, 16:144], ACT.Exp, bias=bc(3, 16), scale=1.0)
            A(EE[0:16, z, 144:272], ps[0:16, b, 144:272], ACT.Exp, bias=bc(4, 16), scale=1.0)
            e = A(EE[:, z, 400:528], ps[:, b, 144:272], ACT.Exp, bias=bc(5, 128), scale=1.0)
            free(b, e)
            A(EE[:, z, 272:400], EE[:, z, 272:400], ACT.Exp)
            e = A(EE[:, z, 528:656], EE[:, z, 528:656], ACT.Exp)
            TT(EE[0:16, z, 0:272], EE[0:16, z, 0:272], CBm[0:16, h // 4, 0:272], ALU.mult, e, cb_tok[h // 4])
            return TT(EE[:, z, 272:656], EE[:, z, 272:656], CBm[:, h // 4, 272:656], ALU.mult)

        def head_out(j, h, t):
            z = j % 3
            r = 64 * (h % 2)
            if h % 2 == 0:
                y_bank[0] = take()
            b = y_bank[0]
            hc = slice(64 * h, 64 * h + 64)
            mm(ps[r:r + 64, b, 0:272], XD[0:16, 0, hc], EE[0:16, z, 0:272], True, False, t, xd_tok[-1])
            mm(ps[r:r + 64, b, 16:272], XD[:, 1, hc], EE[:, z, 272:528], False, False)
            t = mm(ps[r:r + 64, b, 144:272], XD[:, 2, hc], EE[:, z, 528:656], False, True, sig=True)
            ee_free[z] = t
            if h % 2:
                x = h // 2
                t = STT(YS[:, x, :], XC[:, x, :], V("dskip", x), ps[:, b, 0:NT], ALU.mult, ALU.add, t)
                free(b, t)
                ys_tok.append(TT(YS[:, x, :], YS[:, x, :], ZS[:, x, :], ALU.mult, t, zs_tok[x]))
                if x == 0:
                    y_bank["ms"] = take()
                else:
                    group_sum(x - 1)
                y_bank["sq"] = A(XC[:, x, :], YS[:, x, :], ACT.Square, ys_tok[x])

        def group_sum(x):
            g = x // 2
            y_bank["sum"] = mm(ps[0:4, y_bank["ms"], 0:NT], C("strip4")[:, 3 - g:7 - g], XC[:, x, :], x == 0, x == 7,
                               y_bank["sq"], sig=(x == 7))

        heads = steps(list(range(16)), [(0, head_decay), (2, head_out)])

        def scan(f):
            if f == 20:
                hold["sc"] = sc_inverse(hold["sc"])
            if f == 22:
                sc_norm(0, 5, hold["sc"])
            sc_tile(f, *hold["tile"])
            if f == 0:
                hold["b6"] = decay_sums()
            elif f < 5:
                group_cb(f - 1)
                if f < 4:
                    token_x(f - 1)
            else:
                next(heads, None)
            if f % 3 == 1 and f > 3:
                x = f // 3 - 1
                hold["sc"] = sc_sum(x, 0 if x < 6 else 6, 5 if x < 6 else 7)

        for i in range(12):
            w = chunk("win", 12 + i)
            for m in range(2):
                f = 2 * i + m
                b, t = win_tile(w, m)
                if f:
                    scan(f - 1)
                hold["tile"] = b, t
            chunk_done()
        win_end = pe.last
        scan(23)
        for _ in heads:
            pass

        def last_tiles():
            sc_norm(6, 7, sc_inverse(sc_sum(7, 6, 7)))
            group_sum(7)
            t = A(sd_root[0:4, :], ps[0:4, y_bank["ms"], 0:NT], ACT.Sqrt, y_bank["sum"], bias=EPS6[0:4, :], scale=1.0)
            free(y_bank["ms"], t)
            hold["sd"] = RECIP(sd_root[0:4, :], sd_root[0:4, :], t)

        act.wait(win_end)
        dve.wait(win_end)

        def wout_half(half, i, toks, stats=None, between=None):
            w = chunk("wout", half, i)
            bs = take(), take()
            done = [None, None]
            order = [(m, k) for m in range(2) for k in range(8)]
            if between:
                order = [(m, k) for k in range(6) for m in range(2)] + [(m, k) for m in range(2) for k in (6, 7)]
            for n, (m, k) in enumerate(order):
                if between and n == 12:
                    between()
                t = mm3(ps[:, bs[m], 0:NT], w, slice(256 * k + 128 * m, 256 * k + 128 * m + 128), at(YP, 8 * half + k),
                        k, 8, toks[k], sig=(k == 7))
                done[m] = t or done[m]
            for m in range(2):
                j, b, t = 2 * i + m, bs[m], done[m]
                rtok[j] = TT(R[:, j, :], R[:, j, :], ps[:, b, 0:NT], ALU.add, t)
                free(b, rtok[j])
                if stats:
                    stats.add(j, rtok[j])
            chunk_done()

        SQ2 = ZS
        stats = rms_stats(SQ2)
        for i in range(4):
            wout_half(1, i, yc_tok, between=None if i else last_tiles)
            for x in (2 * i, 2 * i + 1):
                if x % 2 == 0:
                    b = take()
                    t = mm(ps[:, b, 0:NT], ident[0:4, i:i + 1].to_broadcast([4, 128]), sd_root[0:4, :], True, True, hold["sd"],
                           sig=True)
                t_y = STT(YS[:, x, :], YS[:, x, :], V("ssdn", x), ps[:, b, 0:NT], ALU.mult, ALU.mult, t)
                ys_tok[x] = split(at(YP, x), YS[:, x, :], t_y)
            free(b, t_y)
        for i in range(4):
            wout_half(0, i, ys_tok, stats)
        rms_bank = stats.end()

        new_phase()
        area(2 * HALF * 512)
        UT = tuple(PARTS[:, a:a + 3072].rearrange("p (c f) -> p c f", c=3) for a in (0, 3072))
        P = PARTS[:, 6144:7680].rearrange("p (c s) -> p c s", c=3)
        PT = PARTS[:, 7680:7680 + 4 * NT].rearrange("p (g t) -> p g t", g=4)
        Y = PARTS[:, 8768:9792], PARTS[:, 9792:10816]
        HT = tuple(PARTS[:, a:a + 1024].rearrange("p (z s) -> p z s", z=2) for a in (0, 1024))
        XG = parts(8, 512)
        UF = area(8, NT)
        RSTD = area(NT)
        SG = area(2, 512)
        CNT = area(16)
        CW = area(16)
        lg = area(3, 20)
        comb = area(3, 4, 4)
        hot = area(3, 3, 4)
        pr = area(3, 4, 4)
        sel, ew = area(3, 4), area(3, 4)
        col = area(8, 3)
        uf_tok = rms_norm(rms_bank, RSTD, "nffn", UF)
        b_r, t_r = by_token("rw", 20, RSTD, uf_tok)

        def over(a, n=4):
            return a.unsqueeze(2).to_broadcast([128, 3, n])

        def first_max(src, m, h, tok):
            t = RMAX(m, src, tok)
            t = TT(h, src, over(m), ALU.is_equal, t)
            t = TT(h, h, C("rank").unsqueeze(1).to_broadcast([128, 3, 4]), ALU.mult, t)
            t = RMAX(col[:, 7, :], h, t)
            return TT(h, h, over(col[:, 7, :]), ALU.is_equal, t)

        gate_tok = []

        def route(t):
            tz = dve.do(lambda e: e.memset(lg.rearrange("p a b -> p (a b)"), 0.0))
            for c in range(3):
                n = TLEN[c]
                tl = TT(lg[0:n, c, :], ps[0:n, b_r, 20 * c:20 * c + 20], V("rb", 0, 20)[0:n, :], ALU.add, t, tz)
            free(b_r, tl)
            gl = lg[:, :, 0:4]
            el = lg[:, :, 4:20].rearrange("p c (g e) -> p c g e", g=4)
            gm, m1, m2, ex, gs, w1, w2 = (col[:, i, :] for i in range(7))
            gh, h1, h2 = (hot[:, i, :, :] for i in range(3))
            tg = first_max(gl, gm, gh, tl)
            gate_tok.append(tg)
            t = TT(ew, gl, over(gm), ALU.subtract, tg)
            te = A(ew, ew, ACT.Exp, t)
            for c in range(3):
                t = TT(pr[:, c, :, :], el[:, c, :, :], gh[:, c, :].unsqueeze(2).to_broadcast([128, 4, 4]), ALU.mult, tg)
            t = dve.do(lambda e: e.tensor_reduce(sel, pr.rearrange("p c g e -> p c e g"), AX.X, ALU.add), t)
            t = first_max(sel, m1, h1, t)
            t = STT(sel, h1, -3e38, sel, ALU.mult, ALU.add, t)
            t = first_max(sel, m2, h2, t)
            t = TT(ex, m2, m1, ALU.subtract, t)
            tx = A(ex, ex, ACT.Exp, t, te)
            t = dve.do(lambda e: e.tensor_reduce(gs, ew, AX.X, ALU.add), te)
            t = STT(w1, ex, 1.0, gs, ALU.add, ALU.mult, tx, t)
            t = RECIP(w1, w1, t)
            t = TT(w2, ex, w1, ALU.mult, t)
            t = TT(h2, h2, over(w2), ALU.mult, t)
            t1 = TT(h1, h1, over(w1), ALU.mult)
            t = TT(h1, h1, h2, ALU.add, t, t1)
            for c in range(3):
                t0 = TT(comb[:, c, :, :], h1[:, c, :].unsqueeze(1).to_broadcast([128, 4, 4]),
                        gh[:, c, :].unsqueeze(2).to_broadcast([128, 4, 4]), ALU.mult, t)
            return t0

        t_comb = route(t_r)
        gh = hot[:, 0, :, :]

        ut_tok, ut_low = ([], []), []
        for c in range(3):
            o, n = TOFF[c], TLEN[c]
            for a in range(2):
                b = take()
                for k in range(4):
                    t = tr(ps[0:n, b, 128 * k:128 * k + 128], UF[:, 4 * a + k, o:o + n], ident, uf_tok[4 * a + k],
                           sig=(k == 3))
                h = slice(512 * a, 512 * a + 512)
                hi = UT[0][0:n, c, h]
                t = A(hi, ps[0:n, b, :], ACT.Copy, t)
                ut_tok[0].append(t)
                ut_low.append((UT[1][0:n, c, h], b, n, hi, t))

        b = take()
        for c in range(4):
            m = TLEN[c] if c < 3 else 128
            for c2 in range(min(c, 2) + 1):
                n = TLEN[c2]
                t = mm(ps[0:m, b, 4 * c:4 * c + 4], C("tri" if c2 == c else "ones")[0:n, 0:m], gh[0:n, c2, :],
                       c2 == 0, c2 == min(c, 2), gate_tok[0], sig=(c == 3 and c2 == 2))
        for c in range(4):
            m = TLEN[c] if c < 3 else 128
            o, i = CNT[0:m, 4 * c:4 * c + 4], ps[0:m, b, 4 * c:4 * c + 4]
            t_cnt = TT(o, i, gh[0:m, c, :], ALU.mult, t) if c < 3 else CP(o, i, t)
        free(b, t_cnt)
        for c in range(3):
            n = TLEN[c]
            for g in range(4):
                t_p = TS(P[0:n, c, 128 * g:128 * g + 128], C("slot")[0:n, :], CNT[0:n, 4 * c + g:4 * c + g + 1],
                         None, ALU.is_equal, None, t_cnt)
        t = RMAX(small[:, 0:1], CNT[:, 12:16], t_cnt)
        flag_tok = TS(flag[:, :], small[:, 0:1], float(CAP), None, ALU.is_gt, None, t)

        for o, b, n, hi, t in ut_low:
            t = TT(o, ps[0:n, b, :], hi.bitcast(F32), ALU.subtract, t)
            free(b, t)
            ut_tok[1].append(t)

        xg_tok = [None] * 16
        for p in range(2):
            for k in range(8):
                b = take()
                for c in range(3):
                    n = TLEN[c]
                    t = mm(ps[:, b, :], UT[p][0:n, c, 128 * k:128 * k + 128], P[0:n, c, :], c == 0, c == 2, t_p, *ut_tok[p],
                           sig=(c == 2))
                o = XG[p][:, k, :]
                t = CP(o, ps[:, b, :], t) if p and k % 2 else A(o, ps[:, b, :], ACT.Copy, t)
                free(b, t)
                xg_tok[2 * k + p] = t
        gathered = pe.last

        PF = P.bitcast(F32)

        def weights_by_slot():
            b = take()
            for g in range(4):
                for c in range(3):
                    n = TLEN[c]
                    t = mm(ps[:, b, 4 * g:4 * g + 4], PF[0:n, c, 128 * g:128 * g + 128], comb[0:n, c, g, :], c == 0, c == 2,
                           t_comb, sig=(g == 3 and c == 2))
            t_cw = CP(CW, ps[:, b, 0:16], t)
            free(b, t_cw)
            return t_cw

        pt_tok = []

        def slots_by_token(g):
            b = take()
            for c in range(3):
                o, n = TOFF[c], TLEN[c]
                t = tr(ps[:, b, o:o + n], PF[0:n, c, 128 * g:128 * g + 128], ident[0:n, 0:n], sig=(c == 2))
            t = A(PT[:, g, :], ps[:, b, 0:NT], ACT.Copy, t)
            free(b, t)
            pt_tok.append(t)

        sg_free = [None] * 2
        ht_free = [gathered] * 2
        sg_tok = {}
        ht_tok = {}
        y_banks = []
        y_tok = []
        y_free = [None]

        def expert_in(kind, e):
            gs = slice(128 * (e // 4), 128 * (e // 4) + 128)
            b = take()
            for i in range(2):
                w = chunk(kind, e, i)
                for k in range(4 * i, 4 * i + 4):
                    c = slice(512 * (k - 4 * i), 512 * (k - 4 * i) + 512)
                    mm(ps[:, b, :], XG[0][:, k, gs], w[0][:, c], k == 0, False, xg_tok[2 * k])
                    mm(ps[:, b, :], XG[0][:, k, gs], w[1][:, c], False, False)
                    t = mm(ps[:, b, :], XG[1][:, k, gs], w[0][:, c], False, k == 7, xg_tok[2 * k + 1], sig=(k % 4 == 3))
                chunk_done()
            return b, t

        def expert_turn(e):
            z = e % 2
            b = take()
            for m in range(4):
                t = tr(ps[:, b, 128 * m:128 * m + 128], SG[:, z, 128 * m:128 * m + 128], ident, sg_tok[e], sig=(m == 3))
            sg_free[z] = t

            def go():
                ht_tok[e] = split((HT[0][:, z, :], HT[1][:, z, :]), ps[:, b, :], t, ht_free[z])
                free(b, ht_tok[e])
            return go

        def expert_out(e):
            z = e % 2
            if e % 4 == 0:
                y_banks[:] = [take(), take()]
            for i in range(2):
                w = chunk("ed", e, i)
                for k in range(2 * i, 2 * i + 2):
                    hs = slice(128 * k, 128 * k + 128)
                    first, last = e % 4 == k == 0, e % 4 == k == 3
                    for p, q in ((0, 0), (0, 1), (1, 0)):
                        for n in range(2):
                            c = slice(1024 * (k - 2 * i) + 512 * n, 1024 * (k - 2 * i) + 512 * n + 512)
                            t = mm(ps[:, y_banks[n], :], HT[p][:, z, hs], w[q][:, c], first and p == q == 0, last and p == 1,
                                   ht_tok[e], sig=(k % 2 == 1 and p == 1 and n == 1))
                chunk_done()
            ht_free[z] = t
            if e % 4 == 3:
                y_tok.clear()
                for n in range(2):
                    c = slice(512 * n, 512 * n + 512)
                    y_tok.append(split((Y[0][:, c], Y[1][:, c]), ps[:, y_banks[n], :], t, y_free[0]))
                    free(y_banks[n], y_tok[n])

        def scatter(g):
            for j in range(8):
                b = take()
                for p in range(2):
                    t = mm(ps[:, b, 0:NT], Y[p][:, 128 * j:128 * j + 128], PT[:, g, :], p == 0, p == 1, y_tok[j // 4],
                           pt_tok[g], sig=(p == 1))
                rtok[j] = TT(R[:, j, :], R[:, j, :], ps[:, b, 0:NT], ALU.add, t)
                free(b, rtok[j])
            y_free[0] = t

        def gate_done(e, b, t):
            def go():
                sg_tok[e] = A(SG[:, e % 2, :], ps[:, b, :], ACT.Silu, t, sg_free[e % 2])
                free(b, sg_tok[e])
            return go

        def up_done(e, b, t):
            def go():
                sg_tok[e] = STT(SG[:, e % 2, :], SG[:, e % 2, :], CW[:, e:e + 1], ps[:, b, :], ALU.mult, ALU.mult,
                                sg_tok[e], t, t_cw)
                free(b, sg_tok[e])
            return go

        for e in range(NE):
            later.append(gate_done(e, *expert_in("eg", e)))
            if e:
                later.append(expert_turn(e - 1))
            if e == 0:
                t_cw = weights_by_slot()
            later.append(up_done(e, *expert_in("eu", e)))
            if e < 4:
                slots_by_token(e)
            if e:
                expert_out(e - 1)
            if e % 4 == 1 and e > 1:
                scatter(e // 4 - 1)
        for go in later:
            go()
        later.clear()
        expert_turn(NE - 1)()
        expert_out(NE - 1)
        scatter(3)

        main = (pe, act, dve)
        entry = [q.last for q in main]
        spill = tuple(Queue(sem(n)) for n in ("s_over_pe", "s_over_act", "s_over_dve"))
        s_over = sem("s_over")
        pe, act, dve = spill
        bank_free.clear()
        for q in spill:
            q.wait(*entry)
        G = arena[:, 0:4 * NT].rearrange("p (a b) -> p a b", a=4)
        CB = arena[:, 4 * NT:5 * NT]
        SB = arena[:, 5 * NT:5 * NT + 12]
        t = None
        for c in range(3):
            n = TLEN[c]
            TS(SB[0:n, 4 * c:4 * c + 4], CNT[0:n, 4 * c:4 * c + 4], float(CAP), None, ALU.is_gt, None)
        past = dve.last
        for c in range(3):
            n = TLEN[c]
            t_ov = TT(comb[0:n, c, :, :], comb[0:n, c, :, :], SB[0:n, 4 * c:4 * c + 4].unsqueeze(2).to_broadcast([n, 4, 4]),
                      ALU.mult, past)
        over_loads = []
        rt = [None] * 8
        cb_free = None

        def two_chunks(*key):
            over_loads.append((key, [pe.last] if over_loads else entry))
            pe.wait((s_over, 32 * len(over_loads)))

        def dense_in(kind, e, m):
            b = take()
            for k in range(8):
                t = mm(ps[:, b, 0:NT], ring[:, 512 * k + 128 * m:512 * k + 128 * m + 128], UF[:, k, :], k == 0, k == 7,
                       sig=(k == 7))
            return b, t

        for e in range(NE):
            b = take()
            for c in range(3):
                o, n = TOFF[c], TLEN[c]
                t = mm(ps[:, b, o:o + n], comb[0:n, c, e // 4, e % 4:e % 4 + 1].to_broadcast([n, 128]), ident[0:n, 0:n],
                       True, True, t_ov, sig=(c == 2))
            t_cb = CP(CB, ps[:, b, 0:NT], t, dve.last)
            free(b, t_cb)
            two_chunks("eg", e)
            g_tok = []
            done = pe.last
            for m in range(4):
                b, t = dense_in("eg", e, m)
                t = A(G[:, m, :], ps[:, b, 0:NT], ACT.Silu, t, done)
                g_tok.append(t)
                free(b, t)
            two_chunks("eu", e)
            for m in range(4):
                b, t = dense_in("eu", e, m)
                s = TT(G[:, m, :], G[:, m, :], CB, ALU.mult, g_tok[m], t_cb)
                g_tok[m] = TT(G[:, m, :], G[:, m, :], ps[:, b, 0:NT], ALU.mult, s, t)
                free(b, g_tok[m])
            two_chunks("ed", e)
            for j in range(8):
                b = take()
                for k in range(4):
                    t = mm(ps[:, b, 0:NT], ring[:, 1024 * k + 128 * j:1024 * k + 128 * j + 128], G[:, k, :], k == 0, k == 3,
                           g_tok[k], sig=(k == 3))
                rt[j] = TT(R[:, j, :], R[:, j, :], ps[:, b, 0:NT], ALU.add, t, rt[j])
                free(b, rt[j])
        for q in spill:
            q.wait(*[o.last for o in spill])
        pe, act, dve = main
        cut = [len(q.items) for q in main]
        bank_free.clear()

        new_phase()
        SQ2 = area(8, NT)
        RSTD = area(NT)
        OUT = area(8, NT)
        stats = rms_stats(SQ2)
        for j in range(8):
            stats.add(j, rtok[j])
        otok = rms_norm(stats.end(), RSTD, "nfin", OUT)

        block = ctx.enter_context(nc.Block())
        offs = np.cumsum([0] + [128 * c for _, c in plan])
        index = {key: n for n, (key, _) in enumerate(plan)}

        def over_capacity(e, name):
            r = e.alloc_register("over_" + name)
            e.wait_ge(*flag_tok)
            e.reg_load(r, flag[0:1, 0:1])
            return e.If_ne(r, 0)

        def emit_all(e, i, name):
            main[i].emit(e, 0, cut[i])
            with over_capacity(e, name):
                spill[i].emit(e)
            main[i].emit(e, cut[i])

        @block.sync
        def _(sp):
            for n, (key, c) in enumerate(plan):
                if slot_ready(n):
                    sp.wait_ge(*slot_ready(n))
                src = wts[int(offs[n]):int(offs[n + 1])].rearrange("(p c) -> p c", p=128)
                sp.dma_start(raw(n), src).then_inc(s_w[slot_of[n]], 16)
                if n == 7:
                    sp.dma_start(X.rearrange("p a b -> p (a b)"), xin).then_inc(s_x, 16)
                if n == 9:
                    sp.dma_start(vec[:, :], vecs).then_inc(s_v, 16)
                    sp.dma_start(cst[:, :], csts).then_inc(s_c, 16)
            with over_capacity(sp, "sp"):
                for n, (key, done) in enumerate(over_loads):
                    for t in done:
                        sp.wait_ge(*t)
                    for i in range(2):
                        m = index[key + (i,)]
                        src = wts[int(offs[m]):int(offs[m + 1])].rearrange("(p c) -> p c", p=128)
                        sp.dma_start(ring[:, i * SLOT:i * SLOT + SLOT], src).then_inc(s_over, 16)
                for q in spill:
                    sp.wait_ge(*q.last)
            for h in range(2):
                sp.wait_ge(*otok[4 * h + 3])
                sp.dma_start(out.rearrange("p (j t) -> p j t", j=8)[:, 4 * h:4 * h + 4, :],
                             OUT[:, 4 * h:4 * h + 4, 16:NT]).then_inc(s_out, 16)
            sp.wait_ge(s_out, 32)

        @block.gpsimd
        def _(e):
            e.dma_start(MT[:, :], meta).then_inc(s_m, 16)
            pool.emit(e)

        @block.scalar
        def _(e):
            e.dma_start(cond[:, :], conds).then_inc(s_cd, 16)
            emit_all(e, 1, "act")

        @block.vector
        def _(e):
            emit_all(e, 2, "dve")

        @block.tensor
        def _(e):
            emit_all(e, 0, "pe")


def kernel(**inputs):
    import concourse.bacc as bacc
    from concourse.bass_utils import run_bass_kernel_spmd as run

    x = {k: np.asarray(v) for k, v in inputs.items()}
    nc = bacc.Bacc("TRN2", target_bir_lowering=False, num_devices=1)
    fmajor = lambda a: a.T.reshape(8, 128, -1).transpose(1, 0, 2)
    xin = np.concatenate([fmajor(x["x"][0]), fmajor(x["ctx"][0])], -1).reshape(128, -1)
    arrays = {
        "wts": np.concatenate([host_chunk(x, k).reshape(-1) for k, _ in chunk_plan()]),
        "xin": xin,
        "meta": fmajor(x["meta_tokens_2"]).reshape(128, -1),
        "vecs": host_vec(x),
        "conds": np.concatenate([np.stack([host_cols(x["c"][0]), host_cols(x["c_ctx"])], -1).reshape(128, 16),
                                 np.tile(np.eye(2, dtype=np.float32), (64, 1))]
                                + [host_cols(x["b_mod"][l]) for l in range(2)], 1),
        "csts": consts(),
    }
    arrays = {k: np.ascontiguousarray(v) for k, v in arrays.items()}
    args = [nc.dram_tensor(k, v.shape, F32, kind="ExternalInput").ap() for k, v in arrays.items()]
    out = nc.dram_tensor("out", (128, 2048), F32, kind="ExternalOutput").ap()
    build(nc, *args, out)
    r = run(nc, [arrays], core_ids=[0])
    got = np.asarray(r.results[0]["out"]).reshape(128, 8, 256)
    return np.ascontiguousarray(got.transpose(2, 1, 0).reshape(1, 256, 1024))
```
